# Optimizing a Trainium2 kernel written in Bass

```python
import math
import jax, jax.numpy as jnp
from jax import lax
import numpy as np

"""One inference step of a hybrid decoder layer stack (DEPTH layers), run for a prompt group and a
sample group that share the same weights.

Layer (pre-RMSNorm, plain residual adds):
  h = x + W_out[ concat( RMSNorm(stick-breaking heads), RMSNorm(short gated conv groups) ) ]
      with one combined input projection whose columns are split into q | k | v | B | C | xv
  h = h + CrossAttn(RMSNorm(h), memory K/V)   (4 heads, 256 memory tokens)
  h = h + SwiGLU(RMSNorm(h))
final RMSNorm.

Inputs:
  x_prompt    (BATCH, SEQ, D_MODEL)
  x_sample    (DEC_BATCH, DEC_SEQ, D_MODEL)
  mem_prompt  (BATCH, N_MEM, D_MODEL)
  cache_sb_k, cache_sb_v  (DEPTH, N_POOL, PAGE_SIZE, SB_HEADS, SB_HEAD_DIM)   paged stick-breaking K/V
  cache_mem_k, cache_mem_v (DEPTH, DEC_BATCH, N_MEM, CA_HEADS, CA_HEAD_DIM)  memory K/V
  state_conv  (DEPTH, DEC_BATCH, CONV_K - 1, CONV_CH)  last conv-input rows
  page_table  (DEC_BATCH, N_PAGES) int32
  then the weights.
Returns (y_prompt, y_sample, sb_k_prompt, sb_v_prompt, conv_state_prompt, mem_k_prompt, mem_v_prompt,
         sb_k_sample, sb_v_sample, conv_state_sample):
  y_prompt          (BATCH, SEQ, D_MODEL)
  y_sample          (DEC_BATCH, DEC_SEQ, D_MODEL)
  sb_k_prompt/v     (DEPTH, BATCH, SEQ, SB_HEADS, SB_HEAD_DIM)        rows for positions 0..SEQ-1
  conv_state_prompt (DEPTH, BATCH, CONV_K - 1, CONV_CH)
  mem_k_prompt/v    (DEPTH, BATCH, N_MEM, CA_HEADS, CA_HEAD_DIM)
  sb_k_sample/v     (DEPTH, DEC_BATCH, DEC_SEQ, SB_HEADS, SB_HEAD_DIM) rows for positions PAST_LEN..PAST_LEN+DEC_SEQ-1
  conv_state_sample (DEPTH, DEC_BATCH, CONV_K - 1, CONV_CH)
"""

D_MODEL = 1024
BATCH = 1
SEQ = 512
DEPTH = 1
DEC_BATCH = 8
DEC_SEQ = 8
PAST_LEN = 4096
PAGE_SIZE = 128

MIX_WIDTH = D_MODEL
SB_HEAD_DIM = 64
SB_WIDTH = MIX_WIDTH // 2
SB_HEADS = SB_WIDTH // SB_HEAD_DIM
SB_SCALE = SB_HEAD_DIM ** -0.5
SB_BIAS_INIT = -7.0
CONV_CH = MIX_WIDTH - SB_WIDTH
CONV_GROUP_DIM = 64
CONV_GROUPS = CONV_CH // CONV_GROUP_DIM
CONV_K = 3
IN_WIDTH = 3 * SB_WIDTH + 3 * CONV_CH
N_MEM = 256
CA_HEADS = 4
CA_HEAD_DIM = 128
CA_WIDTH = CA_HEADS * CA_HEAD_DIM
CA_SCALE = CA_HEAD_DIM ** -0.5
D_FF = ((8 * D_MODEL // 3 + 255) // 256) * 256
BLOCK_Q = 128
EPS = 1e-6

kernel_name = "hymba_stickbreak_shortconv_decode_step"

def rmsnorm(x, g):
    xf = x.astype(jnp.float32)
    y = xf * lax.rsqrt(jnp.mean(xf * xf, axis=-1, keepdims=True) + EPS)
    return (y * g.astype(jnp.float32)).astype(x.dtype)

def sb_logits(q, k, sb_bias):
    z = jnp.einsum("bqhd,bkhd->bhqk", q, k).astype(jnp.float32) * SB_SCALE
    return z + sb_bias.astype(jnp.float32)[None, :, None, None]

def sb_block(z, mask, v, carry):
    log_om = jnp.where(mask, jax.nn.log_sigmoid(-z), 0.0)
    suffix = lax.cumsum(log_om, axis=3, reverse=True) - log_om + carry[..., None]
    a = jnp.where(mask, jnp.exp(jax.nn.log_sigmoid(z) + suffix), 0.0)
    o = jnp.einsum("bhqk,bkhd->bqhd", a, v.astype(jnp.float32))
    return o, carry + jnp.sum(log_om, axis=3)

def sb_attention_prompt(q, k, v, sb_bias):
    b, s, h, d = q.shape
    nb = s // BLOCK_Q
    q_blocks = q.reshape(b, nb, BLOCK_Q, h, d).swapaxes(0, 1)
    key_pos = jnp.arange(s)

    def one_block(args):
        q_blk, blk = args
        query_pos = blk * BLOCK_Q + jnp.arange(BLOCK_Q)
        mask = key_pos[None, :] < query_pos[:, None]
        z = sb_logits(q_blk, k, sb_bias)
        o, _ = sb_block(z, mask, v, jnp.zeros(z.shape[:3], jnp.float32))
        return o

    o = lax.map(one_block, (q_blocks, jnp.arange(nb)))
    return o.swapaxes(0, 1).reshape(b, s, h * d).astype(q.dtype)

def sb_attention_sample(q, k_new, v_new, cache_k, cache_v, page_table, sb_bias):
    b, t, h, d = q.shape
    new_pos = jnp.arange(t)
    mask = new_pos[None, :] < new_pos[:, None]
    z = sb_logits(q, k_new, sb_bias)
    o, carry = sb_block(z, mask, v_new, jnp.zeros(z.shape[:3], jnp.float32))

    def page_step(state, phys):
        o_acc, carry = state
        kp = cache_k[phys]
        vp = cache_v[phys]
        zp = sb_logits(q, kp, sb_bias)
        o_p, carry = sb_block(zp, True, vp, carry)
        return (o_acc + o_p, carry), None

    (o, _), _ = lax.scan(page_step, (o, carry), page_table.T, reverse=True)
    return o.reshape(b, t, h * d).astype(q.dtype)

def mixer_inputs(x, g_mix, w_in):
    b, s, _ = x.shape
    hn = rmsnorm(x, g_mix)
    p = hn @ w_in
    q, k, v, bg, cg, xv = jnp.split(
        p, [SB_WIDTH, 2 * SB_WIDTH, 3 * SB_WIDTH, 3 * SB_WIDTH + CONV_CH, 3 * SB_WIDTH + 2 * CONV_CH], axis=-1)
    heads = lambda t_: t_.reshape(b, s, SB_HEADS, SB_HEAD_DIM)
    return heads(q), heads(k), heads(v), bg, cg * xv

def causal_conv3(u_ext, w_conv):
    s = u_ext.shape[1] - (CONV_K - 1)
    return w_conv[0] * u_ext[:, :s] + w_conv[1] * u_ext[:, 1:s + 1] + w_conv[2] * u_ext[:, 2:]

def mixer_output(x, attn, bg, conv_y, g_attn_out, g_conv_out, w_out):
    a = rmsnorm(attn, g_attn_out)
    c = rmsnorm(bg * conv_y, g_conv_out)
    return x + jnp.concatenate([a, c], axis=-1) @ w_out

def memory_kv(mem, g_mem, w_ck, w_cv):
    b = mem.shape[0]
    mn = rmsnorm(mem, g_mem)
    mk = (mn @ w_ck).reshape(b, N_MEM, CA_HEADS, CA_HEAD_DIM)
    mv = (mn @ w_cv).reshape(b, N_MEM, CA_HEADS, CA_HEAD_DIM)
    return mk, mv

def cross_attention(x, mk, mv, g_ca, w_cq, w_co):
    b, s, _ = x.shape
    q = (rmsnorm(x, g_ca) @ w_cq).reshape(b, s, CA_HEADS, CA_HEAD_DIM)
    sc = jnp.einsum("bqhd,bmhd->bhqm", q, mk).astype(jnp.float32) * CA_SCALE
    p = jax.nn.softmax(sc, axis=-1)
    o = jnp.einsum("bhqm,bmhd->bqhd", p, mv.astype(jnp.float32)).astype(x.dtype)
    return x + o.reshape(b, s, CA_WIDTH) @ w_co

def swiglu_ffn(x, g_ffn, w_gate, w_up, w_down):
    hn = rmsnorm(x, g_ffn)
    return x + (jax.nn.silu(hn @ w_gate) * (hn @ w_up)) @ w_down

def setup_inputs(seed: int = 0) -> dict:
    key = jax.random.key(seed)
    ks = jax.random.split(key, 32)
    n_pages = PAST_LEN // PAGE_SIZE
    n_used = DEC_BATCH * n_pages
    n_pool = n_used + (n_used + 3) // 4

    def normal(k, shape, scale=1.0):
        return scale * jax.random.normal(k, shape, jnp.float32)

    def gain(k, dim):
        return 1.0 + 0.02 * jax.random.normal(k, (DEPTH, dim), jnp.float32)

    page_table = jax.random.permutation(ks[8], n_pool)[:n_used].reshape(DEC_BATCH, n_pages).astype(jnp.int32)
    return {
        "x_prompt": normal(ks[0], (BATCH, SEQ, D_MODEL)),
        "x_sample": normal(ks[1], (DEC_BATCH, DEC_SEQ, D_MODEL)),
        "mem_prompt": normal(ks[2], (BATCH, N_MEM, D_MODEL)),
        "cache_sb_k": normal(ks[3], (DEPTH, n_pool, PAGE_SIZE, SB_HEADS, SB_HEAD_DIM)),
        "cache_sb_v": normal(ks[4], (DEPTH, n_pool, PAGE_SIZE, SB_HEADS, SB_HEAD_DIM)),
        "cache_mem_k": normal(ks[5], (DEPTH, DEC_BATCH, N_MEM, CA_HEADS, CA_HEAD_DIM)),
        "cache_mem_v": normal(ks[6], (DEPTH, DEC_BATCH, N_MEM, CA_HEADS, CA_HEAD_DIM)),
        "state_conv": normal(ks[7], (DEPTH, DEC_BATCH, CONV_K - 1, CONV_CH)),
        "page_table": page_table,
        "g_mix": gain(ks[10], D_MODEL),
        "w_in": normal(ks[11], (DEPTH, D_MODEL, IN_WIDTH), D_MODEL ** -0.5),
        "sb_bias": SB_BIAS_INIT + 0.1 * jax.random.normal(ks[27], (DEPTH, SB_HEADS), jnp.float32),
        "w_conv": normal(ks[12], (DEPTH, CONV_K, CONV_CH), CONV_K ** -0.5),
        "g_attn_out": gain(ks[13], SB_WIDTH),
        "g_conv_out": gain(ks[14], CONV_CH),
        "w_out": normal(ks[15], (DEPTH, MIX_WIDTH, D_MODEL), MIX_WIDTH ** -0.5),
        "g_mem": gain(ks[16], D_MODEL),
        "g_ca": gain(ks[17], D_MODEL),
        "w_cq": normal(ks[18], (DEPTH, D_MODEL, CA_WIDTH), D_MODEL ** -0.5),
        "w_ck": normal(ks[19], (DEPTH, D_MODEL, CA_WIDTH), D_MODEL ** -0.5),
        "w_cv": normal(ks[20], (DEPTH, D_MODEL, CA_WIDTH), D_MODEL ** -0.5),
        "w_co": normal(ks[21], (DEPTH, CA_WIDTH, D_MODEL), CA_WIDTH ** -0.5),
        "g_ffn": gain(ks[22], D_MODEL),
        "w_gate": normal(ks[23], (DEPTH, D_MODEL, D_FF), D_MODEL ** -0.5),
        "w_up": normal(ks[24], (DEPTH, D_MODEL, D_FF), D_MODEL ** -0.5),
        "w_down": normal(ks[25], (DEPTH, D_FF, D_MODEL), D_FF ** -0.5),
        "g_final": 1.0 + 0.02 * jax.random.normal(ks[26], (D_MODEL,), jnp.float32),
    }

def reference(x_prompt, x_sample, mem_prompt, cache_sb_k, cache_sb_v, cache_mem_k, cache_mem_v,
              state_conv, page_table, g_mix, w_in, sb_bias, w_conv, g_attn_out, g_conv_out, w_out,
              g_mem, g_ca, w_cq, w_ck, w_cv, w_co, g_ffn, w_gate, w_up, w_down, g_final):
    yp, ys = x_prompt, x_sample
    kp_l, vp_l, cp_l, mkp_l, mvp_l, ks_l, vs_l, cs_l = [], [], [], [], [], [], [], []
    for l in range(DEPTH):
        q, k, v, bg, u = mixer_inputs(yp, g_mix[l], w_in[l])
        attn = sb_attention_prompt(q, k, v, sb_bias[l])
        u_ext = jnp.pad(u, ((0, 0), (CONV_K - 1, 0), (0, 0)))
        yp = mixer_output(yp, attn, bg, causal_conv3(u_ext, w_conv[l]), g_attn_out[l], g_conv_out[l], w_out[l])
        mk, mv = memory_kv(mem_prompt, g_mem[l], w_ck[l], w_cv[l])
        yp = cross_attention(yp, mk, mv, g_ca[l], w_cq[l], w_co[l])
        yp = swiglu_ffn(yp, g_ffn[l], w_gate[l], w_up[l], w_down[l])
        kp_l.append(k)
        vp_l.append(v)
        cp_l.append(u_ext[:, -(CONV_K - 1):])
        mkp_l.append(mk)
        mvp_l.append(mv)
        q, k, v, bg, u = mixer_inputs(ys, g_mix[l], w_in[l])
        attn = sb_attention_sample(q, k, v, cache_sb_k[l], cache_sb_v[l], page_table, sb_bias[l])
        u_ext = jnp.concatenate([state_conv[l].astype(u.dtype), u], axis=1)
        ys = mixer_output(ys, attn, bg, causal_conv3(u_ext, w_conv[l]), g_attn_out[l], g_conv_out[l], w_out[l])
        ys = cross_attention(ys, cache_mem_k[l], cache_mem_v[l], g_ca[l], w_cq[l], w_co[l])
        ys = swiglu_ffn(ys, g_ffn[l], w_gate[l], w_up[l], w_down[l])
        ks_l.append(k)
        vs_l.append(v)
        cs_l.append(u_ext[:, -(CONV_K - 1):])
    y_prompt = rmsnorm(yp, g_final)
    y_sample = rmsnorm(ys, g_final)
    return (y_prompt, y_sample, jnp.stack(kp_l), jnp.stack(vp_l), jnp.stack(cp_l), jnp.stack(mkp_l),
            jnp.stack(mvp_l), jnp.stack(ks_l), jnp.stack(vs_l), jnp.stack(cs_l))


_drawn_inputs = setup_inputs


def setup_inputs(seed=0):
    import zlib

    import numpy as np

    out = dict(_drawn_inputs(seed))
    spreads = {}
    factors = {'g_attn_out': 5.335,
     'g_conv_out': 5.779,
     'g_mem': 2.861,
     'g_ca': 8.0,
     'g_ffn': 5.062,
     'g_final': 2.794}
    for name, (base, spread) in spreads.items():
        noise = np.random.default_rng([zlib.crc32(name.encode()), seed]).standard_normal(out[name].shape)
        drawn = base * np.exp(spread * noise) if base else spread * noise
        out[name] = __import__('jax').numpy.asarray(drawn.astype(out[name].dtype))
    for name, factor in factors.items():
        out[name] = (out[name] * factor).astype(out[name].dtype)
    return out
```

```python
from contextlib import ExitStack

import numpy as np

import concourse.bass as bass
from concourse import mybir

F32 = mybir.dt.float32
F32R = mybir.dt.float32r
I32 = mybir.dt.int32
ALU = mybir.AluOpType
ACT = mybir.ActivationFunctionType
AX = mybir.AxisListType

P = 128
D = 1024
KD = D // P
SEQ = 512
NB = SEQ // P
BS, TS = 8, 8
NS = BS * TS
T = SEQ + NS
HALF = T // 2
HEADS, HD = 8, 64
HP = HEADS * HD // P
CH = 512
KC = CH // P
PAGES = 32
NMEM = 256
MT = NMEM // P
CAH = 4
SB_SCALE = HD ** -0.5
CA_SCALE = P ** -0.5
EPS = 1e-6
GROUPS = BS // 2
CP = 4
SLOTW = 256
N_POOL = 320

G_MIX, G_MEM, G_CA, G_FFN, G_FIN, G_ATT, G_CONV, W_CONV, NVEC = 0, 8, 16, 24, 32, 40, 44, 48, 60
C_ID, C_SMASK, C_CMASK, C_SEL, NCONST = 0, 128, 384, 512, 640


def hybrid_layer(nc, x_p, x_s, mem, ck, cv, cmk, cmv, st_conv, ptab, g_mix, w_in, sb_bias, w_conv,
                 g_att, g_conv, w_out, g_mem, g_ca, w_cq, w_ck, w_cv, w_co, g_ffn, w_gate, w_up,
                 w_down, g_fin, shape_consts,
                 y_p, y_s, out_k_p, out_v_p, out_c_p, out_mk, out_mv, out_k_s, out_v_s, out_c_s):
    ctx = ExitStack()
    with ctx:
        lo_addr = (nc.sbuf_base + 63) // 64 * 64
        size = 207 * 1024 - 128
        ctx.enter_context(nc.sbuf_tensor("arena", [P, size // 4], F32))
        cursor = [lo_addr]

        def region(n):
            off = cursor[0]
            cursor[0] += n
            assert cursor[0] <= lo_addr + size, cursor[0] - lo_addr
            return off

        def at(name, shape, off, dt=F32):
            return nc.alloc_sbuf_tensor_at(name, [P] + shape, dt, offset=off)

        def sem(name):
            return ctx.enter_context(nc.semaphore(name))

        R_X, R_H, R_P = region(KD * T * 4), region(2 * KD * T * 4), region(24 * T * 4)
        R_W, R_M, R_K = region(6 * 8192), region(16384), region(8192)
        R_V, R_C, R_R = region(14336), region(4096), region(2304 + 1024 + 1024 + 320)
        xT = at("xT", [KD, T], R_X)
        h_hi = at("h_hi", [KD, T], R_H, F32R)
        h_lo = at("h_lo", [KD, T], R_H + KD * T * 4, F32R)
        pT = at("pT", [24, T], R_P)
        w_raw = [at(f"w_raw{i}", [8, SLOTW], R_W + i * 8192) for i in range(2)]
        w_hi = [at(f"w_hi{i}", [8, SLOTW], R_W + (2 + i) * 8192, F32R) for i in range(2)]
        w_lo = [at(f"w_lo{i}", [8, SLOTW], R_W + (4 + i) * 8192, F32R) for i in range(2)]
        rstd = at("rstd", [T], R_R)
        rstd_m = at("rstd_m", [NMEM], R_R + 2304)
        ptb = at("ptb", [BS * PAGES], R_R + 3328, I32)
        cs = at("cs", [KC, 18], R_R + 4352)
        sq = at("sq", [KD, T], R_P)
        x_tok = at("x_tok", [5, D], R_P + 18432)
        mT = at("mT", [KD, NMEM], R_P + 38912)
        m_sq = at("m_sq", [KD, NMEM], R_P + 47104)
        m_tok = at("m_tok", [MT, D], R_V)
        st_rows = at("st_rows", [CH], R_V + 8192)
        vec_rows = at("vec_rows", [P], R_V + 10240)
        m_hi = at("m_hi", [KD, NMEM], R_M, F32R)
        m_lo = at("m_lo", [KD, NMEM], R_M + 8192, F32R)
        mkT = at("mkT", [CAH, NMEM], R_K)
        mv_tok = at("mv_tok", [MT, CH], R_K + 4096)
        v_tok = at("v_tok", [5, CH], R_V)
        mvT = at("mvT", [CAH, NMEM], R_V + 10240)
        k_rows = at("k_rows", [5, CH], R_H)
        mk_rows = at("mk_rows", [MT, CH], R_H + 10240)
        cs_rows = at("cs_rows", [CH], R_V)
        T_Q, T_K, T_A, T_B, T_C, T_U = 0, 4, 8, 12, 16, 20
        beta = at("beta", [2, SEQ], R_P + T_B * T * 4)
        om = at("om", [2, SEQ], R_P + T_B * T * 4 + 4096)
        aw = at("aw", [2, SEQ], R_P + T_U * T * 4)
        awT = at("awT", [2, 4, P], R_P + T_U * T * 4 + 4096)
        run = at("run", [2, SEQ + 1], R_M)
        q_fix = at("q_fix", [SEQ], R_M + 4224)
        k_fix = at("k_fix", [SEQ], R_M + 6272)
        v_fix = at("v_fix", [4, P], R_M + 8320)
        q_bd = at("q_bd", [2, HP, 32], R_M + 10368)
        o_pair = at("o_pair", [2, P], R_M + 11392)
        k_page = [at(f"k_page{i}", [8, CH], R_H + i * 16384) for i in range(2)]
        v_page = [at(f"v_page{i}", [8, CH], R_W + i * 16384) for i in range(2)]
        kT = at("kT", [2, HP, SEQ], R_W + 32768)
        sq_a = at("sq_a", [KC, T], R_P)
        sq_c = at("sq_c", [KC, T], R_P + KC * T * 4)
        nrm = at("nrm", [T], R_M)
        caq = at("caq", [CAH, T], R_P)
        caoT = at("caoT", [CAH, T], R_P + CAH * T * 4)
        R_CA = R_P + 2 * CAH * T * 4
        prob = at("prob", [4, NMEM], R_CA)
        probT = at("probT", [MT, SEQ], R_CA + 4096)
        qc = at("qc", [4, CAH, 32], R_CA + 8192)
        sq_ca = at("sq_ca", [KD, T], R_CA + 10240)
        smk_tok = at("smk_tok", [4, MT, CH], R_M)
        smkT = at("smkT", [4, CAH, NMEM], R_H)
        smv_tok = at("smv_tok", [4, MT, CH], R_H + 16384)
        f_hi = at("f_hi", [12, T], R_P, F32R)
        f_lo = at("f_lo", [12, T], R_P + 12 * T * 4, F32R)
        gbuf = at("gbuf", [2, T], R_M)
        sbuf_ = at("sbuf_", [2, T], R_M + 4608)
        ubuf = at("ubuf", [2, T], R_M + 9216)
        yT = at("yT", [KD, T], R_P + 18432)
        y_rows = at("y_rows", [5, D], R_W)
        cc = at("cc", [NCONST], R_C)
        ident = cc[:, C_ID:C_ID + P]
        cvec = at("cvec", [NVEC], R_C + 2560)
        ones = at("ones", [P], R_C + 2816)
        cst = at("cst", [8], R_C + 3328)
        bias_p = at("bias_p", [2, HEADS], R_C + 3360)
        bias_s = at("bias_s", [2], R_C + 3424)
        bias_col = at("bias_col", [1], R_C + 3456)
        bias_dg = at("bias_dg", [HEADS], R_C + 3488)
        stT = at("stT", [KC, 2 * BS], R_C + 3520)
        sm = at("sm", [40], R_C + 3776)
        bias_fix = at("bias_fix", [2, 2], R_C + 4000)
        token = at("token", [64], region(256))

        ps = ctx.enter_context(nc.psum_tensor("ps", [P, 8, 512], F32))

        def halves(ap):
            return ap.rearrange("p (a b) -> p a b", a=2)

        def tiled(ap, f=P):
            return ap.rearrange("p (a f) -> p a f", f=f)

        def kview(w):
            return w[0].rearrange("(k p) n -> p k n", p=P)

        views = {"in": kview(w_in), "ck": kview(w_ck), "cv": kview(w_cv), "out": kview(w_out),
                 "cq": kview(w_cq), "co": kview(w_co), "gate": kview(w_gate), "up": kview(w_up),
                 "down": kview(w_down)}
        STAGES = [("in", 8, 6), ("ck", 8, 1), ("cv", 8, 1), ("out", 8, 2), ("cq", 8, 1), ("co", 4, 2),
                  ("gu0", 8, 6), ("down0", 6, 4), ("gu1", 8, 5), ("down1", 5, 4)]
        FF0 = (0, 12)
        NAMES = [name for name, _, _ in STAGES]
        KN = {name: kn for name, kn, _ in STAGES}
        PAIRS = {name: pairs for name, _, pairs in STAGES}
        SLOT0 = {name: sum(2 * p for _, _, p in STAGES[:i]) for i, name in enumerate(NAMES)}

        s_const, s_x, s_m, s_pt = sem("consts_loaded"), sem("x_loaded"), sem("mem_loaded"), sem("ptab_loaded")
        s_set = sem("ones_and_token_set")
        s_tr, s_ev = sem("unit_transposed"), sem("unit_copied")
        s_bmm, s_bc = sem("bias_product"), sem("bias_copied")
        s_full = [sem("weights_loaded0"), sem("weights_loaded1")]
        s_whi, s_wlo = sem("weights_hi"), sem("weights_lo")
        s_tile = {n: sem(f"tile_{n}") for n in NAMES}
        s_free = {n: sem(f"banks_{n}") for n in NAMES}
        s_op = {n: sem(f"operand_{n}") for n in ("in", "ck", "out", "cq", "co", "gu0")}
        NORMS = ["in", "ck", "att", "conv", "cq", "gu0", "fin"]
        s_sq = {n: sem(f"squares_{n}") for n in NORMS}
        s_sum = {n: sem(f"sums_{n}") for n in NORMS}
        s_ms = {n: sem(f"meansq_{n}") for n in NORMS}
        s_rt = {n: sem(f"root_{n}") for n in NORMS}
        s_evac = {n: sem(f"evacuated_{n}") for n in NAMES}
        s_dve = sem("vector_step")
        s_out = sem("outputs_stored")
        s_conv, s_cs = sem("conv_done"), sem("conv_rows_staged")
        s_sig = sem("sigmoid_done")
        s_y = sem("y_scaled")
        p_ = {n: sem(f"prompt_{n}") for n in ("qk_fixed", "bias_fixed", "v_fixed", "score", "beta", "om", "scan", "weight", "tr",
                                              "copied_a", "copied_d", "out", "out_copied")}
        m_ = {n: sem(f"sample_{n}") for n in ("queries", "k_copied_a", "k_copied_d", "score", "beta",
                                              "om", "run", "weight", "tr", "tr_copied", "pv", 
                                              "rows", "rows_tr", "rows_copied")}
        s_kp = [sem("k_pages0"), sem("k_pages1")]
        s_vp = [sem("v_pages0"), sem("v_pages1")]
        s_ktr = sem("k_page_transposed")
        c_ = {n: sem(f"cross_{n}") for n in ("score", "max", "exp", "prob", "tr", "tr_copied", "out", "out_copied",
                                             "queries")}
        s_cmk, s_cmv = sem("mem_k_loaded"), sem("mem_v_loaded")

        steps, grants = [0], [0]

        def step(dve, ins):
            steps[0] += 1
            ins.then_inc(s_dve, 1)
            dve.wait_ge(s_dve, steps[0])

        def grant(semaphore, n):
            grants[0] += 1
            nc.vector.memset(token[0:1, grants[0]:grants[0] + 1], 0.0).then_inc(semaphore, n)

        units = []

        def batch(pairs_):
            a = len(units)
            units.extend(pairs_)
            return range(a, len(units))

        def rows_of(m):
            return P if m < NB else NS

        def to_tokens(src, k0, m, dst):
            r = rows_of(m)
            return [src[:, k0 + j, m * P:m * P + r] for j in range(4)], tiled(dst[0:r, :])

        U_VEC = batch([([vec_rows[0:NVEC, :]], cvec[:, :].rearrange("p (a f) -> p a f", a=1)),
                       ([st_rows[0:2 * BS, j * P:(j + 1) * P] for j in range(4)], stT[:, :, :])])
        U_X = batch([([x_tok[0:rows_of(m), m, (4 * kh + j) * P:(4 * kh + j + 1) * P] for j in range(4)],
                      xT[:, 4 * kh:4 * kh + 4, m * P:m * P + rows_of(m)]) for m in range(5) for kh in range(2)])
        U_M = batch([([m_tok[:, m, (4 * kh + j) * P:(4 * kh + j + 1) * P] for j in range(4)],
                      mT[:, 4 * kh:4 * kh + 4, m * P:(m + 1) * P]) for m in range(MT) for kh in range(2)])
        U_VT = batch([to_tokens(pT, T_A, m, v_tok[:, m, :]) for m in range(5)])
        U_KT = batch([to_tokens(pT, T_K, m, k_rows[:, m, :]) for m in range(5)])
        U_MK = batch([([src[:, j, m * P:(m + 1) * P] for j in range(4)], tiled(dst[:, m, :]))
                      for src, dst in ((mkT, mk_rows), (mvT, mv_tok)) for m in range(MT)])
        U_CS = batch([([cs[:, j, :] for j in range(4)], tiled(cs_rows[0:18, :]))])
        U_SMK = [batch([([smk_tok[:, b, m, j * P:(j + 1) * P] for j in range(4)], smkT[:, b, :, m * P:(m + 1) * P])
                        for b in range(4) for m in range(MT)]) for _ in range(2)]
        U_Y = batch([to_tokens(yT, 4 * kh, m, y_rows[:, m, kh * 512:(kh + 1) * 512])
                     for m in range(5) for kh in range(2)])

        def tr_pe(pe, us):
            for u in us:
                srcs, _ = units[u]
                if u >= 2:
                    pe.wait_ge(s_ev, u - 1)
                for j, src in enumerate(srcs):
                    p_in, f = src.shape[0], src.shape[-1]
                    op = nc.tensor.transpose(ps[0:f, 4 + u % 2, j * P:j * P + p_in], src, ident[0:p_in, 0:p_in])
                op.then_inc(s_tr, 1)

        def tr_act(act, us):
            for u in us:
                srcs, dst = units[u]
                p_in, f = srcs[0].shape[0], srcs[0].shape[-1]
                act.wait_ge(s_tr, u + 1)
                bank = tiled(ps[0:f, 4 + u % 2, 0:len(srcs) * P])[:, :, 0:p_in]
                nc.scalar.activation(dst, bank, ACT.Copy).then_inc(s_ev, 1)

        def rms_sum(dve, name, buf, kt):
            dve.wait_ge(s_sq[name], 1)
            while kt > 2:
                kt //= 2
                step(dve, nc.vector.tensor_tensor(buf[:, 0:kt, :], buf[:, 0:kt, :], buf[:, kt:2 * kt, :], ALU.add))
            nc.vector.tensor_tensor(buf[:, 0, :], buf[:, 0, :], buf[:, 1, :], ALU.add).then_inc(s_sum[name], 1)

        def rms_pe(pe, name, buf, n, after=None):
            if after:
                pe.wait_ge(s_rt[after], 1)
            pe.wait_ge(s_sum[name], 1)
            w = n // 2
            for hf in range(2):
                op = nc.tensor.matmul(ps[:, 6 + hf, 0:w], ones[:, :], buf[:, 0, hf * w:(hf + 1) * w],
                                      start=True, stop=True)
            op.then_inc(s_ms[name], 1)

        def rms_root(act, name, dst, n, feats):
            act.wait_ge(s_ms[name], 1)
            nc.scalar.activation(halves(dst), ps[:, 6:8, 0:n // 2], ACT.Sqrt,
                                 bias=cst[:, 0:1], scale=1.0 / feats).then_inc(s_rt[name], 1)

        def rms_inv(dve, name, buf):
            dve.wait_ge(s_rt[name], 1)
            step(dve, nc.vector.reciprocal(buf, buf))

        def scale_split(dve, src, g0, hi, lo, kt, ready):
            for k in range(kt):
                g = cvec[:, g0 + k:g0 + k + 1]
                step(dve, nc.vector.tensor_scalar(hi[:, k, :], src[:, k, :], g, None, ALU.mult))
                op = nc.vector.scalar_tensor_tensor(out=lo[:, k, :], in0=src[:, k, :], scalar=g,
                                                    in1=hi[:, k, :].bitcast(F32), op0=ALU.mult, op1=ALU.subtract)
            op.then_inc(ready, 1)

        def load_stage(sp, name, grants=()):
            n0, kn = SLOT0[name], KN[name]

            def body(i, first):
                for s in range(2):
                    if not first:
                        sp.wait_ge(s_wlo, i * 2 + (n0 + s - 1))
                    if name[:2] == "gu":
                        src = views["gate" if s == 0 else "up"][:, :, bass.ds(i * SLOTW + FF0[int(name[2])] * P, SLOTW)]
                    elif name[:4] == "down":
                        k0 = FF0[int(name[4])] + s * kn
                        src = views["down"][:, k0:k0 + kn, bass.ds(i * SLOTW, SLOTW)]
                    else:
                        src = views[name][:, :, bass.ds(i * (2 * SLOTW) + s * SLOTW, SLOTW)]
                    sp.dma_start(w_raw[s][:, 0:kn, :], src).then_inc(s_full[s], 16)
            if n0 == 0:
                body(0, True)
                with sp.Fori(1, PAIRS[name]) as i:
                    body(i, False)
            else:
                with sp.Fori(0, PAIRS[name]) as i:
                    body(i, False)

        def split_hi(act, name, i, s):
            act.wait_ge(s_full[s], i * 16 + (SLOT0[name] * 8 + 16))
            nc.scalar.activation(w_hi[s][:, 0:KN[name], :], w_raw[s][:, 0:KN[name], :], ACT.Copy).then_inc(s_whi, 1)

        def split_stage(act, name, more=None):
            prev = NAMES[NAMES.index(name) - 1] if name != "in" else None
            for s in range(2):
                if prev:
                    act.wait_ge(s_tile[prev], 4 * PAIRS[prev] - 2 + 2 * s)
                split_hi(act, name, 0, s)
            if more:
                more(0)
            if PAIRS[name] > 1:
                with act.Fori(1, PAIRS[name]) as i:
                    for s in range(2):
                        act.wait_ge(s_tile[name], i * 4 + (2 * s - 2))
                        split_hi(act, name, i, s)
                    if more:
                        more(i)

        def lo_stage(pool, name):
            with pool.Fori(0, PAIRS[name]) as i:
                for s in range(2):
                    pool.wait_ge(s_whi, i * 2 + (SLOT0[name] + s + 1))
                    nc.gpsimd.tensor_tensor(w_lo[s][:, 0:KN[name], :], w_raw[s][:, 0:KN[name], :],
                                            w_hi[s][:, 0:KN[name], :].bitcast(F32), ALU.subtract).then_inc(s_wlo, 1)

        def gemm(pe, name, hi, lo, n=T):
            kn, down = KN[name], name[:4] == "down"
            parts = [(a, min(a + HALF, n)) for a in range(0, n, HALF)]
            with pe.Fori(0, PAIRS[name]) as i:
                for s in range(2):
                    pe.wait_ge(s_wlo, i * 2 + (SLOT0[name] + s + 1))
                    for t in range(2):
                        if not down:
                            pe.wait_ge(s_free[name], i * 4 + (2 * s + t + 1))
                        elif s == 0:
                            pe.wait_ge(s_free[name], i * 2 + (t + 1))
                        begin, end, k0 = not down or s == 0, not down or s == 1, s * kn if down else 0
                        for k in range(kn):
                            for w, (weights, x) in enumerate(((w_hi, hi), (w_hi, lo), (w_lo, hi))):
                                for hf, (a, b) in enumerate(parts):
                                    op = nc.tensor.matmul(ps[:, 2 * t + hf, 0:b - a],
                                                          weights[s][:, k, t * P:(t + 1) * P], x[:, k0 + k, a:b],
                                                          start=begin and k == 0 and w == 0,
                                                          stop=end and k == kn - 1 and w == 2)
                        op.then_inc(s_tile[name], 1)

        def pair(t):
            return ps[:, 2 * t:2 * t + 2, 0:HALF]

        def tile_of(dst, i):
            return dst[:, bass.ds(i, 1), :].rearrange("p o (a b) -> p (o a) b", a=2)

        def evac_scaled(dve, name, dst, scale):
            with dve.Fori(0, PAIRS[name]) as i:
                for j in range(4):
                    dve.wait_ge(s_tile[name], i * 4 + (j + 1))
                    nc.vector.tensor_tensor(tile_of(dst, i * 4 + j), pair(j % 2), halves(scale), ALU.mult)\
                        .then_inc(s_free[name], 1)

        def evac_mem(dve, name, dst):
            for j in range(4):
                dve.wait_ge(s_tile[name], j + 1)
                nc.vector.tensor_tensor(dst[:, j, :], ps[:, 2 * (j % 2), 0:NMEM], rstd_m[:, :], ALU.mult)\
                    .then_inc(s_free[name], 1)

        def evac_residual(dve, name):
            down = name[:4] == "down"
            with dve.Fori(0, PAIRS[name]) as i:
                for j in range(2 if down else 4):
                    dve.wait_ge(s_tile[name], i * 4 + (j + 3 if down else j + 1))
                    x = tile_of(xT, i * (2 if down else 4) + j)
                    nc.vector.tensor_tensor(x, pair(j % 2), x, ALU.add).then_inc(s_free[name], 1)

        KB = [0, 1, 2, 5]

        def cross_act(act):
            nc.scalar.preload_act_table(ACT.Exp)
            for u in range(CAH + 2):
                if u >= CAH:
                    tr_act(act, U_SMK[u - CAH])
                act.wait_ge(c_["max"], u + 1)
                for j in range(4 if u < CAH else 1):
                    z = ps[:, j // 2, (j % 2) * NMEM:(j % 2 + 1) * NMEM]
                    op = nc.scalar.activation(prob[:, j, :], z, ACT.Exp, scale=CA_SCALE,
                                              bias=sm[:, 4 + j:5 + j], accum_out=sm[:, 8 + j:9 + j])
                op.then_inc(c_["exp"], 1)
                act.wait_ge(c_["tr"], u + 1)
                w = SEQ if u < CAH else P
                nc.scalar.activation(probT[:, :, 0:w], ps[:, 2:4, 0:w], ACT.Copy).then_inc(c_["tr_copied"], 1)
                act.wait_ge(c_["out"], u + 1)
                if u < CAH:
                    dst, src = caoT[:, u, 0:SEQ], ps[:, 6, :]
                else:
                    dst = caoT[:, :, SEQ + 32 * (u - CAH):SEQ + 32 * (u - CAH) + 32]
                    src = tiled(ps[:, 6, 0:P], 32)
                nc.scalar.activation(dst, src, ACT.Copy).then_inc(c_["out_copied"], 1)

        s_h = sem("hidden_step")
        s_hid = sem("hidden_ready")

        def hidden_dve(dve, half):
            name = f"gu{half}"
            h0 = 8 * PAIRS["gu0"] * half
            g0 = 2 * PAIRS["gu0"] * half
            with dve.Fori(0, PAIRS[name]) as i:
                for t in range(2):
                    dve.wait_ge(s_tile[name], i * 4 + (t + 1))
                    nc.vector.tensor_tensor(halves(gbuf[:, t, :]), pair(t), halves(rstd[:, :]), ALU.mult)\
                        .then_inc(s_free[name], 1)
                for t in range(2):
                    dve.wait_ge(s_tile[name], i * 4 + (t + 3))
                    nc.vector.tensor_tensor(halves(ubuf[:, t, :]), pair(t), halves(rstd[:, :]), ALU.mult)\
                        .then_inc(s_free[name], 1)
                    dve.wait_ge(s_sig, i * 2 + (g0 + t + 1))
                    nc.vector.tensor_tensor(gbuf[:, t, :], gbuf[:, t, :], sbuf_[:, t, :], ALU.mult).then_inc(s_h, 1)
                    dve.wait_ge(s_h, i * 8 + (h0 + 4 * t + 1))
                    nc.vector.tensor_tensor(ubuf[:, t, :], ubuf[:, t, :], gbuf[:, t, :], ALU.mult).then_inc(s_h, 1)
                    dve.wait_ge(s_h, i * 8 + (h0 + 4 * t + 2))
                    hi = f_hi[:, bass.ds(i * 2 + t, 1), :].rearrange("p o n -> p (o n)")
                    lo = f_lo[:, bass.ds(i * 2 + t, 1), :].rearrange("p o n -> p (o n)")
                    nc.vector.tensor_copy(hi, ubuf[:, t, :]).then_inc(s_h, 1)
                    dve.wait_ge(s_h, i * 8 + (h0 + 4 * t + 3))
                    nc.vector.tensor_tensor(lo, ubuf[:, t, :], hi.bitcast(F32), ALU.subtract).then_inc(s_h, 1)
            grant(s_hid, 1)

        def cross_dve(dve):
            for u in range(CAH + 2):
                n = 4 if u < CAH else 1
                if u >= CAH:
                    gg = u - CAH
                    if gg == 0:
                        step(dve, nc.vector.memset(qc[:, :, :, :], 0.0))
                    for b in range(4):
                        c0 = SEQ + 32 * gg + 8 * b
                        op = nc.vector.tensor_copy(qc[:, b, :, 8 * b:8 * b + 8], caq[:, :, c0:c0 + 8])
                    op.then_inc(c_["queries"], 1)
                dve.wait_ge(c_["score"], u + 1)
                if n == 4:
                    z = ps[:, 0:2, :].rearrange("p a (b m) -> p a b m", b=2)
                    step(dve, nc.vector.tensor_reduce(sm[:, 0:4].rearrange("p (a b) -> p a b", a=2), z, AX.X, ALU.max))
                else:
                    step(dve, nc.vector.tensor_reduce(sm[:, 0:1], ps[:, 0, 0:NMEM], AX.X, ALU.max))
                nc.vector.tensor_scalar(sm[:, 4:4 + n], sm[:, 0:n], -CA_SCALE, None, ALU.mult).then_inc(c_["max"], 1)
                dve.wait_ge(c_["exp"], u + 1)
                step(dve, nc.vector.reciprocal(sm[:, 12:12 + n], sm[:, 8:8 + n]))
                for j in range(n):
                    op = nc.vector.tensor_scalar(prob[:, j, :], prob[:, j, :], sm[:, 12 + j:13 + j], None, ALU.mult)
                op.then_inc(c_["prob"], 1)

        def cross_pe(pe):
            pe.wait_ge(s_evac["cq"], 1)
            for u in range(CAH + 2):
                if u:
                    pe.wait_ge(c_["tr_copied"], u)
                if u < CAH:
                    for qb in range(NB):
                        op = nc.tensor.matmul(ps[:, qb // 2, (qb % 2) * NMEM:(qb % 2 + 1) * NMEM],
                                              caq[:, u, qb * P:(qb + 1) * P], mkT[:, u, :], start=True, stop=True)
                else:
                    gg = u - CAH
                    pe.wait_ge(s_cmk, 64 * (gg + 1))
                    tr_pe(pe, U_SMK[gg])
                    pe.wait_ge(s_ev, U_SMK[gg][-1] + 1)
                    pe.wait_ge(c_["queries"], gg + 1)
                    for b in range(4):
                        for h in range(CAH):
                            op = nc.tensor.matmul(ps[32 * h:32 * h + 32, 0, 0:NMEM], qc[:, b, h, :], smkT[:, b, h, :],
                                                  start=b == 0, stop=b == 3)
                op.then_inc(c_["score"], 1)
                pe.wait_ge(c_["prob"], u + 1)
                for m in range(MT):
                    for j in range(4 if u < CAH else 1):
                        op = nc.tensor.transpose(ps[:, 2 + m, j * P:(j + 1) * P], prob[:, j, m * P:(m + 1) * P], ident)
                op.then_inc(c_["tr"], 1)
                pe.wait_ge(c_["tr_copied"], u + 1)
                if u:
                    pe.wait_ge(c_["out_copied"], u)
                if u < CAH:
                    for m in range(MT):
                        op = nc.tensor.matmul(ps[:, 6, :], mv_tok[:, m, u * P:(u + 1) * P], probT[:, m, :],
                                              start=m == 0, stop=m == MT - 1)
                else:
                    pe.wait_ge(s_cmv, 64 * (u - CAH + 1))
                    for h in range(CAH):
                        for b in range(4):
                            c0 = 32 * h + 8 * b
                            for m in range(MT):
                                op = nc.tensor.matmul(ps[:, 6, c0:c0 + 8], smv_tok[:, b, m, h * P:(h + 1) * P],
                                                      probT[:, m, c0:c0 + 8], start=m == 0, stop=m == MT - 1)
                op.then_inc(c_["out"], 1)

        block = ctx.enter_context(nc.Block())

        @block.sync
        def _(sp):
            sp.dma_start(cc[:, :], shape_consts).then_inc(s_const, 16)
            for k0, v, n in ((G_MIX, g_mix, 8), (G_MEM, g_mem, 8), (G_CA, g_ca, 8), (G_FFN, g_ffn, 8),
                             (G_ATT, g_att, 4), (G_CONV, g_conv, 4)):
                sp.dma_start(vec_rows[k0:k0 + n, :], v[0].rearrange("(k p) -> k p", p=P)).then_inc(s_const, 16)
            sp.dma_start(vec_rows[G_FIN:G_FIN + 8, :], g_fin.rearrange("(k p) -> k p", p=P)).then_inc(s_const, 16)
            sp.dma_start(vec_rows[W_CONV:NVEC, :], w_conv[0].rearrange("j (k p) -> (j k) p", p=P)).then_inc(s_const, 16)
            sp.dma_start(st_rows[0:2 * BS, :], st_conv[0].rearrange("b k n -> (b k) n")).then_inc(s_const, 16)
            sp.dma_start(bias_col[0:HEADS, :], sb_bias[0].rearrange("(h o) -> h o", o=1)).then_inc(s_const, 16)
            sp.dma_start(x_tok[:, 0:NB, :], x_p[0].rearrange("(m p) n -> p m n", p=P)).then_inc(s_x, 16)
            sp.dma_start(x_tok[0:NS, NB, :], x_s.rearrange("b t n -> (b t) n")).then_inc(s_x, 16)
            sp.dma_start(m_tok[:, :, :], mem[0].rearrange("(m p) n -> p m n", p=P)).then_inc(s_m, 16)
            sp.dma_start(ptb[0:1, :], ptab.rearrange("(o b) n -> o (b n)", o=1)).then_inc(s_pt, 16)
            for name in ("in", "ck", "cv"):
                load_stage(sp, name)
            sp.wait_ge(s_pt, 16)
            with sp.Fori(0, GROUPS) as g:
                with sp.Fori(0, CP) as c:
                    for par in range(2):
                        for s in range(2):
                            for j in range(4):
                                page = sp.value_load(ptb[0:1, bass.ds(g * 64 - c * 8 + (32 * s + 28 - 4 * par + j), 1)],
                                                     min_val=0, max_val=N_POOL - 1)
                                if s == 0 and j == 0:
                                    sp.wait_ge(s_ktr, g * 64 + c * 16 + (8 * par + 8))
                                sp.dma_start(k_page[par][:, 4 * s + j:4 * s + j + 1, :],
                                             ck[0, bass.ds(page, 1)].rearrange("o p h d -> p o (h d)"))\
                                    .then_inc(s_kp[par], 16)
                                if s == 0 and j == 0:
                                    sp.wait_ge(m_["pv"], g * 8 + c * 2 + (par + 1))
                                sp.dma_start(v_page[par][:, 4 * s + j:4 * s + j + 1, :],
                                             cv[0, bass.ds(page, 1)].rearrange("o p h d -> p o (h d)"))\
                                    .then_inc(s_vp[par], 16)
            sp.wait_ge(m_["pv"], 8 * GROUPS + 2)
            sp.wait_ge(m_["score"], 9 * GROUPS)
            load_stage(sp, "out")
            for gg in range(2):
                if gg == 0:
                    sp.wait_ge(s_op["out"], 1)
                else:
                    sp.wait_ge(s_tr, U_SMK[0][-1] + 1)
                for b in range(4):
                    sp.dma_start(smk_tok[:, b, :, :],
                                 cmk[0, 4 * gg + b].rearrange("(m p) h d -> p m (h d)", p=P)).then_inc(s_cmk, 16)
                if gg == 0:
                    load_stage(sp, "cq")
                    sp.wait_ge(s_tile["cq"], 4)
                else:
                    sp.wait_ge(c_["out"], 5)
                for b in range(4):
                    sp.dma_start(smv_tok[:, b, :, :],
                                 cmv[0, 4 * gg + b].rearrange("(m p) h d -> p m (h d)", p=P)).then_inc(s_cmv, 16)
            for name in ("co", "gu0", "down0", "gu1", "down1"):
                load_stage(sp, name)
            sp.wait_ge(s_out, 16 * 10)

        @block.gpsimd
        def _(pool):
            for name in NAMES:
                lo_stage(pool, name)

        @block.scalar
        def _(act):
            act.wait_ge(s_set, 2)
            tr_act(act, U_VEC)
            act.wait_ge(s_bmm, 1)
            nc.scalar.activation(bias_p[:, 0, :], ps[:, 6, 0:HEADS], ACT.Copy).then_inc(s_bc, 1)
            nc.scalar.activation(bias_p[:, 1, :], ps[:, 6, 0:HEADS], ACT.Copy, scale=-1.0).then_inc(s_bc, 1)
            nc.scalar.activation(bias_s[:, 0:1], ps[:, 7, 0:1], ACT.Copy).then_inc(s_bc, 1)
            nc.scalar.activation(bias_s[:, 1:2], ps[:, 7, 0:1], ACT.Copy, scale=-1.0).then_inc(s_bc, 1)
            tr_act(act, U_X)
            act.wait_ge(s_ev, U_X[-1] + 1)
            nc.scalar.activation(sq[:, :, :], xT[:, :, :], ACT.Square).then_inc(s_sq["in"], 1)
            tr_act(act, U_M)
            act.wait_ge(s_ev, U_M[-1] + 1)
            nc.scalar.activation(m_sq[:, :, :], mT[:, :, :], ACT.Square).then_inc(s_sq["ck"], 1)
            rms_root(act, "in", rstd[:, :], T, D)
            rms_root(act, "ck", rstd_m[:, :], NMEM, D)
            for name in ("in", "ck", "cv"):
                split_stage(act, name)
            tr_act(act, U_VT)
            tr_act(act, U_KT)
            tr_act(act, U_MK)
            act.wait_ge(s_ev, U_MK[-1] + 1)
            for src, dst_p, dst_s in ((v_tok, out_v_p, out_v_s), (k_rows, out_k_p, out_k_s)):
                act.dma_start(dst_p[0, 0].rearrange("(m p) h d -> p m (h d)", p=P), src[:, 0:NB, :]).then_inc(s_out, 16)
                act.dma_start(dst_s[0].rearrange("b t h d -> (b t) (h d)"), src[0:NS, NB, :]).then_inc(s_out, 16)
            for src, dst in ((mk_rows, out_mk), (mv_tok, out_mv)):
                act.dma_start(dst[0, 0].rearrange("(m p) h d -> p m (h d)", p=P), src[:, :, :]).then_inc(s_out, 16)
            nc.scalar.preload_act_table(ACT.Sigmoid)
            with act.Fori(0, HP) as hp:
                act.wait_ge(p_["score"], hp * 4 + 1)
                act.wait_ge(s_bc, 4)
                nc.scalar.activation(q_fix[:, :], pT[:, bass.ds(hp + T_Q, 1), 0:SEQ].rearrange("p o n -> p (o n)"),
                                     ACT.Copy).then_inc(p_["qk_fixed"], 1)
                nc.scalar.activation(k_fix[:, :], pT[:, bass.ds(hp + T_K, 1), 0:SEQ].rearrange("p o n -> p (o n)"),
                                     ACT.Copy).then_inc(p_["qk_fixed"], 1)
                nc.scalar.activation(bias_fix[:, :, :], bias_p[:, :, bass.ds(hp * 2, 2)], ACT.Copy)\
                    .then_inc(p_["bias_fixed"], 1)
                act.wait_ge(p_["bias_fixed"], hp + 1)

                def sigmoids(qb):
                    nk = (qb + 1) * P
                    act.wait_ge(p_["score"], hp * 4 + (qb + 2))
                    for h2 in range(2):
                        act.wait_ge(p_["weight"], hp * 8 + (2 * qb + h2 + 1))
                        z = ps[:, 2 * (qb % 2) + h2, 0:nk]
                        nc.scalar.activation(beta[:, h2, 0:nk], z, ACT.Sigmoid, scale=SB_SCALE,
                                             bias=bias_fix[:, 0, h2:h2 + 1]).then_inc(p_["beta"], 1)
                        nc.scalar.activation(om[:, h2, 0:nk], z, ACT.Sigmoid, scale=-SB_SCALE,
                                             bias=bias_fix[:, 1, h2:h2 + 1]).then_inc(p_["om"], 1)
                for qb in range(NB):
                    sigmoids(qb)
                    act.wait_ge(p_["tr"], hp * 4 + (qb + 2))
                    nk = (qb + 1) * P
                    nc.scalar.activation(awT[:, 0, 0:qb + 1, :], tiled(ps[:, 4, 0:nk]), ACT.Copy)\
                        .then_inc(p_["copied_a"], 1)
                act.wait_ge(p_["out"], hp + 2)
                act.wait_ge(s_bc, 4)
                nc.scalar.activation(pT[:, bass.ds(hp + T_A, 1), 0:SEQ].rearrange("p o n -> p (o n)"), ps[:, 6, :],
                                     ACT.Copy).then_inc(p_["out_copied"], 1)

            def copy_k(g, c_pages, par):
                for q in range(0, 8, 2):
                    if q == 0:
                        act.wait_ge(m_["score"], c_pages + g + 1)
                    act.wait_ge(s_ktr, c_pages * 8 + (q + 17))
                    nc.scalar.activation(kT[:, q // 4, :, (q % 4) * P:(q % 4 + 1) * P], tiled(ps[:, KB[q % 4], :]),
                                         ACT.Copy).then_inc(m_["k_copied_a"], 1)

            def sample_sigmoids(S, w):
                act.wait_ge(m_["score"], S + 1)
                act.wait_ge(m_["weight"], S + 1)
                nc.scalar.activation(beta[:, 0, 0:w], ps[:, 3, 0:w], ACT.Sigmoid, scale=SB_SCALE,
                                     bias=bias_s[:, 0:1]).then_inc(m_["beta"], 1)
                nc.scalar.activation(om[:, 0, 0:w], ps[:, 3, 0:w], ACT.Sigmoid, scale=-SB_SCALE,
                                     bias=bias_s[:, 1:2]).then_inc(m_["om"], 1)

            def copy_weights(S, new):
                act.wait_ge(m_["tr"], S + 2)
                if new:
                    nc.scalar.activation(awT[:, 0, 0, :], ps[:, 4, 0:P], ACT.Copy).then_inc(m_["tr_copied"], 1)
                else:
                    nc.scalar.activation(awT[:, 0, :, :], tiled(ps[:, 4, :]), ACT.Copy).then_inc(m_["tr_copied"], 1)

            with act.Fori(0, GROUPS) as g:
                sample_sigmoids(g * 9, NS)
                copy_k(g, g * 8, 0)
                copy_weights(g * 9, True)
                with act.Fori(0, 3) as c:
                    for par in range(2):
                        sample_sigmoids(g * 9 + c * 2 + (par + 1), SEQ)
                        copy_k(g, g * 8 + c * 2 + (par + 1), 1 - par)
                        copy_weights(g * 9 + c * 2 + (par + 1), False)
                sample_sigmoids(g * 9 + 7, SEQ)
                copy_k(g, g * 8 + 7, 1)
                copy_weights(g * 9 + 7, False)
                sample_sigmoids(g * 9 + 8, SEQ)
                copy_weights(g * 9 + 8, False)

            act.wait_ge(s_cs, 1)
            tr_act(act, U_CS)
            act.wait_ge(s_ev, U_CS[-1] + 1)
            act.dma_start(out_c_p[0, 0], cs_rows[0:2, :]).then_inc(s_out, 16)
            act.dma_start(out_c_s[0].rearrange("b k n -> (b k) n"), cs_rows[2:18, :]).then_inc(s_out, 16)
            act.wait_ge(m_["rows_copied"], GROUPS + 1)
            nc.scalar.activation(sq_c[:, :, :], pT[:, T_C:T_C + KC, :], ACT.Square).then_inc(s_sq["conv"], 1)
            nc.scalar.activation(sq_a[:, :, :], pT[:, T_A:T_A + KC, :], ACT.Square).then_inc(s_sq["att"], 1)
            rms_root(act, "conv", rstd[:, :], T, CH)
            act.wait_ge(s_evac["in"], 2)
            rms_root(act, "att", rstd[:, :], T, CH)
            split_stage(act, "out")
            act.wait_ge(s_evac["out"], 1)
            nc.scalar.activation(sq_ca[:, :, :], xT[:, :, :], ACT.Square).then_inc(s_sq["cq"], 1)
            rms_root(act, "cq", rstd[:, :], T, D)
            split_stage(act, "cq")
            cross_act(act)
            split_stage(act, "co")
            act.wait_ge(s_evac["co"], 1)
            nc.scalar.activation(sq_ca[:, :, :], xT[:, :, :], ACT.Square).then_inc(s_sq["gu0"], 1)
            rms_root(act, "gu0", rstd[:, :], T, D)

            def sigmoid_of(name):
                def more(i):
                    for t in range(2):
                        act.wait_ge(s_free[name], i * 4 + (t + 3))
                        nc.scalar.activation(sbuf_[:, t, :], gbuf[:, t, :], ACT.Sigmoid).then_inc(s_sig, 1)
                return more
            nc.scalar.preload_act_table(ACT.Sigmoid)
            split_stage(act, "gu0", sigmoid_of("gu0"))
            split_stage(act, "down0")
            split_stage(act, "gu1", sigmoid_of("gu1"))
            split_stage(act, "down1")
            act.wait_ge(s_evac["down1"], 1)
            nc.scalar.activation(sq[:, :, :], xT[:, :, :], ACT.Square).then_inc(s_sq["fin"], 1)
            rms_root(act, "fin", rstd[:, :], T, D)
            tr_act(act, U_Y)
            act.wait_ge(s_ev, U_Y[-1] + 1)
            act.dma_start(y_p[0].rearrange("(m p) n -> p m n", p=P), y_rows[:, 0:NB, :]).then_inc(s_out, 16)
            act.dma_start(y_s.rearrange("b t n -> (b t) n"), y_rows[0:NS, NB, :]).then_inc(s_out, 16)

        @block.vector
        def _(dve):
            nc.vector.memset(ones[:, :], 1.0).then_inc(s_set, 1)
            nc.vector.memset(cst[:, :], EPS).then_inc(s_set, 1)
            grant(s_free["in"], 2)
            dve.wait_ge(s_const, 16 * 11)
            nc.vector.tensor_scalar(bias_dg[0:HEADS, :], ident[0:HEADS, 0:HEADS], bias_col[0:HEADS, 0:1], None,
                                    ALU.mult).then_inc(s_set, 1)
            dve.wait_ge(s_ev, U_X[-1] + 1)
            scale_split(dve, xT, G_MIX, h_hi, h_lo, KD, s_op["in"])
            rms_sum(dve, "in", sq, KD)
            dve.wait_ge(s_ev, U_M[-1] + 1)
            scale_split(dve, mT, G_MEM, m_hi, m_lo, KD, s_op["ck"])
            rms_sum(dve, "ck", m_sq, KD)
            rms_inv(dve, "in", rstd[:, :])
            rms_inv(dve, "ck", rstd_m[:, :])
            evac_scaled(dve, "in", pT, rstd[:, :])
            grant(s_evac["in"], 1)
            grant(s_free["ck"], 2)
            evac_mem(dve, "ck", mkT)
            grant(s_free["cv"], 2)
            evac_mem(dve, "cv", mvT)
            grant(s_evac["cv"], 1)

            dve.wait_ge(s_dve, steps[0])
            step(dve, nc.vector.tensor_tensor(pT[:, T_U:T_U + KC, :], pT[:, T_C:T_C + KC, :], pT[:, T_U:T_U + KC, :],
                                              ALU.mult))
            for k in range(KC):
                w = [cvec[:, W_CONV + 4 * j + k:W_CONV + 4 * j + k + 1] for j in range(3)]
                u, y = pT[:, T_U + k, :], pT[:, T_C + k, :]
                us, ys = (a[:, SEQ:T].rearrange("p (b t) -> p b t", t=TS) for a in (u, y))
                st = stT[:, k, :].rearrange("p (b j) -> p b j", j=2)

                def add(dst, src, wj):
                    step(dve, nc.vector.scalar_tensor_tensor(out=dst, in0=src, scalar=wj, in1=dst,
                                                             op0=ALU.mult, op1=ALU.add))
                step(dve, nc.vector.tensor_scalar(y, u, w[2], None, ALU.mult))
                add(y[:, 1:SEQ], u[:, 0:SEQ - 1], w[1])
                add(y[:, 2:SEQ], u[:, 0:SEQ - 2], w[0])
                add(ys[:, :, 1:TS], us[:, :, 0:TS - 1], w[1])
                add(ys[:, :, 0:1], st[:, :, 1:2], w[1])
                add(ys[:, :, 2:TS], us[:, :, 0:TS - 2], w[0])
                add(ys[:, :, 0:2], st[:, :, 0:2], w[0])
                nc.vector.tensor_copy(cs[:, k, 0:2], u[:, SEQ - 2:SEQ])
                nc.vector.tensor_copy(cs[:, k, 2:18].rearrange("p (b j) -> p b j", j=2), us[:, :, TS - 2:TS])
            step(dve, nc.vector.tensor_tensor(pT[:, T_C:T_C + KC, :], pT[:, T_C:T_C + KC, :], pT[:, T_B:T_B + KC, :],
                                              ALU.mult))
            grant(s_cs, 1)

            dve.wait_ge(s_tile["cv"], 4)
            nc.vector.memset(run[:, :, :], 1.0)
            step(dve, nc.vector.memset(q_bd[:, :, :, :], 0.0))
            dve.wait_ge(s_ev, U_MK[-1] + 1)
            nc.vector.memset(v_tok[NS:P, NB, :], 0.0)
            for name, n in (("score", 1), ("weight", 2), ("tr", 1), ("out", 1), ("out_copied", 1)):
                grant(p_[name], n)
            with dve.Fori(0, HP) as hp:
                dve.wait_ge(p_["out"], hp + 1)
                nc.vector.tensor_copy(v_fix[:, :, :], v_tok[:, 0:NB, bass.ds(hp * P, P)]).then_inc(p_["v_fixed"], 1)
                for qb in range(NB):
                    nk = (qb + 1) * P
                    for h2 in range(2):
                        dve.wait_ge(p_["om"], hp * 8 + (2 * qb + h2 + 1))
                        nc.vector.tensor_tensor_scan(run[:, h2, 0:nk][:, ::-1], om[:, h2, 0:nk][:, ::-1],
                                                     om[:, h2, 0:nk][:, ::-1], 1.0, ALU.mult, ALU.bypass)\
                            .then_inc(p_["scan"], 1)
                        dve.wait_ge(p_["scan"], hp * 8 + (2 * qb + h2 + 1))
                        if h2 == 0:
                            dve.wait_ge(p_["tr"], hp * 4 + (qb + 1))
                        nc.vector.tensor_tensor(aw[:, h2, 0:nk], beta[:, h2, 0:nk], run[:, h2, 1:nk + 1], ALU.mult)\
                            .then_inc(p_["weight"], 1)
                    dve.wait_ge(p_["tr"], hp * 4 + (qb + 2))
                    nc.vector.tensor_copy(awT[:, 1, 0:qb + 1, :], tiled(ps[:, 5, 0:nk])).then_inc(p_["copied_d"], 1)

            dve.wait_ge(p_["out_copied"], HP + 1)
            dve.wait_ge(s_out, 16 * 6)
            grant(s_ktr, 16)
            for name, n in (("k_copied_a", 2), ("k_copied_d", 2), ("weight", 1),
                            ("tr", 1), ("tr_copied", 1), ("pv", 2), ("rows", 1), ("rows_copied", 1)):
                grant(m_[name], n)

            def copy_k(c_pages, g):
                for q in range(1, 8, 2):
                    if q == 1:
                        dve.wait_ge(m_["score"], c_pages + g + 1)
                    dve.wait_ge(s_ktr, c_pages * 8 + (q + 17))
                    nc.vector.tensor_copy(kT[:, q // 4, :, (q % 4) * P:(q % 4 + 1) * P], tiled(ps[:, KB[q % 4], :]))\
                        .then_inc(m_["k_copied_d"], 1)

            def weights(S, R, w):
                dve.wait_ge(m_["om"], S + 1)
                if w == NS:
                    nc.vector.memset(run[:, 0, w:w + 1], 1.0).then_inc(m_["run"], 1)
                    dve.wait_ge(m_["run"], R + 1)
                    R = R + 1
                nc.vector.tensor_tensor_scan(run[:, 0, 0:w][:, ::-1], om[:, 0, 0:w][:, ::-1], om[:, 0, 0:w][:, ::-1],
                                             run[:, 0, w:w + 1], ALU.mult, ALU.bypass).then_inc(m_["run"], 1)
                dve.wait_ge(m_["run"], R + 1)
                dve.wait_ge(m_["tr"], S + 1)
                nc.vector.tensor_tensor(aw[:, 0, 0:w], beta[:, 0, 0:w], run[:, 0, 1:w + 1], ALU.mult)\
                    .then_inc(m_["weight"], 1)
                dve.wait_ge(m_["weight"], S + 2)
                nc.vector.tensor_copy(run[:, 0, SEQ:SEQ + 1], run[:, 0, 0:1]).then_inc(m_["run"], 1)
                dve.wait_ge(m_["run"], R + 2)

            with dve.Fori(0, GROUPS) as g:
                dve.wait_ge(m_["rows_copied"], g + 1)
                for s in range(2):
                    for h2 in range(2):
                        op = nc.vector.tensor_copy(
                            q_bd[64 * h2:64 * h2 + 64, s, :, 16 * s + 8 * h2:16 * s + 8 * h2 + 8],
                            pT[64 * h2:64 * h2 + 64, T_Q:T_Q + HP, bass.ds(g * 16 + (SEQ + 8 * s), 8)])
                op.then_inc(m_["queries"], 1)
                weights(g * 9, g * 19, NS)
                copy_k(g * 8, g)
                with dve.Fori(0, 3) as c:
                    for par in range(2):
                        weights(g * 9 + c * 2 + (par + 1), g * 19 + c * 4 + (3 + 2 * par), SEQ)
                        copy_k(g * 8 + c * 2 + (par + 1), g)
                weights(g * 9 + 7, g * 19 + 15, SEQ)
                copy_k(g * 8 + 7, g)
                weights(g * 9 + 8, g * 19 + 17, SEQ)
                dve.wait_ge(m_["pv"], g * 8 + 10)
                nc.vector.tensor_copy(o_pair[:, :, :], ps[:, 6:8, 0:P]).then_inc(m_["rows"], 1)
                dve.wait_ge(m_["rows_tr"], g + 1)
                for s in range(2):
                    for h2 in range(2):
                        rows = tiled(ps[64 * h2:64 * h2 + 64, 3, s * P:(s + 1) * P], 32)
                        op = nc.vector.tensor_copy(
                            pT[64 * h2:64 * h2 + 64, T_A:T_A + HP, bass.ds(g * 16 + (SEQ + 8 * s), 8)],
                            rows[:, :, 16 * s + 8 * h2:16 * s + 8 * h2 + 8])
                op.then_inc(m_["rows_copied"], 1)

            grant(s_free["out"], 2)
            rms_sum(dve, "conv", sq_c, KC)
            rms_sum(dve, "att", sq_a, KC)
            for name, t0, g0, k0 in (("conv", T_C, G_CONV, 4), ("att", T_A, G_ATT, 0)):
                rms_inv(dve, name, rstd[:, :])
                for k in range(KC):
                    step(dve, nc.vector.scalar_tensor_tensor(out=nrm[:, :], in0=pT[:, t0 + k, :],
                                                             scalar=cvec[:, g0 + k:g0 + k + 1], in1=rstd[:, :],
                                                             op0=ALU.mult, op1=ALU.mult))
                    step(dve, nc.vector.tensor_copy(h_hi[:, k0 + k, :], nrm[:, :]))
                    step(dve, nc.vector.tensor_tensor(h_lo[:, k0 + k, :], nrm[:, :], h_hi[:, k0 + k, :].bitcast(F32),
                                                      ALU.subtract))
                grant(s_evac["in"], 1)
            grant(s_op["out"], 1)
            evac_residual(dve, "out")
            grant(s_evac["out"], 1)
            grant(s_free["cq"], 2)
            dve.wait_ge(s_evac["out"], 1)
            scale_split(dve, xT, G_CA, h_hi, h_lo, KD, s_op["cq"])
            rms_sum(dve, "cq", sq_ca, KD)
            rms_inv(dve, "cq", rstd[:, :])
            evac_scaled(dve, "cq", caq, rstd[:, :])
            grant(s_evac["cq"], 1)
            dve.wait_ge(s_evac["cq"], 1)
            cross_dve(dve)
            grant(s_free["co"], 2)
            dve.wait_ge(c_["out_copied"], CAH + 2)
            for k in range(CAH):
                step(dve, nc.vector.tensor_copy(h_hi[:, k, :], caoT[:, k, :]))
                op = nc.vector.tensor_tensor(h_lo[:, k, :], caoT[:, k, :], h_hi[:, k, :].bitcast(F32), ALU.subtract)
            op.then_inc(s_op["co"], 1)
            evac_residual(dve, "co")
            grant(s_evac["co"], 1)
            grant(s_free["gu0"], 2)
            dve.wait_ge(s_evac["co"], 1)
            scale_split(dve, xT, G_FFN, h_hi, h_lo, KD, s_op["gu0"])
            rms_sum(dve, "gu0", sq_ca, KD)
            rms_inv(dve, "gu0", rstd[:, :])
            for half in range(2):
                hidden_dve(dve, half)
                name = f"down{half}"
                grant(s_free[name], 2)
                evac_residual(dve, name)
                if half == 0:
                    grant(s_free["gu1"], 2)
            grant(s_evac["down1"], 1)
            rms_sum(dve, "fin", sq, KD)
            rms_inv(dve, "fin", rstd[:, :])
            for k in range(KD):
                op = nc.vector.scalar_tensor_tensor(out=yT[:, k, :], in0=xT[:, k, :],
                                                    scalar=cvec[:, G_FIN + k:G_FIN + k + 1], in1=rstd[:, :],
                                                    op0=ALU.mult, op1=ALU.mult)
            op.then_inc(s_y, 1)

        @block.tensor
        def _(pe):
            pe.wait_ge(s_const, 16 * 11)
            tr_pe(pe, U_VEC)
            pe.wait_ge(s_set, 3)
            nc.tensor.matmul(ps[:, 6, 0:HEADS], ones[0:HEADS, :], bias_dg[0:HEADS, :], start=True, stop=True)
            nc.tensor.matmul(ps[:, 7, 0:1], cc[0:HEADS, C_SEL:C_SEL + P], bias_col[0:HEADS, :],
                             start=True, stop=True).then_inc(s_bmm, 1)
            pe.wait_ge(s_x, 32)
            tr_pe(pe, U_X)
            pe.wait_ge(s_m, 16)
            tr_pe(pe, U_M)
            pe.wait_ge(s_bc, 4)
            rms_pe(pe, "in", sq, T)
            rms_pe(pe, "ck", m_sq, NMEM, "in")
            pe.wait_ge(s_op["in"], 1)
            gemm(pe, "in", h_hi, h_lo)
            pe.wait_ge(s_op["ck"], 1)
            gemm(pe, "ck", m_hi, m_lo, NMEM)
            gemm(pe, "cv", m_hi, m_lo, NMEM)
            tr_pe(pe, U_VT)
            tr_pe(pe, U_KT)
            pe.wait_ge(s_evac["cv"], 1)
            tr_pe(pe, U_MK)

            with pe.Fori(0, HP) as hp:
                def score(qb):
                    for h2 in range(2):
                        r = slice(64 * h2, 64 * h2 + 64)
                        z = ps[:, 2 * (qb % 2) + h2, :]
                        nc.tensor.matmul(z[:, 0:(qb + 1) * P], q_fix[r, qb * P:(qb + 1) * P], k_fix[r, 0:(qb + 1) * P],
                                         start=True, stop=False)
                    for h2 in range(2):
                        z = ps[:, 2 * (qb % 2) + h2, :]
                        op = nc.tensor.matmul(z[:, qb * P:(qb + 1) * P], ident, cc[:, C_CMASK:C_CMASK + P],
                                              start=False, stop=True)
                    op.then_inc(p_["score"], 1)

                pe.wait_ge(p_["qk_fixed"], hp * 2 + 2)
                score(0)
                for qb in range(NB):
                    if qb + 1 < NB:
                        score(qb + 1)
                    pe.wait_ge(p_["weight"], hp * 8 + (2 * qb + 4))
                    for h2 in range(2):
                        for kb in range(qb + 1):
                            op = nc.tensor.transpose(ps[:, 4 + h2, kb * P:(kb + 1) * P], aw[:, h2, kb * P:(kb + 1) * P],
                                                     ident)
                    op.then_inc(p_["tr"], 1)
                    if qb == 0:
                        pe.wait_ge(p_["v_fixed"], hp + 1)
                        pe.wait_ge(p_["out_copied"], hp + 1)
                    pe.wait_ge(p_["copied_a"], hp * 4 + (qb + 1))
                    pe.wait_ge(p_["copied_d"], hp * 4 + (qb + 1))
                    for h2 in range(2):
                        for kb in range(qb + 1):
                            op = nc.tensor.matmul(ps[64 * h2:64 * h2 + 64, 6, qb * P:(qb + 1) * P],
                                                  v_fix[:, kb, 64 * h2:64 * h2 + 64], awT[:, h2, kb, :],
                                                  start=kb == 0, stop=kb == qb)
                op.then_inc(p_["out"], 1)

            def k_transposes(C, par):
                for q in range(8):
                    if q == 0:
                        pe.wait_ge(s_kp[par], (C - par) * 64 + 128)
                    pe.wait_ge(m_["k_copied_a" if q % 2 == 0 else "k_copied_d"], C * 4 + (q // 2 + 1))
                    for j in range(HP):
                        op = nc.tensor.transpose(ps[:, KB[q % 4], j * P:(j + 1) * P], k_page[par][:, q, j * P:(j + 1) * P],
                                                 ident)
                    op.then_inc(s_ktr, 1)

            def new_scores(g):
                pe.wait_ge(m_["queries"], g + 1)
                nc.tensor.matmul(ps[:, 3, 0:NS], ident, cc[:, bass.ds(g * NS + C_SMASK, NS)], start=True, stop=False)
                for s in range(2):
                    for j in range(HP):
                        op = nc.tensor.matmul(ps[32 * j:32 * j + 32, 3, 0:NS], q_bd[:, s, j, :],
                                              pT[:, T_K + j, SEQ:T], start=False, stop=s == 1)
                op.then_inc(m_["score"], 1)

            def scores(C):
                pe.wait_ge(m_["k_copied_a"], C * 4 + 6)
                pe.wait_ge(m_["k_copied_d"], C * 4 + 6)
                for s in range(2):
                    for j in range(HP):
                        op = nc.tensor.matmul(ps[32 * j:32 * j + 32, 3, :], q_bd[:, s, j, :], kT[:, s, j, :],
                                              start=s == 0, stop=s == 1)
                op.then_inc(m_["score"], 1)

            def weight_transposes(S, new=False):
                pe.wait_ge(m_["weight"], S + 2)
                pe.wait_ge(m_["tr_copied"], S + 1)
                if new:
                    op = nc.tensor.transpose(ps[:, 4, 0:P], aw[:, 0, 0:P], ident)
                else:
                    for j in range(4):
                        op = nc.tensor.transpose(ps[:, 4, j * P:(j + 1) * P], aw[:, 0, j * P:(j + 1) * P], ident)
                op.then_inc(m_["tr"], 1)

            def new_sums(g):
                pe.wait_ge(m_["tr_copied"], g * 9 + 2)
                pe.wait_ge(m_["rows"], g + 1)
                for s in range(2):
                    for j in range(HP):
                        nc.tensor.matmul(ps[32 * j:32 * j + 32, 6 + s, 0:P], awT[:, 0, 0, 32 * j:32 * j + 32],
                                         v_tok[:, NB, j * P:(j + 1) * P], start=True, stop=False)

            def sums(C, S, par, last=False):
                pe.wait_ge(m_["tr_copied"], S + 2)
                pe.wait_ge(s_vp[par], (C - par) * 64 + 128)
                for s in range(2):
                    for q in range(4):
                        for j in range(HP):
                            op = nc.tensor.matmul(ps[32 * j:32 * j + 32, 6 + s, 0:P], awT[:, 0, q, 32 * j:32 * j + 32],
                                                  v_page[par][:, 4 * s + q, j * P:(j + 1) * P],
                                                  start=False, stop=last and q == 3)
                op.then_inc(m_["pv"], 1)

            with pe.Fori(0, GROUPS) as g:
                new_scores(g)
                k_transposes(g * 8, 0)
                weight_transposes(g * 9, True)
                scores(g * 8)
                new_sums(g)
                with pe.Fori(0, 3) as c:
                    for par in range(2):
                        k_transposes(g * 8 + c * 2 + (par + 1), 1 - par)
                        weight_transposes(g * 9 + c * 2 + (par + 1))
                        scores(g * 8 + c * 2 + (par + 1))
                        sums(g * 8 + c * 2 + par, g * 9 + c * 2 + (par + 1), par)
                k_transposes(g * 8 + 7, 1)
                weight_transposes(g * 9 + 7)
                scores(g * 8 + 7)
                sums(g * 8 + 6, g * 9 + 7, 0)
                weight_transposes(g * 9 + 8)
                sums(g * 8 + 7, g * 9 + 8, 1, True)
                pe.wait_ge(m_["rows"], g + 2)
                for s in range(2):
                    op = nc.tensor.transpose(ps[:, 3, s * P:(s + 1) * P], o_pair[:, s, :], ident)
                op.then_inc(m_["rows_tr"], 1)

            pe.wait_ge(s_cs, 1)
            tr_pe(pe, U_CS)
            rms_pe(pe, "conv", sq_c, T)
            rms_pe(pe, "att", sq_a, T, "conv")
            pe.wait_ge(s_op["out"], 1)
            gemm(pe, "out", h_hi, h_lo)
            rms_pe(pe, "cq", sq_ca, T)
            pe.wait_ge(s_op["cq"], 1)
            gemm(pe, "cq", h_hi, h_lo)
            cross_pe(pe)
            pe.wait_ge(s_op["co"], 1)
            gemm(pe, "co", h_hi, h_lo)
            rms_pe(pe, "gu0", sq_ca, T)
            pe.wait_ge(s_op["gu0"], 1)
            for half in range(2):
                gemm(pe, f"gu{half}", h_hi, h_lo)
                pe.wait_ge(s_hid, half + 1)
                gemm(pe, f"down{half}", f_hi, f_lo)
            rms_pe(pe, "fin", sq, T)
            pe.wait_ge(s_y, 1)
            tr_pe(pe, U_Y)


def shape_table():
    c = np.zeros((P, NCONST), np.float32)
    i = np.arange(P)
    c[i, C_ID + i] = 1.0
    seq, step_ = (i // 16) % 2, i % 8
    for g in range(GROUPS):
        for b in range(BS):
            for t in range(TS):
                seen = (b == 2 * g + seq) & (t < step_)
                c[:, C_SMASK + g * NS + b * TS + t] = np.where(seen, 0.0, -1e30)
    c[:, C_CMASK:C_CMASK + P] = np.where(i[None, :] < i[:, None], 0.0, -1e30)
    head = 2 * (i // 32) + (i // 8) % 2
    c[head, C_SEL + i] = 1.0
    return c


_INS = ["x_prompt", "x_sample", "mem_prompt", "cache_sb_k", "cache_sb_v", "cache_mem_k", "cache_mem_v", "state_conv",
        "page_table", "g_mix", "w_in", "sb_bias", "w_conv", "g_attn_out", "g_conv_out", "w_out", "g_mem", "g_ca",
        "w_cq", "w_ck", "w_cv", "w_co", "g_ffn", "w_gate", "w_up", "w_down", "g_final"]
_OUTS = [(1, SEQ, D), (BS, TS, D), (1, 1, SEQ, HEADS, HD), (1, 1, SEQ, HEADS, HD), (1, 1, 2, CH),
         (1, 1, NMEM, CAH, P), (1, 1, NMEM, CAH, P), (1, BS, TS, HEADS, HD), (1, BS, TS, HEADS, HD), (1, BS, 2, CH)]


def kernel(**inputs):
    import concourse.bacc as bacc
    from concourse.bass_utils import run_bass_kernel_spmd

    nc = bacc.Bacc("TRN2", target_bir_lowering=False, num_devices=1)
    arrays, args = {}, []
    for name in _INS:
        a = np.ascontiguousarray(inputs[name])
        arrays[f"in_{name}"] = a
        args.append(nc.dram_tensor(f"in_{name}", a.shape, mybir.dt.from_np(a.dtype), kind="ExternalInput").ap())
    arrays["shape_constants"] = shape_table()
    args.append(nc.dram_tensor("shape_constants", (P, NCONST), F32, kind="ExternalInput").ap())
    for i, shape in enumerate(_OUTS):
        args.append(nc.dram_tensor(f"out_{i}", shape, F32, kind="ExternalOutput").ap())
    hybrid_layer(nc, *args)
    r = run_bass_kernel_spmd(nc, [arrays], core_ids=[0])
    return tuple(r.results[0][f"out_{i}"] for i in range(len(_OUTS)))
```

```python
from contextlib import ExitStack

import numpy as np

import concourse.bass as bass
from concourse import mybir

F32 = mybir.dt.float32
F32R = mybir.dt.float32r
I32 = mybir.dt.int32
ALU = mybir.AluOpType
ACT = mybir.ActivationFunctionType
AX = mybir.AxisListType

P = 128
D = 1024
KD = D // P
SEQ = 512
NB = SEQ // P
BS, TS = 8, 8
NS = BS * TS
T = SEQ + NS
HALF = T // 2
HEADS, HD = 8, 64
HP = HEADS * HD // P
CH = 512
KC = CH // P
PAGES = 32
NMEM = 256
MT = NMEM // P
CAH = 4
SB_SCALE = HD ** -0.5
CA_SCALE = P ** -0.5
EPS = 1e-6
GROUPS = BS // 2
CP = 4
SLOTW = 256
N_POOL = 320

G_MIX, G_MEM, G_CA, G_FFN, G_FIN, G_ATT, G_CONV, W_CONV, NVEC = 0, 8, 16, 24, 32, 40, 44, 48, 60
C_ID, C_SMASK, C_CMASK, C_SEL, NCONST = 0, 128, 384, 512, 640


def hybrid_layer(nc, x_p, x_s, mem, ck, cv, cmk, cmv, st_conv, ptab, g_mix, w_in, sb_bias, w_conv,
                 g_att, g_conv, w_out, g_mem, g_ca, w_cq, w_ck, w_cv, w_co, g_ffn, w_gate, w_up,
                 w_down, g_fin, shape_consts,
                 y_p, y_s, out_k_p, out_v_p, out_c_p, out_mk, out_mv, out_k_s, out_v_s, out_c_s):
    ctx = ExitStack()
    with ctx:
        lo_addr = (nc.sbuf_base + 63) // 64 * 64
        size = 207 * 1024 - 128
        ctx.enter_context(nc.sbuf_tensor("arena", [P, size // 4], F32))
        cursor = [lo_addr]

        def region(n):
            off = cursor[0]
            cursor[0] += n
            assert cursor[0] <= lo_addr + size, cursor[0] - lo_addr
            return off

        def at(name, shape, off, dt=F32):
            return nc.alloc_sbuf_tensor_at(name, [P] + shape, dt, offset=off)

        def sem(name):
            return ctx.enter_context(nc.semaphore(name))

        R_X, R_H, R_P = region(KD * T * 4), region(2 * KD * T * 4), region(24 * T * 4)
        R_W, R_M, R_K = region(6 * 8192), region(16384), region(8192)
        R_V, R_C, R_R = region(14336), region(4096), region(2304 + 1024 + 1024 + 320)
        xT = at("xT", [KD, T], R_X)
        h_hi = at("h_hi", [KD, T], R_H, F32R)
        h_lo = at("h_lo", [KD, T], R_H + KD * T * 4, F32R)
        pT = at("pT", [24, T], R_P)
        w_raw = [at(f"w_raw{i}", [8, SLOTW], R_W + i * 8192) for i in range(2)]
        w_hi = [at(f"w_hi{i}", [8, SLOTW], R_W + (2 + i) * 8192, F32R) for i in range(2)]
        w_lo = [at(f"w_lo{i}", [8, SLOTW], R_W + (4 + i) * 8192, F32R) for i in range(2)]
        rstd = at("rstd", [T], R_R)
        rstd_m = at("rstd_m", [NMEM], R_R + 2304)
        ptb = at("ptb", [BS * PAGES], R_R + 3328, I32)
        cs = at("cs", [KC, 18], R_R + 4352)
        sq = at("sq", [KD, T], R_P)
        x_tok = at("x_tok", [5, D], R_P + 18432)
        mT = at("mT", [KD, NMEM], R_P + 38912)
        m_sq = at("m_sq", [KD, NMEM], R_P + 47104)
        m_tok = at("m_tok", [MT, D], R_V)
        st_rows = at("st_rows", [CH], R_V + 8192)
        vec_rows = at("vec_rows", [P], R_V + 10240)
        m_hi = at("m_hi", [KD, NMEM], R_M, F32R)
        m_lo = at("m_lo", [KD, NMEM], R_M + 8192, F32R)
        mkT = at("mkT", [CAH, NMEM], R_K)
        mv_tok = at("mv_tok", [MT, CH], R_K + 4096)
        v_tok = at("v_tok", [5, CH], R_V)
        mvT = at("mvT", [CAH, NMEM], R_V + 10240)
        k_rows = at("k_rows", [5, CH], R_H)
        mk_rows = at("mk_rows", [MT, CH], R_H + 10240)
        cs_rows = at("cs_rows", [CH], R_V)
        T_Q, T_K, T_A, T_B, T_C, T_U = 0, 4, 8, 12, 16, 20
        beta = at("beta", [2, SEQ], R_P + T_B * T * 4)
        om = at("om", [2, SEQ], R_P + T_B * T * 4 + 4096)
        aw = at("aw", [2, SEQ], R_P + T_U * T * 4)
        awT = at("awT", [2, 4, P], R_P + T_U * T * 4 + 4096)
        run = at("run", [2, SEQ + 1], R_M)
        q_fix = at("q_fix", [SEQ], R_M + 4224)
        k_fix = at("k_fix", [SEQ], R_M + 6272)
        v_fix = at("v_fix", [4, P], R_M + 8320)
        q_bd = at("q_bd", [2, HP, 32], R_M + 10368)
        beta_s = at("beta_s", [SEQ], R_M + 11392)
        om_s = at("om_s", [SEQ], R_M + 13440)
        aw_s = at("aw_s", [SEQ], R_H + 32768)
        awT_s = at("awT_s", [4, P], R_H + 34816)
        zeros = at("zeros", [32], region(128))
        run_s = at("run_s", [SEQ + 1], region(2080))
        o_pair = at("o_pair", [2, P], region(1024))
        k_page = [at(f"k_page{i}", [8, CH], R_H + i * 16384) for i in range(2)]
        v_page = [at(f"v_page{i}", [8, CH], R_W + i * 16384) for i in range(2)]
        kT = at("kT", [2, HP, SEQ], R_W + 32768)
        sq_a = at("sq_a", [KC, T], R_P)
        sq_c = at("sq_c", [KC, T], R_P + KC * T * 4)
        nrm = at("nrm", [T], R_M)
        caq = at("caq", [CAH, T], R_P)
        caoT = at("caoT", [CAH, T], R_P + CAH * T * 4)
        R_CA = R_P + 2 * CAH * T * 4
        prob = at("prob", [4, NMEM], R_CA)
        probT = at("probT", [MT, SEQ], R_CA + 4096)
        qc = at("qc", [4, CAH, 32], R_CA + 8192)
        sq_ca = at("sq_ca", [KD, T], R_CA + 10240)
        smk_tok = at("smk_tok", [4, MT, CH], R_M)
        smkT = at("smkT", [4, CAH, NMEM], R_H)
        smv_tok = at("smv_tok", [4, MT, CH], R_H + 16384)
        f_hi = at("f_hi", [12, T], R_P, F32R)
        f_lo = at("f_lo", [12, T], R_P + 12 * T * 4, F32R)
        gbuf = at("gbuf", [2, T], R_M)
        sbuf_ = at("sbuf_", [2, T], R_M + 4608)
        ubuf = at("ubuf", [2, T], R_M + 9216)
        yT = at("yT", [KD, T], R_P + 18432)
        y_rows = at("y_rows", [5, D], R_W)
        cc = at("cc", [NCONST], R_C)
        ident = cc[:, C_ID:C_ID + P]
        cvec = at("cvec", [NVEC], R_C + 2560)
        ones = at("ones", [P], R_C + 2816)
        cst = at("cst", [8], R_C + 3328)
        bias_p = at("bias_p", [2, HEADS], R_C + 3360)
        bias_s = at("bias_s", [2], R_C + 3424)
        bias_col = at("bias_col", [1], R_C + 3456)
        bias_dg = at("bias_dg", [HEADS], R_C + 3488)
        stT = at("stT", [KC, 2 * BS], R_C + 3520)
        sm = at("sm", [40], R_C + 3776)
        bias_fix = at("bias_fix", [2, 2], R_C + 4000)
        token = at("token", [64], region(256))

        ps = ctx.enter_context(nc.psum_tensor("ps", [P, 8, 512], F32))

        def halves(ap):
            return ap.rearrange("p (a b) -> p a b", a=2)

        def tiled(ap, f=P):
            return ap.rearrange("p (a f) -> p a f", f=f)

        def kview(w):
            return w[0].rearrange("(k p) n -> p k n", p=P)

        views = {"in": kview(w_in), "ck": kview(w_ck), "cv": kview(w_cv), "out": kview(w_out),
                 "cq": kview(w_cq), "co": kview(w_co), "gate": kview(w_gate), "up": kview(w_up),
                 "down": kview(w_down)}
        STAGES = [("in", 8, 6), ("ck", 8, 1), ("cv", 8, 1), ("out", 8, 2), ("cq", 8, 1), ("co", 4, 2),
                  ("gu0", 8, 6), ("down0", 6, 4), ("gu1", 8, 5), ("down1", 5, 4)]
        FF0 = (0, 12)
        NAMES = [name for name, _, _ in STAGES]
        KN = {name: kn for name, kn, _ in STAGES}
        PAIRS = {name: pairs for name, _, pairs in STAGES}
        SLOT0 = {name: sum(2 * p for _, _, p in STAGES[:i]) for i, name in enumerate(NAMES)}

        s_const, s_x, s_m, s_pt = sem("consts_loaded"), sem("x_loaded"), sem("mem_loaded"), sem("ptab_loaded")
        s_set = sem("ones_and_token_set")
        s_tr, s_ev = sem("unit_transposed"), sem("unit_copied")
        s_bmm, s_bc = sem("bias_product"), sem("bias_copied")
        s_full = [sem("weights_loaded0"), sem("weights_loaded1")]
        s_whi, s_wlo = sem("weights_hi"), sem("weights_lo")
        s_tile = {n: sem(f"tile_{n}") for n in NAMES}
        s_free = {n: sem(f"banks_{n}") for n in NAMES}
        s_op = {n: sem(f"operand_{n}") for n in ("in", "ck", "out", "cq", "co", "gu0")}
        NORMS = ["in", "ck", "att", "conv", "cq", "gu0", "fin"]
        s_sq = {n: sem(f"squares_{n}") for n in NORMS}
        s_sum = {n: sem(f"sums_{n}") for n in NORMS}
        s_ms = {n: sem(f"meansq_{n}") for n in NORMS}
        s_rt = {n: sem(f"root_{n}") for n in NORMS}
        s_evac = {n: sem(f"evacuated_{n}") for n in NAMES}
        s_dve = sem("vector_step")
        s_out = sem("outputs_stored")
        s_conv, s_cs = sem("conv_done"), sem("conv_rows_staged")
        s_sig = sem("sigmoid_done")
        s_y = sem("y_scaled")
        p_ = {n: sem(f"prompt_{n}") for n in ("qk_fixed", "bias_fixed", "v_fixed", "score", "beta", "om", "scan", "weight", "tr",
                                              "copied_a", "copied_d", "out", "out_copied")}
        m_ = {n: sem(f"sample_{n}") for n in ("queries", "k_copied_a", "k_copied_d", "score", "beta",
                                              "om", "run", "weight", "tr", "tr_copied", "pv", 
                                              "rows", "rows_tr", "rows_copied")}
        s_kp = [sem("k_pages0"), sem("k_pages1")]
        s_vp = [sem("v_pages0"), sem("v_pages1")]
        s_ktr = sem("k_page_transposed")
        c_ = {n: sem(f"cross_{n}") for n in ("score", "max", "exp", "prob", "tr", "tr_copied", "out", "out_copied",
                                             "queries")}
        s_cmk, s_cmv = sem("mem_k_loaded"), sem("mem_v_loaded")

        steps, grants = [0], [0]

        def step(dve, ins):
            steps[0] += 1
            ins.then_inc(s_dve, 1)
            dve.wait_ge(s_dve, steps[0])

        def grant(semaphore, n):
            grants[0] += 1
            nc.vector.memset(token[0:1, grants[0]:grants[0] + 1], 0.0).then_inc(semaphore, n)

        units = []

        def batch(pairs_):
            a = len(units)
            units.extend(pairs_)
            return range(a, len(units))

        def rows_of(m):
            return P if m < NB else NS

        def to_tokens(src, k0, m, dst):
            r = rows_of(m)
            return [src[:, k0 + j, m * P:m * P + r] for j in range(4)], tiled(dst[0:r, :])

        U_VEC = batch([([vec_rows[0:NVEC, :]], cvec[:, :].rearrange("p (a f) -> p a f", a=1)),
                       ([st_rows[0:2 * BS, j * P:(j + 1) * P] for j in range(4)], stT[:, :, :])])
        U_X = batch([([x_tok[0:rows_of(m), m, (4 * kh + j) * P:(4 * kh + j + 1) * P] for j in range(4)],
                      xT[:, 4 * kh:4 * kh + 4, m * P:m * P + rows_of(m)]) for m in range(5) for kh in range(2)])
        U_M = batch([([m_tok[:, m, (4 * kh + j) * P:(4 * kh + j + 1) * P] for j in range(4)],
                      mT[:, 4 * kh:4 * kh + 4, m * P:(m + 1) * P]) for m in range(MT) for kh in range(2)])
        U_VT = batch([to_tokens(pT, T_A, m, v_tok[:, m, :]) for m in range(5)])
        U_KT = batch([to_tokens(pT, T_K, m, k_rows[:, m, :]) for m in range(5)])
        U_MK = batch([([src[:, j, m * P:(m + 1) * P] for j in range(4)], tiled(dst[:, m, :]))
                      for src, dst in ((mkT, mk_rows), (mvT, mv_tok)) for m in range(MT)])
        U_CS = batch([([cs[:, j, :] for j in range(4)], tiled(cs_rows[0:18, :]))])
        U_SMK = [batch([([smk_tok[:, b, m, j * P:(j + 1) * P] for j in range(4)], smkT[:, b, :, m * P:(m + 1) * P])
                        for b in range(4) for m in range(MT)]) for _ in range(2)]
        U_Y = batch([to_tokens(yT, 4 * kh, m, y_rows[:, m, kh * 512:(kh + 1) * 512])
                     for m in range(5) for kh in range(2)])

        def tr_pe(pe, us):
            for u in us:
                srcs, _ = units[u]
                if u >= 2:
                    pe.wait_ge(s_ev, u - 1)
                for j, src in enumerate(srcs):
                    p_in, f = src.shape[0], src.shape[-1]
                    op = nc.tensor.transpose(ps[0:f, 4 + u % 2, j * P:j * P + p_in], src, ident[0:p_in, 0:p_in])
                op.then_inc(s_tr, 1)

        def tr_act(act, us):
            for u in us:
                srcs, dst = units[u]
                p_in, f = srcs[0].shape[0], srcs[0].shape[-1]
                act.wait_ge(s_tr, u + 1)
                bank = tiled(ps[0:f, 4 + u % 2, 0:len(srcs) * P])[:, :, 0:p_in]
                nc.scalar.activation(dst, bank, ACT.Copy).then_inc(s_ev, 1)

        def rms_sum(dve, name, buf, kt):
            dve.wait_ge(s_sq[name], 1)
            while kt > 2:
                kt //= 2
                step(dve, nc.vector.tensor_tensor(buf[:, 0:kt, :], buf[:, 0:kt, :], buf[:, kt:2 * kt, :], ALU.add))
            nc.vector.tensor_tensor(buf[:, 0, :], buf[:, 0, :], buf[:, 1, :], ALU.add).then_inc(s_sum[name], 1)

        def rms_pe(pe, name, buf, n, after=None):
            if after:
                pe.wait_ge(s_rt[after], 1)
            pe.wait_ge(s_sum[name], 1)
            w = n // 2
            for hf in range(2):
                op = nc.tensor.matmul(ps[:, 6 + hf, 0:w], ones[:, :], buf[:, 0, hf * w:(hf + 1) * w],
                                      start=True, stop=True)
            op.then_inc(s_ms[name], 1)

        def rms_root(act, name, dst, n, feats):
            act.wait_ge(s_ms[name], 1)
            nc.scalar.activation(halves(dst), ps[:, 6:8, 0:n // 2], ACT.Sqrt,
                                 bias=cst[:, 0:1], scale=1.0 / feats).then_inc(s_rt[name], 1)

        def rms_inv(dve, name, buf):
            dve.wait_ge(s_rt[name], 1)
            step(dve, nc.vector.reciprocal(buf, buf))

        def scale_split(dve, src, g0, hi, lo, kt, ready):
            for k in range(kt):
                g = cvec[:, g0 + k:g0 + k + 1]
                step(dve, nc.vector.tensor_scalar(hi[:, k, :], src[:, k, :], g, None, ALU.mult))
                op = nc.vector.scalar_tensor_tensor(out=lo[:, k, :], in0=src[:, k, :], scalar=g,
                                                    in1=hi[:, k, :].bitcast(F32), op0=ALU.mult, op1=ALU.subtract)
            op.then_inc(ready, 1)

        def load_stage(sp, name, grants=()):
            n0, kn = SLOT0[name], KN[name]

            def body(i, first):
                for s in range(2):
                    if not first:
                        sp.wait_ge(s_wlo, i * 2 + (n0 + s - 1))
                    if name[:2] == "gu":
                        src = views["gate" if s == 0 else "up"][:, :, bass.ds(i * SLOTW + FF0[int(name[2])] * P, SLOTW)]
                    elif name[:4] == "down":
                        k0 = FF0[int(name[4])] + s * kn
                        src = views["down"][:, k0:k0 + kn, bass.ds(i * SLOTW, SLOTW)]
                    else:
                        src = views[name][:, :, bass.ds(i * (2 * SLOTW) + s * SLOTW, SLOTW)]
                    sp.dma_start(w_raw[s][:, 0:kn, :], src).then_inc(s_full[s], 16)
            if n0 == 0:
                body(0, True)
                with sp.Fori(1, PAIRS[name]) as i:
                    body(i, False)
            else:
                with sp.Fori(0, PAIRS[name]) as i:
                    body(i, False)

        def split_hi(act, name, i, s):
            act.wait_ge(s_full[s], i * 16 + (SLOT0[name] * 8 + 16))
            nc.scalar.activation(w_hi[s][:, 0:KN[name], :], w_raw[s][:, 0:KN[name], :], ACT.Copy).then_inc(s_whi, 1)

        def split_stage(act, name, more=None):
            prev = NAMES[NAMES.index(name) - 1] if name != "in" else None
            for s in range(2):
                if prev:
                    act.wait_ge(s_tile[prev], 4 * PAIRS[prev] - 2 + 2 * s)
                split_hi(act, name, 0, s)
            if more:
                more(0)
            if PAIRS[name] > 1:
                with act.Fori(1, PAIRS[name]) as i:
                    for s in range(2):
                        act.wait_ge(s_tile[name], i * 4 + (2 * s - 2))
                        split_hi(act, name, i, s)
                    if more:
                        more(i)

        def lo_stage(pool, name):
            with pool.Fori(0, PAIRS[name]) as i:
                for s in range(2):
                    pool.wait_ge(s_whi, i * 2 + (SLOT0[name] + s + 1))
                    nc.gpsimd.tensor_tensor(w_lo[s][:, 0:KN[name], :], w_raw[s][:, 0:KN[name], :],
                                            w_hi[s][:, 0:KN[name], :].bitcast(F32), ALU.subtract).then_inc(s_wlo, 1)

        def gemm(pe, name, hi, lo, n=T):
            kn, down = KN[name], name[:4] == "down"
            parts = [(a, min(a + HALF, n)) for a in range(0, n, HALF)]
            with pe.Fori(0, PAIRS[name]) as i:
                for s in range(2):
                    pe.wait_ge(s_wlo, i * 2 + (SLOT0[name] + s + 1))
                    for t in range(2):
                        if not down:
                            pe.wait_ge(s_free[name], i * 4 + (2 * s + t + 1))
                        elif s == 0:
                            pe.wait_ge(s_free[name], i * 2 + (t + 1))
                        begin, end, k0 = not down or s == 0, not down or s == 1, s * kn if down else 0
                        for k in range(kn):
                            for w, (weights, x) in enumerate(((w_hi, hi), (w_hi, lo), (w_lo, hi))):
                                for hf, (a, b) in enumerate(parts):
                                    op = nc.tensor.matmul(ps[:, 2 * t + hf, 0:b - a],
                                                          weights[s][:, k, t * P:(t + 1) * P], x[:, k0 + k, a:b],
                                                          start=begin and k == 0 and w == 0,
                                                          stop=end and k == kn - 1 and w == 2)
                        op.then_inc(s_tile[name], 1)

        def load_pages(eng, g, c, cache, buf, loaded, used, uses):
            for par in range(2):
                for s in range(2):
                    for j in range(4):
                        page = eng.value_load(ptb[0:1, bass.ds(g * 64 + (32 * s + 28 - 8 * c - 4 * par + j), 1)],
                                              min_val=0, max_val=N_POOL - 1)
                        if s == 0 and j == 0:
                            eng.wait_ge(used, g * (8 * uses) + (2 * c + par + 1) * uses)
                            eng.wait_ge(s_pt, 16)
                        eng.dma_start(buf[par][:, 4 * s + j:4 * s + j + 1, :],
                                      cache[0, bass.ds(page, 1)].rearrange("o p h d -> p o (h d)"))\
                            .then_inc(loaded[par], 16)

        def pair(t):
            return ps[:, 2 * t:2 * t + 2, 0:HALF]

        def tile_of(dst, i):
            return dst[:, bass.ds(i, 1), :].rearrange("p o (a b) -> p (o a) b", a=2)

        def evac_scaled(dve, name, dst, scale):
            with dve.Fori(0, PAIRS[name]) as i:
                for j in range(4):
                    dve.wait_ge(s_tile[name], i * 4 + (j + 1))
                    nc.vector.tensor_tensor(tile_of(dst, i * 4 + j), pair(j % 2), halves(scale), ALU.mult)\
                        .then_inc(s_free[name], 1)

        def evac_mem(dve, name, dst):
            for j in range(4):
                dve.wait_ge(s_tile[name], j + 1)
                nc.vector.tensor_tensor(dst[:, j, :], ps[:, 2 * (j % 2), 0:NMEM], rstd_m[:, :], ALU.mult)\
                    .then_inc(s_free[name], 1)

        def evac_residual(dve, name):
            down = name[:4] == "down"
            with dve.Fori(0, PAIRS[name]) as i:
                for j in range(2 if down else 4):
                    dve.wait_ge(s_tile[name], i * 4 + (j + 3 if down else j + 1))
                    x = tile_of(xT, i * (2 if down else 4) + j)
                    nc.vector.tensor_tensor(x, pair(j % 2), x, ALU.add).then_inc(s_free[name], 1)


        def cross_act(act):
            nc.scalar.preload_act_table(ACT.Exp)
            for u in range(CAH + 2):
                if u >= CAH:
                    tr_act(act, U_SMK[u - CAH])
                act.wait_ge(c_["max"], u + 1)
                for j in range(4 if u < CAH else 1):
                    z = ps[:, j // 2, (j % 2) * NMEM:(j % 2 + 1) * NMEM]
                    op = nc.scalar.activation(prob[:, j, :], z, ACT.Exp, scale=CA_SCALE,
                                              bias=sm[:, 4 + j:5 + j], accum_out=sm[:, 8 + j:9 + j])
                op.then_inc(c_["exp"], 1)
                act.wait_ge(c_["tr"], u + 1)
                w = SEQ if u < CAH else P
                nc.scalar.activation(probT[:, :, 0:w], ps[:, 2:4, 0:w], ACT.Copy).then_inc(c_["tr_copied"], 1)
                act.wait_ge(c_["out"], u + 1)
                if u < CAH:
                    dst, src = caoT[:, u, 0:SEQ], ps[:, 6, :]
                else:
                    dst = caoT[:, :, SEQ + 32 * (u - CAH):SEQ + 32 * (u - CAH) + 32]
                    src = tiled(ps[:, 6, 0:P], 32)
                nc.scalar.activation(dst, src, ACT.Copy).then_inc(c_["out_copied"], 1)

        s_h = sem("hidden_step")
        s_hid = sem("hidden_ready")

        def hidden_dve(dve, half):
            name = f"gu{half}"
            h0 = 8 * PAIRS["gu0"] * half
            g0 = 2 * PAIRS["gu0"] * half
            with dve.Fori(0, PAIRS[name]) as i:
                for t in range(2):
                    dve.wait_ge(s_tile[name], i * 4 + (t + 1))
                    nc.vector.tensor_tensor(halves(gbuf[:, t, :]), pair(t), halves(rstd[:, :]), ALU.mult)\
                        .then_inc(s_free[name], 1)
                for t in range(2):
                    dve.wait_ge(s_tile[name], i * 4 + (t + 3))
                    nc.vector.tensor_tensor(halves(ubuf[:, t, :]), pair(t), halves(rstd[:, :]), ALU.mult)\
                        .then_inc(s_free[name], 1)
                    dve.wait_ge(s_sig, i * 2 + (g0 + t + 1))
                    nc.vector.tensor_tensor(gbuf[:, t, :], gbuf[:, t, :], sbuf_[:, t, :], ALU.mult).then_inc(s_h, 1)
                    dve.wait_ge(s_h, i * 8 + (h0 + 4 * t + 1))
                    nc.vector.tensor_tensor(ubuf[:, t, :], ubuf[:, t, :], gbuf[:, t, :], ALU.mult).then_inc(s_h, 1)
                    dve.wait_ge(s_h, i * 8 + (h0 + 4 * t + 2))
                    hi = f_hi[:, bass.ds(i * 2 + t, 1), :].rearrange("p o n -> p (o n)")
                    lo = f_lo[:, bass.ds(i * 2 + t, 1), :].rearrange("p o n -> p (o n)")
                    nc.vector.tensor_copy(hi, ubuf[:, t, :]).then_inc(s_h, 1)
                    dve.wait_ge(s_h, i * 8 + (h0 + 4 * t + 3))
                    nc.vector.tensor_tensor(lo, ubuf[:, t, :], hi.bitcast(F32), ALU.subtract).then_inc(s_h, 1)
            grant(s_hid, 1)

        def cross_dve(dve):
            for u in range(CAH + 2):
                n = 4 if u < CAH else 1
                if u >= CAH:
                    gg = u - CAH
                    if gg == 0:
                        step(dve, nc.vector.memset(qc[:, :, :, :], 0.0))
                    for b in range(4):
                        c0 = SEQ + 32 * gg + 8 * b
                        op = nc.vector.tensor_copy(qc[:, b, :, 8 * b:8 * b + 8], caq[:, :, c0:c0 + 8])
                    op.then_inc(c_["queries"], 1)
                dve.wait_ge(c_["score"], u + 1)
                if n == 4:
                    z = ps[:, 0:2, :].rearrange("p a (b m) -> p a b m", b=2)
                    step(dve, nc.vector.tensor_reduce(sm[:, 0:4].rearrange("p (a b) -> p a b", a=2), z, AX.X, ALU.max))
                else:
                    step(dve, nc.vector.tensor_reduce(sm[:, 0:1], ps[:, 0, 0:NMEM], AX.X, ALU.max))
                nc.vector.tensor_scalar(sm[:, 4:4 + n], sm[:, 0:n], -CA_SCALE, None, ALU.mult).then_inc(c_["max"], 1)
                dve.wait_ge(c_["exp"], u + 1)
                step(dve, nc.vector.reciprocal(sm[:, 12:12 + n], sm[:, 8:8 + n]))
                for j in range(n):
                    op = nc.vector.tensor_scalar(prob[:, j, :], prob[:, j, :], sm[:, 12 + j:13 + j], None, ALU.mult)
                op.then_inc(c_["prob"], 1)

        def cross_pe(pe):
            pe.wait_ge(s_evac["cq"], 1)
            for u in range(CAH + 2):
                if u:
                    pe.wait_ge(c_["tr_copied"], u)
                if u < CAH:
                    for qb in range(NB):
                        op = nc.tensor.matmul(ps[:, qb // 2, (qb % 2) * NMEM:(qb % 2 + 1) * NMEM],
                                              caq[:, u, qb * P:(qb + 1) * P], mkT[:, u, :], start=True, stop=True)
                else:
                    gg = u - CAH
                    pe.wait_ge(s_cmk, 64 * (gg + 1))
                    tr_pe(pe, U_SMK[gg])
                    pe.wait_ge(s_ev, U_SMK[gg][-1] + 1)
                    pe.wait_ge(c_["queries"], gg + 1)
                    for b in range(4):
                        for h in range(CAH):
                            op = nc.tensor.matmul(ps[32 * h:32 * h + 32, 0, 0:NMEM], qc[:, b, h, :], smkT[:, b, h, :],
                                                  start=b == 0, stop=b == 3)
                op.then_inc(c_["score"], 1)
                pe.wait_ge(c_["prob"], u + 1)
                for m in range(MT):
                    for j in range(4 if u < CAH else 1):
                        op = nc.tensor.transpose(ps[:, 2 + m, j * P:(j + 1) * P], prob[:, j, m * P:(m + 1) * P], ident)
                op.then_inc(c_["tr"], 1)
                pe.wait_ge(c_["tr_copied"], u + 1)
                if u:
                    pe.wait_ge(c_["out_copied"], u)
                if u < CAH:
                    for m in range(MT):
                        op = nc.tensor.matmul(ps[:, 6, :], mv_tok[:, m, u * P:(u + 1) * P], probT[:, m, :],
                                              start=m == 0, stop=m == MT - 1)
                else:
                    pe.wait_ge(s_cmv, 64 * (u - CAH + 1))
                    for h in range(CAH):
                        for b in range(4):
                            c0 = 32 * h + 8 * b
                            for m in range(MT):
                                op = nc.tensor.matmul(ps[:, 6, c0:c0 + 8], smv_tok[:, b, m, h * P:(h + 1) * P],
                                                      probT[:, m, c0:c0 + 8], start=m == 0, stop=m == MT - 1)
                op.then_inc(c_["out"], 1)

        block = ctx.enter_context(nc.Block())

        @block.sync
        def _(sp):
            sp.dma_start(cc[:, :], shape_consts).then_inc(s_const, 16)
            for k0, v, n in ((G_MIX, g_mix, 8), (G_MEM, g_mem, 8), (G_CA, g_ca, 8), (G_FFN, g_ffn, 8),
                             (G_ATT, g_att, 4), (G_CONV, g_conv, 4)):
                sp.dma_start(vec_rows[k0:k0 + n, :], v[0].rearrange("(k p) -> k p", p=P)).then_inc(s_const, 16)
            sp.dma_start(vec_rows[G_FIN:G_FIN + 8, :], g_fin.rearrange("(k p) -> k p", p=P)).then_inc(s_const, 16)
            sp.dma_start(vec_rows[W_CONV:NVEC, :], w_conv[0].rearrange("j (k p) -> (j k) p", p=P)).then_inc(s_const, 16)
            sp.dma_start(st_rows[0:2 * BS, :], st_conv[0].rearrange("b k n -> (b k) n")).then_inc(s_const, 16)
            sp.dma_start(bias_col[0:HEADS, :], sb_bias[0].rearrange("(h o) -> h o", o=1)).then_inc(s_const, 16)
            sp.dma_start(x_tok[:, 0:NB, :], x_p[0].rearrange("(m p) n -> p m n", p=P)).then_inc(s_x, 16)
            sp.dma_start(x_tok[0:NS, NB, :], x_s.rearrange("b t n -> (b t) n")).then_inc(s_x, 16)
            sp.dma_start(m_tok[:, :, :], mem[0].rearrange("(m p) n -> p m n", p=P)).then_inc(s_m, 16)
            sp.dma_start(ptb[0:1, :], ptab.rearrange("(o b) n -> o (b n)", o=1)).then_inc(s_pt, 16)
            for name in ("in", "ck", "cv"):
                load_stage(sp, name)
            sp.wait_ge(s_pt, 16)
            with sp.Fori(0, GROUPS) as g:
                for c in range(CP):
                    load_pages(sp, g, c, ck, k_page, s_kp, s_ktr, 8)
            sp.wait_ge(m_["pv"], 8 * GROUPS + 2)
            sp.wait_ge(m_["score"], 9 * GROUPS)
            load_stage(sp, "out")
            for gg in range(2):
                if gg == 0:
                    sp.wait_ge(s_op["out"], 1)
                else:
                    sp.wait_ge(s_tr, U_SMK[0][-1] + 1)
                for b in range(4):
                    sp.dma_start(smk_tok[:, b, :, :],
                                 cmk[0, 4 * gg + b].rearrange("(m p) h d -> p m (h d)", p=P)).then_inc(s_cmk, 16)
                if gg == 0:
                    load_stage(sp, "cq")
                    sp.wait_ge(s_tile["cq"], 4)
                else:
                    sp.wait_ge(c_["out"], 5)
                for b in range(4):
                    sp.dma_start(smv_tok[:, b, :, :],
                                 cmv[0, 4 * gg + b].rearrange("(m p) h d -> p m (h d)", p=P)).then_inc(s_cmv, 16)
            for name in ("co", "gu0", "down0", "gu1", "down1"):
                load_stage(sp, name)
            sp.wait_ge(s_out, 16 * 10)

        @block.gpsimd
        def _(pool):
            for name in ("in", "ck", "cv"):
                lo_stage(pool, name)
            pool.wait_ge(s_pt, 16)
            with pool.Fori(0, GROUPS) as g:
                for c in range(CP):
                    load_pages(pool, g, c, cv, v_page, s_vp, m_["pv"], 1)
            for name in NAMES[3:]:
                lo_stage(pool, name)

        @block.scalar
        def _(act):
            act.wait_ge(s_set, 2)
            tr_act(act, U_VEC)
            act.wait_ge(s_bmm, 1)
            nc.scalar.activation(bias_p[:, 0, :], ps[:, 6, 0:HEADS], ACT.Copy).then_inc(s_bc, 1)
            nc.scalar.activation(bias_p[:, 1, :], ps[:, 6, 0:HEADS], ACT.Copy, scale=-1.0).then_inc(s_bc, 1)
            nc.scalar.activation(bias_s[:, 0:1], ps[:, 7, 0:1], ACT.Copy).then_inc(s_bc, 1)
            nc.scalar.activation(bias_s[:, 1:2], ps[:, 7, 0:1], ACT.Copy, scale=-1.0).then_inc(s_bc, 1)
            tr_act(act, U_X)
            act.wait_ge(s_ev, U_X[-1] + 1)
            nc.scalar.activation(sq[:, :, :], xT[:, :, :], ACT.Square).then_inc(s_sq["in"], 1)
            tr_act(act, U_M)
            act.wait_ge(s_ev, U_M[-1] + 1)
            nc.scalar.activation(m_sq[:, :, :], mT[:, :, :], ACT.Square).then_inc(s_sq["ck"], 1)
            rms_root(act, "in", rstd[:, :], T, D)
            rms_root(act, "ck", rstd_m[:, :], NMEM, D)
            for name in ("in", "ck", "cv"):
                split_stage(act, name)
            tr_act(act, U_VT)
            tr_act(act, U_KT)
            tr_act(act, U_MK)
            act.wait_ge(s_ev, U_MK[-1] + 1)
            for src, dst_p, dst_s in ((v_tok, out_v_p, out_v_s), (k_rows, out_k_p, out_k_s)):
                act.dma_start(dst_p[0, 0].rearrange("(m p) h d -> p m (h d)", p=P), src[:, 0:NB, :]).then_inc(s_out, 16)
                act.dma_start(dst_s[0].rearrange("b t h d -> (b t) (h d)"), src[0:NS, NB, :]).then_inc(s_out, 16)
            for src, dst in ((mk_rows, out_mk), (mv_tok, out_mv)):
                act.dma_start(dst[0, 0].rearrange("(m p) h d -> p m (h d)", p=P), src[:, :, :]).then_inc(s_out, 16)
            nc.scalar.preload_act_table(ACT.Sigmoid)

            def copy_k(g, c):
                for q in range(0, 8, 2):
                    if q == 0:
                        act.wait_ge(m_["score"], g * 9 + (c + 1))
                    act.wait_ge(s_ktr, g * 64 + (8 * c + q + 17))
                    nc.scalar.activation(kT[:, q // 4, :, (q % 4) * P:(q % 4 + 1) * P], tiled(ps[:, q % 3, :]),
                                         ACT.Copy).then_inc(m_["k_copied_a"], 1)

            def sample_sigmoids(S, w):
                act.wait_ge(m_["score"], S + 1)
                act.wait_ge(m_["weight"], S + 1)
                nc.scalar.activation(beta_s[:, 0:w], ps[:, 3, 0:w], ACT.Sigmoid, scale=SB_SCALE,
                                     bias=bias_s[:, 0:1]).then_inc(m_["beta"], 1)
                nc.scalar.activation(om_s[:, 0:w], ps[:, 3, 0:w], ACT.Sigmoid, scale=-SB_SCALE,
                                     bias=bias_s[:, 1:2]).then_inc(m_["om"], 1)

            def copy_weights(S, new):
                act.wait_ge(m_["tr"], S + 2)
                if new:
                    nc.scalar.activation(awT_s[:, 0, :], ps[:, 4, 0:P], ACT.Copy).then_inc(m_["tr_copied"], 1)
                else:
                    nc.scalar.activation(awT_s[:, :, :], tiled(ps[:, 4, :]), ACT.Copy).then_inc(m_["tr_copied"], 1)

            def prompt_sigmoids(g, qb):
                nk = (qb + 1) * P
                act.wait_ge(p_["score"], g * 4 + (qb + 2))
                for h2 in range(2):
                    act.wait_ge(p_["weight"], g * 8 + (2 * qb + h2 + 1))
                    z = ps[:, 5 + 2 * h2, 0:nk]
                    nc.scalar.activation(beta[:, h2, 0:nk], z, ACT.Sigmoid, scale=SB_SCALE,
                                         bias=bias_fix[:, 0, h2:h2 + 1]).then_inc(p_["beta"], 1)
                    nc.scalar.activation(om[:, h2, 0:nk], z, ACT.Sigmoid, scale=-SB_SCALE,
                                         bias=bias_fix[:, 1, h2:h2 + 1]).then_inc(p_["om"], 1)

            def prompt_out(g, qb):
                act.wait_ge(p_["out"], g * 4 + (qb + 2))
                act.wait_ge(s_bc, 4)
                nc.scalar.activation(pT[:, bass.ds(g + T_A, 1), qb * P:(qb + 1) * P].rearrange("p o n -> p (o n)"),
                                     ps[:, 4, 0:P], ACT.Copy).then_inc(p_["out_copied"], 1)

            with act.Fori(0, GROUPS) as g:
                act.wait_ge(p_["score"], g * 4 + 1)
                act.wait_ge(s_bc, 4)
                nc.scalar.activation(q_fix[:, :], pT[:, bass.ds(g + T_Q, 1), 0:SEQ].rearrange("p o n -> p (o n)"),
                                     ACT.Copy).then_inc(p_["qk_fixed"], 1)
                nc.scalar.activation(k_fix[:, :], pT[:, bass.ds(g + T_K, 1), 0:SEQ].rearrange("p o n -> p (o n)"),
                                     ACT.Copy).then_inc(p_["qk_fixed"], 1)
                nc.scalar.activation(bias_fix[:, :, :], bias_p[:, :, bass.ds(g * 2, 2)], ACT.Copy)\
                    .then_inc(p_["bias_fixed"], 1)
                act.wait_ge(p_["bias_fixed"], g + 1)
                sample_sigmoids(g * 9, NS)
                copy_k(g, 0)
                copy_weights(g * 9, True)
                for c in range(8):
                    sample_sigmoids(g * 9 + (c + 1), SEQ)
                    if c % 2 == 0 and c:
                        prompt_out(g, c // 2 - 1)
                    if c < 7:
                        copy_k(g, c + 1)
                    copy_weights(g * 9 + (c + 1), False)
                    if c % 2 == 0:
                        prompt_sigmoids(g, c // 2)
                    else:
                        act.wait_ge(p_["tr"], g * 4 + (c // 2 + 2))
                        nc.scalar.activation(awT[:, 0, 0:c // 2 + 1, :], tiled(ps[:, 5, 0:(c // 2 + 1) * P]), ACT.Copy)\
                            .then_inc(p_["copied_a"], 1)
                prompt_out(g, 3)

            act.wait_ge(s_cs, 1)
            tr_act(act, U_CS)
            act.wait_ge(s_ev, U_CS[-1] + 1)
            act.dma_start(out_c_p[0, 0], cs_rows[0:2, :]).then_inc(s_out, 16)
            act.dma_start(out_c_s[0].rearrange("b k n -> (b k) n"), cs_rows[2:18, :]).then_inc(s_out, 16)
            act.wait_ge(m_["rows_copied"], GROUPS + 1)
            act.wait_ge(p_["out_copied"], 4 * GROUPS + 1)
            nc.scalar.activation(sq_c[:, :, :], pT[:, T_C:T_C + KC, :], ACT.Square).then_inc(s_sq["conv"], 1)
            nc.scalar.activation(sq_a[:, :, :], pT[:, T_A:T_A + KC, :], ACT.Square).then_inc(s_sq["att"], 1)
            rms_root(act, "conv", rstd[:, :], T, CH)
            act.wait_ge(s_evac["in"], 2)
            rms_root(act, "att", rstd[:, :], T, CH)
            split_stage(act, "out")
            act.wait_ge(s_evac["out"], 1)
            nc.scalar.activation(sq_ca[:, :, :], xT[:, :, :], ACT.Square).then_inc(s_sq["cq"], 1)
            rms_root(act, "cq", rstd[:, :], T, D)
            split_stage(act, "cq")
            cross_act(act)
            split_stage(act, "co")
            act.wait_ge(s_evac["co"], 1)
            nc.scalar.activation(sq_ca[:, :, :], xT[:, :, :], ACT.Square).then_inc(s_sq["gu0"], 1)
            rms_root(act, "gu0", rstd[:, :], T, D)

            def sigmoid_of(name):
                def more(i):
                    for t in range(2):
                        act.wait_ge(s_free[name], i * 4 + (t + 3))
                        nc.scalar.activation(sbuf_[:, t, :], gbuf[:, t, :], ACT.Sigmoid).then_inc(s_sig, 1)
                return more
            nc.scalar.preload_act_table(ACT.Sigmoid)
            split_stage(act, "gu0", sigmoid_of("gu0"))
            split_stage(act, "down0")
            split_stage(act, "gu1", sigmoid_of("gu1"))
            split_stage(act, "down1")
            act.wait_ge(s_evac["down1"], 1)
            nc.scalar.activation(sq[:, :, :], xT[:, :, :], ACT.Square).then_inc(s_sq["fin"], 1)
            rms_root(act, "fin", rstd[:, :], T, D)
            tr_act(act, U_Y)
            act.wait_ge(s_ev, U_Y[-1] + 1)
            act.dma_start(y_p[0].rearrange("(m p) n -> p m n", p=P), y_rows[:, 0:NB, :]).then_inc(s_out, 16)
            act.dma_start(y_s.rearrange("b t n -> (b t) n"), y_rows[0:NS, NB, :]).then_inc(s_out, 16)

        @block.vector
        def _(dve):
            nc.vector.memset(ones[:, :], 1.0).then_inc(s_set, 1)
            nc.vector.memset(cst[:, :], EPS).then_inc(s_set, 1)
            grant(s_free["in"], 2)
            dve.wait_ge(s_const, 16 * 11)
            nc.vector.tensor_scalar(bias_dg[0:HEADS, :], ident[0:HEADS, 0:HEADS], bias_col[0:HEADS, 0:1], None,
                                    ALU.mult).then_inc(s_set, 1)
            dve.wait_ge(s_ev, U_X[-1] + 1)
            scale_split(dve, xT, G_MIX, h_hi, h_lo, KD, s_op["in"])
            rms_sum(dve, "in", sq, KD)
            dve.wait_ge(s_ev, U_M[-1] + 1)
            scale_split(dve, mT, G_MEM, m_hi, m_lo, KD, s_op["ck"])
            rms_sum(dve, "ck", m_sq, KD)
            rms_inv(dve, "in", rstd[:, :])
            rms_inv(dve, "ck", rstd_m[:, :])
            evac_scaled(dve, "in", pT, rstd[:, :])
            grant(s_evac["in"], 1)
            grant(s_free["ck"], 2)
            evac_mem(dve, "ck", mkT)
            grant(s_free["cv"], 2)
            evac_mem(dve, "cv", mvT)
            grant(s_evac["cv"], 1)

            dve.wait_ge(s_dve, steps[0])
            step(dve, nc.vector.tensor_tensor(pT[:, T_U:T_U + KC, :], pT[:, T_C:T_C + KC, :], pT[:, T_U:T_U + KC, :],
                                              ALU.mult))
            for k in range(KC):
                w = [cvec[:, W_CONV + 4 * j + k:W_CONV + 4 * j + k + 1] for j in range(3)]
                u, y = pT[:, T_U + k, :], pT[:, T_C + k, :]
                us, ys = (a[:, SEQ:T].rearrange("p (b t) -> p b t", t=TS) for a in (u, y))
                st = stT[:, k, :].rearrange("p (b j) -> p b j", j=2)

                def add(dst, src, wj):
                    step(dve, nc.vector.scalar_tensor_tensor(out=dst, in0=src, scalar=wj, in1=dst,
                                                             op0=ALU.mult, op1=ALU.add))
                step(dve, nc.vector.tensor_scalar(y, u, w[2], None, ALU.mult))
                add(y[:, 1:SEQ], u[:, 0:SEQ - 1], w[1])
                add(y[:, 2:SEQ], u[:, 0:SEQ - 2], w[0])
                add(ys[:, :, 1:TS], us[:, :, 0:TS - 1], w[1])
                add(ys[:, :, 0:1], st[:, :, 1:2], w[1])
                add(ys[:, :, 2:TS], us[:, :, 0:TS - 2], w[0])
                add(ys[:, :, 0:2], st[:, :, 0:2], w[0])
                nc.vector.tensor_copy(cs[:, k, 0:2], u[:, SEQ - 2:SEQ])
                nc.vector.tensor_copy(cs[:, k, 2:18].rearrange("p (b j) -> p b j", j=2), us[:, :, TS - 2:TS])
            step(dve, nc.vector.tensor_tensor(pT[:, T_C:T_C + KC, :], pT[:, T_C:T_C + KC, :], pT[:, T_B:T_B + KC, :],
                                              ALU.mult))
            grant(s_cs, 1)

            dve.wait_ge(s_tile["cv"], 4)
            nc.vector.memset(run[:, :, :], 1.0)
            nc.vector.memset(zeros[:, :], 0.0)
            nc.vector.memset(aw_s[:, :], 0.0)
            step(dve, nc.vector.memset(q_bd[:, :, :, :], 0.0))
            dve.wait_ge(s_ev, U_MK[-1] + 1)
            nc.vector.memset(v_tok[NS:P, NB, :], 0.0)
            for name, n in (("score", 1), ("weight", 2), ("tr", 1), ("out", 1), ("out_copied", 1)):
                grant(p_[name], n)
            dve.wait_ge(s_out, 16 * 6)
            grant(s_ktr, 16)
            for name, n in (("k_copied_a", 4), ("k_copied_d", 4), ("weight", 1),
                            ("tr", 1), ("tr_copied", 1), ("pv", 2), ("rows", 1), ("rows_copied", 1)):
                grant(m_[name], n)

            def copy_k(g, c):
                for q in range(1, 8, 2):
                    if q == 1:
                        dve.wait_ge(m_["score"], g * 9 + (c + 1))
                    dve.wait_ge(s_ktr, g * 64 + (8 * c + q + 17))
                    nc.vector.tensor_copy(kT[:, q // 4, :, (q % 4) * P:(q % 4 + 1) * P], tiled(ps[:, q % 3, :]))\
                        .then_inc(m_["k_copied_d"], 1)

            def weights(S, R, w):
                dve.wait_ge(m_["om"], S + 1)
                if w == NS:
                    nc.vector.memset(run_s[:, w:w + 1], 1.0).then_inc(m_["run"], 1)
                    dve.wait_ge(m_["run"], R + 1)
                    R = R + 1
                nc.vector.tensor_tensor_scan(run_s[:, 0:w][:, ::-1], om_s[:, 0:w][:, ::-1], om_s[:, 0:w][:, ::-1],
                                             run_s[:, w:w + 1], ALU.mult, ALU.bypass).then_inc(m_["run"], 1)
                dve.wait_ge(m_["run"], R + 1)
                dve.wait_ge(m_["tr"], S + 1)
                nc.vector.tensor_tensor(aw_s[:, 0:w], beta_s[:, 0:w], run_s[:, 1:w + 1], ALU.mult)\
                    .then_inc(m_["weight"], 1)
                dve.wait_ge(m_["weight"], S + 2)
                nc.vector.tensor_copy(run_s[:, SEQ:SEQ + 1], run_s[:, 0:1]).then_inc(m_["run"], 1)
                dve.wait_ge(m_["run"], R + 2)

            def prompt_weights(g, qb):
                nk = (qb + 1) * P
                for h2 in range(2):
                    dve.wait_ge(p_["om"], g * 8 + (2 * qb + h2 + 1))
                    nc.vector.tensor_tensor_scan(run[:, h2, 0:nk][:, ::-1], om[:, h2, 0:nk][:, ::-1],
                                                 om[:, h2, 0:nk][:, ::-1], 1.0, ALU.mult, ALU.bypass)\
                        .then_inc(p_["scan"], 1)
                    dve.wait_ge(p_["scan"], g * 8 + (2 * qb + h2 + 1))
                    if h2 == 0:
                        dve.wait_ge(p_["tr"], g * 4 + (qb + 1))
                    nc.vector.tensor_tensor(aw[:, h2, 0:nk], beta[:, h2, 0:nk], run[:, h2, 1:nk + 1], ALU.mult)\
                        .then_inc(p_["weight"], 1)

            with dve.Fori(0, GROUPS) as g:
                dve.wait_ge(m_["rows_copied"], g + 1)
                for s in range(2):
                    for h2 in range(2):
                        op = nc.vector.tensor_copy(
                            q_bd[64 * h2:64 * h2 + 64, s, :, 16 * s + 8 * h2:16 * s + 8 * h2 + 8],
                            pT[64 * h2:64 * h2 + 64, T_Q:T_Q + HP, bass.ds(g * 16 + (SEQ + 8 * s), 8)])
                op.then_inc(m_["queries"], 1)
                dve.wait_ge(p_["out"], g * 4 + 1)
                nc.vector.tensor_copy(v_fix[:, :, :], v_tok[:, 0:NB, bass.ds(g * P, P)]).then_inc(p_["v_fixed"], 1)
                weights(g * 9, g * 19, NS)
                copy_k(g, 0)
                for c in range(8):
                    weights(g * 9 + (c + 1), g * 19 + (3 + 2 * c), SEQ)
                    if c < 7:
                        copy_k(g, c + 1)
                    if c % 2 == 0:
                        prompt_weights(g, c // 2)
                    else:
                        dve.wait_ge(p_["tr"], g * 4 + (c // 2 + 2))
                        nc.vector.tensor_copy(awT[:, 1, 0:c // 2 + 1, :], tiled(ps[:, 7, 0:(c // 2 + 1) * P]))\
                            .then_inc(p_["copied_d"], 1)
                dve.wait_ge(m_["pv"], g * 8 + 10)
                nc.vector.tensor_copy(o_pair[:, :, :], tiled(ps[:, 6, 0:2 * P])).then_inc(m_["rows"], 1)
                dve.wait_ge(m_["rows_tr"], g + 1)
                for s in range(2):
                    for h2 in range(2):
                        rows = tiled(ps[64 * h2:64 * h2 + 64, 3, s * P:(s + 1) * P], 32)
                        op = nc.vector.tensor_copy(
                            pT[64 * h2:64 * h2 + 64, T_A:T_A + HP, bass.ds(g * 16 + (SEQ + 8 * s), 8)],
                            rows[:, :, 16 * s + 8 * h2:16 * s + 8 * h2 + 8])
                op.then_inc(m_["rows_copied"], 1)

            grant(s_free["out"], 2)
            rms_sum(dve, "conv", sq_c, KC)
            rms_sum(dve, "att", sq_a, KC)
            for name, t0, g0, k0 in (("conv", T_C, G_CONV, 4), ("att", T_A, G_ATT, 0)):
                rms_inv(dve, name, rstd[:, :])
                for k in range(KC):
                    step(dve, nc.vector.scalar_tensor_tensor(out=nrm[:, :], in0=pT[:, t0 + k, :],
                                                             scalar=cvec[:, g0 + k:g0 + k + 1], in1=rstd[:, :],
                                                             op0=ALU.mult, op1=ALU.mult))
                    step(dve, nc.vector.tensor_copy(h_hi[:, k0 + k, :], nrm[:, :]))
                    step(dve, nc.vector.tensor_tensor(h_lo[:, k0 + k, :], nrm[:, :], h_hi[:, k0 + k, :].bitcast(F32),
                                                      ALU.subtract))
                grant(s_evac["in"], 1)
            grant(s_op["out"], 1)
            evac_residual(dve, "out")
            grant(s_evac["out"], 1)
            grant(s_free["cq"], 2)
            dve.wait_ge(s_evac["out"], 1)
            scale_split(dve, xT, G_CA, h_hi, h_lo, KD, s_op["cq"])
            rms_sum(dve, "cq", sq_ca, KD)
            rms_inv(dve, "cq", rstd[:, :])
            evac_scaled(dve, "cq", caq, rstd[:, :])
            grant(s_evac["cq"], 1)
            dve.wait_ge(s_evac["cq"], 1)
            cross_dve(dve)
            grant(s_free["co"], 2)
            dve.wait_ge(c_["out_copied"], CAH + 2)
            for k in range(CAH):
                step(dve, nc.vector.tensor_copy(h_hi[:, k, :], caoT[:, k, :]))
                op = nc.vector.tensor_tensor(h_lo[:, k, :], caoT[:, k, :], h_hi[:, k, :].bitcast(F32), ALU.subtract)
            op.then_inc(s_op["co"], 1)
            evac_residual(dve, "co")
            grant(s_evac["co"], 1)
            grant(s_free["gu0"], 2)
            dve.wait_ge(s_evac["co"], 1)
            scale_split(dve, xT, G_FFN, h_hi, h_lo, KD, s_op["gu0"])
            rms_sum(dve, "gu0", sq_ca, KD)
            rms_inv(dve, "gu0", rstd[:, :])
            for half in range(2):
                hidden_dve(dve, half)
                name = f"down{half}"
                grant(s_free[name], 2)
                evac_residual(dve, name)
                if half == 0:
                    grant(s_free["gu1"], 2)
            grant(s_evac["down1"], 1)
            rms_sum(dve, "fin", sq, KD)
            rms_inv(dve, "fin", rstd[:, :])
            for k in range(KD):
                op = nc.vector.scalar_tensor_tensor(out=yT[:, k, :], in0=xT[:, k, :],
                                                    scalar=cvec[:, G_FIN + k:G_FIN + k + 1], in1=rstd[:, :],
                                                    op0=ALU.mult, op1=ALU.mult)
            op.then_inc(s_y, 1)

        @block.tensor
        def _(pe):
            pe.wait_ge(s_const, 16 * 11)
            tr_pe(pe, U_VEC)
            pe.wait_ge(s_set, 3)
            nc.tensor.matmul(ps[:, 6, 0:HEADS], ones[0:HEADS, :], bias_dg[0:HEADS, :], start=True, stop=True)
            nc.tensor.matmul(ps[:, 7, 0:1], cc[0:HEADS, C_SEL:C_SEL + P], bias_col[0:HEADS, :],
                             start=True, stop=True).then_inc(s_bmm, 1)
            pe.wait_ge(s_x, 32)
            tr_pe(pe, U_X)
            pe.wait_ge(s_m, 16)
            tr_pe(pe, U_M)
            pe.wait_ge(s_bc, 4)
            rms_pe(pe, "in", sq, T)
            rms_pe(pe, "ck", m_sq, NMEM, "in")
            pe.wait_ge(s_op["in"], 1)
            gemm(pe, "in", h_hi, h_lo)
            pe.wait_ge(s_op["ck"], 1)
            gemm(pe, "ck", m_hi, m_lo, NMEM)
            gemm(pe, "cv", m_hi, m_lo, NMEM)
            tr_pe(pe, U_VT)
            tr_pe(pe, U_KT)
            pe.wait_ge(s_evac["cv"], 1)
            tr_pe(pe, U_MK)

            def prompt_scores(g, qb):
                if qb == 0:
                    pe.wait_ge(p_["qk_fixed"], g * 2 + 2)
                for h2 in range(2):
                    r = slice(64 * h2, 64 * h2 + 64)
                    nc.tensor.matmul(ps[:, 5 + 2 * h2, 0:(qb + 1) * P], q_fix[r, qb * P:(qb + 1) * P],
                                     k_fix[r, 0:(qb + 1) * P], start=True, stop=False)
                for h2 in range(2):
                    op = nc.tensor.matmul(ps[:, 5 + 2 * h2, qb * P:(qb + 1) * P], ident, cc[:, C_CMASK:C_CMASK + P],
                                          start=False, stop=True)
                op.then_inc(p_["score"], 1)

            def prompt_transposes(g, qb):
                pe.wait_ge(p_["weight"], g * 8 + (2 * qb + 4))
                for h2 in range(2):
                    for kb in range(qb + 1):
                        op = nc.tensor.transpose(ps[:, 5 + 2 * h2, kb * P:(kb + 1) * P], aw[:, h2, kb * P:(kb + 1) * P],
                                                 ident)
                op.then_inc(p_["tr"], 1)

            def prompt_sums(g, qb):
                if qb == 0:
                    pe.wait_ge(p_["v_fixed"], g + 1)
                pe.wait_ge(p_["copied_a"], g * 4 + (qb + 1))
                pe.wait_ge(p_["copied_d"], g * 4 + (qb + 1))
                for h2 in range(2):
                    for kb in range(qb + 1):
                        op = nc.tensor.matmul(ps[64 * h2:64 * h2 + 64, 4, 0:P], v_fix[:, kb, 64 * h2:64 * h2 + 64],
                                              awT[:, h2, kb, :], start=kb == 0, stop=kb == qb)
                op.then_inc(p_["out"], 1)

            def k_transposes(g, c):
                for q in range(8):
                    if q == 0:
                        pe.wait_ge(s_kp[c % 2], g * 512 + 128 * (c // 2 + 1))
                    last = (q - 3) if q >= 3 else (6, 7, 5)[q] - 8
                    pe.wait_ge(m_["k_copied_a" if last % 2 == 0 else "k_copied_d"],
                               g * 32 + (4 * c + 4 + last // 2 + 1))
                    for j in range(HP):
                        op = nc.tensor.transpose(ps[:, q % 3, j * P:(j + 1) * P],
                                                 k_page[c % 2][:, q, j * P:(j + 1) * P], ident)
                    op.then_inc(s_ktr, 1)

            def new_scores(g):
                pe.wait_ge(m_["queries"], g + 1)
                nc.tensor.matmul(ps[:, 3, 0:NS], ident, cc[:, bass.ds(g * NS + C_SMASK, NS)], start=True, stop=False)
                for s in range(2):
                    for j in range(HP):
                        op = nc.tensor.matmul(ps[32 * j:32 * j + 32, 3, 0:NS], q_bd[:, s, j, :],
                                              pT[:, T_K + j, SEQ:T], start=False, stop=s == 1)
                op.then_inc(m_["score"], 1)

            def scores(g, c):
                pe.wait_ge(m_["k_copied_a"], g * 32 + (4 * c + 8))
                pe.wait_ge(m_["k_copied_d"], g * 32 + (4 * c + 8))
                for s in range(2):
                    for j in range(HP):
                        op = nc.tensor.matmul(ps[32 * j:32 * j + 32, 3, :], q_bd[:, s, j, :], kT[:, s, j, :],
                                              start=s == 0, stop=s == 1)
                op.then_inc(m_["score"], 1)

            def weight_transposes(g, c):
                S = g * 9 + (c + 1)
                if c % 2 == 0 or c < 0:
                    pe.wait_ge(p_["out_copied"], g * 4 + (max(c, 0) // 2 + 1))
                pe.wait_ge(m_["weight"], S + 2)
                pe.wait_ge(m_["tr_copied"], S + 1)
                for j in range(4 if c >= 0 else 1):
                    op = nc.tensor.transpose(ps[:, 4, j * P:(j + 1) * P], aw_s[:, j * P:(j + 1) * P], ident)
                op.then_inc(m_["tr"], 1)

            def new_sums(g):
                pe.wait_ge(m_["tr_copied"], g * 9 + 2)
                pe.wait_ge(m_["rows"], g + 1)
                for j in range(HP):
                    v = v_tok[:, NB:NB + 1, j * P:(j + 1) * P].to_broadcast([P, 2, P])
                    nc.tensor.matmul(tiled(ps[32 * j:32 * j + 32, 6, 0:2 * P]), awT_s[:, 0, 32 * j:32 * j + 32],
                                     v, start=True, stop=False)

            def sums(g, c):
                pe.wait_ge(m_["tr_copied"], g * 9 + (c + 3))
                pe.wait_ge(s_vp[c % 2], g * 512 + 128 * (c // 2 + 1))
                for s in range(2):
                    for q in range(4):
                        for j in range(HP):
                            op = nc.tensor.matmul(ps[32 * j:32 * j + 32, 6, s * P:(s + 1) * P],
                                                  awT_s[:, q, 32 * j:32 * j + 32],
                                                  v_page[c % 2][:, 4 * s + q, j * P:(j + 1) * P],
                                                  start=False, stop=False, skip_group_check=True)
                if c == 7:
                    for j in range(HP):
                        op = nc.tensor.matmul(tiled(ps[32 * j:32 * j + 32, 6, 0:2 * P]), zeros[:, :], tiled(cc[:, 0:2 * P]),
                                              start=False, stop=True)
                op.then_inc(m_["pv"], 1)

            with pe.Fori(0, GROUPS) as g:
                new_scores(g)
                k_transposes(g, 0)
                weight_transposes(g, -1)
                scores(g, 0)
                new_sums(g)
                for c in range(8):
                    if c < 7:
                        k_transposes(g, c + 1)
                    weight_transposes(g, c)
                    if c % 2 == 0:
                        prompt_scores(g, c // 2)
                    else:
                        prompt_transposes(g, c // 2)
                    if c < 7:
                        scores(g, c + 1)
                    sums(g, c)
                    if c % 2 == 1:
                        prompt_sums(g, c // 2)
                pe.wait_ge(m_["rows"], g + 2)
                for s in range(2):
                    op = nc.tensor.transpose(ps[:, 3, s * P:(s + 1) * P], o_pair[:, s, :], ident)
                op.then_inc(m_["rows_tr"], 1)

            pe.wait_ge(s_cs, 1)
            pe.wait_ge(p_["out_copied"], 4 * GROUPS + 1)
            tr_pe(pe, U_CS)
            rms_pe(pe, "conv", sq_c, T)
            rms_pe(pe, "att", sq_a, T, "conv")
            pe.wait_ge(s_op["out"], 1)
            gemm(pe, "out", h_hi, h_lo)
            rms_pe(pe, "cq", sq_ca, T)
            pe.wait_ge(s_op["cq"], 1)
            gemm(pe, "cq", h_hi, h_lo)
            cross_pe(pe)
            pe.wait_ge(s_op["co"], 1)
            gemm(pe, "co", h_hi, h_lo)
            rms_pe(pe, "gu0", sq_ca, T)
            pe.wait_ge(s_op["gu0"], 1)
            for half in range(2):
                gemm(pe, f"gu{half}", h_hi, h_lo)
                pe.wait_ge(s_hid, half + 1)
                gemm(pe, f"down{half}", f_hi, f_lo)
            rms_pe(pe, "fin", sq, T)
            pe.wait_ge(s_y, 1)
            tr_pe(pe, U_Y)


def shape_table():
    c = np.zeros((P, NCONST), np.float32)
    i = np.arange(P)
    c[i, C_ID + i] = 1.0
    seq, step_ = (i // 16) % 2, i % 8
    for g in range(GROUPS):
        for b in range(BS):
            for t in range(TS):
                seen = (b == 2 * g + seq) & (t < step_)
                c[:, C_SMASK + g * NS + b * TS + t] = np.where(seen, 0.0, -1e30)
    c[:, C_CMASK:C_CMASK + P] = np.where(i[None, :] < i[:, None], 0.0, -1e30)
    head = 2 * (i // 32) + (i // 8) % 2
    c[head, C_SEL + i] = 1.0
    return c


_INS = ["x_prompt", "x_sample", "mem_prompt", "cache_sb_k", "cache_sb_v", "cache_mem_k", "cache_mem_v", "state_conv",
        "page_table", "g_mix", "w_in", "sb_bias", "w_conv", "g_attn_out", "g_conv_out", "w_out", "g_mem", "g_ca",
        "w_cq", "w_ck", "w_cv", "w_co", "g_ffn", "w_gate", "w_up", "w_down", "g_final"]
_OUTS = [(1, SEQ, D), (BS, TS, D), (1, 1, SEQ, HEADS, HD), (1, 1, SEQ, HEADS, HD), (1, 1, 2, CH),
         (1, 1, NMEM, CAH, P), (1, 1, NMEM, CAH, P), (1, BS, TS, HEADS, HD), (1, BS, TS, HEADS, HD), (1, BS, 2, CH)]


def kernel(**inputs):
    import concourse.bacc as bacc
    from concourse.bass_utils import run_bass_kernel_spmd

    nc = bacc.Bacc("TRN2", target_bir_lowering=False, num_devices=1)
    arrays, args = {}, []
    for name in _INS:
        a = np.ascontiguousarray(inputs[name])
        arrays[f"in_{name}"] = a
        args.append(nc.dram_tensor(f"in_{name}", a.shape, mybir.dt.from_np(a.dtype), kind="ExternalInput").ap())
    arrays["shape_constants"] = shape_table()
    args.append(nc.dram_tensor("shape_constants", (P, NCONST), F32, kind="ExternalInput").ap())
    for i, shape in enumerate(_OUTS):
        args.append(nc.dram_tensor(f"out_{i}", shape, F32, kind="ExternalOutput").ap())
    hybrid_layer(nc, *args)
    r = run_bass_kernel_spmd(nc, [arrays], core_ids=[0])
    return tuple(r.results[0][f"out_{i}"] for i in range(len(_OUTS)))
```

```python
from contextlib import ExitStack

import numpy as np

import concourse.bass as bass
from concourse import mybir

F32 = mybir.dt.float32
F32R = mybir.dt.float32r
I32 = mybir.dt.int32
ALU = mybir.AluOpType
ACT = mybir.ActivationFunctionType
AX = mybir.AxisListType

P = 128
D = 1024
KD = D // P
SEQ = 512
NB = SEQ // P
BS, TS = 8, 8
NS = BS * TS
T = SEQ + NS
HALF = T // 2
HEADS, HD = 8, 64
HP = HEADS * HD // P
CH = 512
KC = CH // P
PAGES = 32
NMEM = 256
MT = NMEM // P
CAH = 4
SB_SCALE = HD ** -0.5
CA_SCALE = P ** -0.5
EPS = 1e-6
GROUPS = BS // 2
CP = 4
SLOTW = 256
N_POOL = 320

G_MIX, G_MEM, G_CA, G_FFN, G_FIN, G_ATT, G_CONV, W_CONV, NVEC = 0, 8, 16, 24, 32, 40, 44, 48, 60
C_ID, C_SMASK, C_CMASK, C_SEL, NCONST = 0, 128, 384, 512, 640


def hybrid_layer(nc, x_p, x_s, mem, ck, cv, cmk, cmv, st_conv, ptab, g_mix, w_in, sb_bias, w_conv,
                 g_att, g_conv, w_out, g_mem, g_ca, w_cq, w_ck, w_cv, w_co, g_ffn, w_gate, w_up,
                 w_down, g_fin, shape_consts,
                 y_p, y_s, out_k_p, out_v_p, out_c_p, out_mk, out_mv, out_k_s, out_v_s, out_c_s):
    ctx = ExitStack()
    with ctx:
        lo_addr = (nc.sbuf_base + 63) // 64 * 64
        size = 207 * 1024 - 128
        ctx.enter_context(nc.sbuf_tensor("arena", [P, size // 4], F32))
        cursor = [lo_addr]

        def region(n):
            off = cursor[0]
            cursor[0] += n
            assert cursor[0] <= lo_addr + size, cursor[0] - lo_addr
            return off

        def at(name, shape, off, dt=F32):
            return nc.alloc_sbuf_tensor_at(name, [P] + shape, dt, offset=off)

        def sem(name):
            return ctx.enter_context(nc.semaphore(name))

        R_X, R_H, R_P = region(KD * T * 4), region(2 * KD * T * 4), region(24 * T * 4)
        R_W, R_M, R_K = region(6 * 8192), region(16384), region(8192)
        R_V, R_C, R_R = region(14336), region(4096), region(2304 + 1024 + 1024 + 320)
        xT = at("xT", [KD, T], R_X)
        h_hi = at("h_hi", [KD, T], R_H, F32R)
        h_lo = at("h_lo", [KD, T], R_H + KD * T * 4, F32R)
        pT = at("pT", [24, T], R_P)
        w_raw = [at(f"w_raw{i}", [8, SLOTW], R_W + i * 8192) for i in range(2)]
        w_hi = [at(f"w_hi{i}", [8, SLOTW], R_W + (4 - 2 * i) * 8192, F32R) for i in range(2)]
        w_lo = [at(f"w_lo{i}", [8, SLOTW], R_W + (5 - 2 * i) * 8192, F32R) for i in range(2)]
        rstd = at("rstd", [T], R_R)
        rstd_m = at("rstd_m", [NMEM], R_R + 2304)
        ptb = at("ptb", [BS * PAGES], R_R + 3328, I32)
        cs = at("cs", [KC, 18], R_R + 4352)
        x_sq = at("x_sq", [D], R_P)
        x_dg = at("x_dg", [5, P], R_P + 4096)
        x_tok = at("x_tok", [5, D], R_P + 18432)
        mT = at("mT", [KD, NMEM], R_K)
        m_dg = at("m_dg", [MT, P], R_P + 6656)
        m_tok = at("m_tok", [MT, D], R_V)
        st_rows = at("st_rows", [CH], R_V + 8192)
        vec_rows = at("vec_rows", [P], R_V + 10240)
        m_hi = at("m_hi", [KD, NMEM], R_M, F32R)
        m_lo = at("m_lo", [KD, NMEM], R_M + 8192, F32R)
        mkT = at("mkT", [CAH, NMEM], R_K)
        mv_tok = at("mv_tok", [MT, CH], R_K + 4096)
        v_tok = at("v_tok", [5, CH], R_V)
        mvT = at("mvT", [CAH, NMEM], R_V + 10240)
        k_rows = at("k_rows", [5, CH], R_H + 16384)
        c_sum = at("c_sum", [T], R_V)
        c_sq = at("c_sq", [T], R_V + 2304)
        rstd_c = at("rstd_c", [T], R_P + 12 * T * 4 + 6656)
        T_Q, T_K, T_A, T_B, T_C, T_U = 0, 4, 8, 12, 16, 20
        mk_rows = at("mk_rows", [MT, CH], R_P + T_B * T * 4)
        cs_rows = at("cs_rows", [CH], R_P + T_B * T * 4 + 4096)
        beta = at("beta", [2, SEQ], R_P + T_B * T * 4)
        om = at("om", [2, SEQ], R_P + T_B * T * 4 + 4096)
        aw = at("aw", [2, SEQ], R_P + T_U * T * 4)
        awT = at("awT", [2, 4, P], R_P + T_U * T * 4 + 4096)
        run = at("run", [2, SEQ + 1], R_M)
        q_fix = at("q_fix", [SEQ], R_M + 4224)
        k_fix = at("k_fix", [SEQ], R_M + 6272)
        v_fix = at("v_fix", [4, P], R_M + 8320)
        q_bd = at("q_bd", [2, HP, 32], R_M + 10368)
        beta_s = at("beta_s", [SEQ], R_M + 11392)
        om_s = at("om_s", [SEQ], R_M + 13440)
        aw_s = at("aw_s", [SEQ], R_H + 32768)
        awT_s = at("awT_s", [4, P], R_H + 34816)
        zeros = at("zeros", [32], region(128))
        run_s = at("run_s", [SEQ + 1], region(2080))
        o_pair = at("o_pair", [2, P], region(1024))
        k_page = [at(f"k_page{i}", [8, CH], R_H + i * 16384) for i in range(2)]
        v_page = [at(f"v_page{i}", [8, CH], R_W + i * 16384) for i in range(2)]
        kT = at("kT", [2, HP, SEQ], R_W + 32768)
        sq_a = at("sq_a", [KC, T], R_P)
        caq = at("caq", [CAH, T], R_P)
        caoT = at("caoT", [CAH, T], R_P + CAH * T * 4)
        R_CA = R_P + 2 * CAH * T * 4
        prob = at("prob", [2, 4, NMEM], R_CA)
        probT = at("probT", [2, MT, SEQ], R_CA + 8192)
        qc = at("qc", [4, CAH, 32], R_CA + 16384)
        ca_rows = at("ca_rows", [P], region(512))
        r_sum = at("r_sum", [T], R_CA + 18432)
        r_sq = at("r_sq", [T], R_CA + 18432 + T * 4)
        mem_off = [R_M + i * 4096 for i in range(4)] + [R_V + i * 4096 for i in range(3)] + \
            [R_CA + 18432 + 2 * T * 4 + i * 4096 for i in range(3)]
        mem_place = [at(f"mem_place{i}", [MT, CH], off) for i, off in enumerate(mem_off)]
        smk_tok = mem_place[0:BS]
        smv_tok = mem_place[BS:BS + 2] + mem_place[0:BS - 2]
        smkT = at("smkT", [BS, CAH, NMEM], R_H)
        f_hi = at("f_hi", [12, T], R_P, F32R)
        f_lo = at("f_lo", [12, T], R_P + 12 * T * 4, F32R)
        gbuf = at("gbuf", [2, T], R_M)
        sbuf_ = at("sbuf_", [2, T], R_M + 4608)
        ubuf = at("ubuf", [2, T], R_M + 9216)
        yT = at("yT", [KD, T], R_H)
        y_rows = at("y_rows", [5, D], R_P)
        cc = at("cc", [NCONST], R_C)
        ident = cc[:, C_ID:C_ID + P]
        cvec = at("cvec", [NVEC], R_C + 2560)
        ones = at("ones", [P], R_C + 2816)
        cst = at("cst", [8], R_C + 3328)
        bias_p = at("bias_p", [2, HEADS], R_C + 3360)
        bias_s = at("bias_s", [2], R_C + 3424)
        bias_col = at("bias_col", [1], R_C + 3456)
        bias_dg = at("bias_dg", [HEADS], R_C + 3488)
        stT = at("stT", [KC, 2 * BS], R_C + 3520)
        sm = at("sm", [40], R_C + 3776)
        bias_fix = at("bias_fix", [2, 2], R_C + 4000)
        token = at("token", [64], region(256))
        x_ss = at("x_ss", [8], R_C + 4032)
        y_r = at("y_r", [5], R_C + 4064)

        ps = ctx.enter_context(nc.psum_tensor("ps", [P, 8, 512], F32))

        def halves(ap):
            return ap.rearrange("p (a b) -> p a b", a=2)

        def tiled(ap, f=P):
            return ap.rearrange("p (a f) -> p a f", f=f)

        def kview(w):
            return w[0].rearrange("(k p) n -> p k n", p=P)

        views = {"inb": kview(w_in)[:, :, T_B * P:], "in": kview(w_in), "ck": kview(w_ck), "cv": kview(w_cv), "out": kview(w_out),
                 "cq": kview(w_cq), "co": kview(w_co), "gate": kview(w_gate), "up": kview(w_up),
                 "down": kview(w_down)}
        STAGES = [("inb", 8, 3), ("in", 8, 3), ("ck", 8, 1), ("cv", 8, 1), ("out", 8, 2), ("cq", 8, 1), ("co", 4, 2),
                  ("gu0", 8, 6), ("down0", 6, 4), ("gu1", 8, 5), ("down1", 5, 4)]
        FF0 = (0, 12)
        NAMES = [name for name, _, _ in STAGES]
        KN = {name: kn for name, kn, _ in STAGES}
        PAIRS = {name: pairs for name, _, pairs in STAGES}
        SLOT0 = {name: sum(2 * p for _, _, p in STAGES[:i]) for i, name in enumerate(NAMES)}

        s_id, s_x = sem("identity_loaded"), [sem(f"x_loaded{i}") for i in range(3)]
        s_const, s_m, s_pt = sem("consts_loaded"), sem("mem_loaded"), sem("ptab_loaded")
        s_set = sem("ones_and_token_set")
        s_tr, s_ev = sem("unit_transposed"), [sem("bank4_copied"), sem("bank5_copied")]
        s_bmm, s_bc = sem("bias_product"), sem("bias_copied")
        s_full = [sem("weights_loaded0"), sem("weights_loaded1")]
        s_whi, s_wlo = sem("weights_hi"), sem("weights_lo")
        s_half_hi, s_half_lo = sem("half_slot_hi"), sem("half_slot_lo")
        s_tile = {n: sem(f"tile_{n}") for n in NAMES}
        s_free = {n: sem(f"banks_{n}") for n in NAMES}
        s_op = {n: sem(f"operand_{n}") for n in ("inb", "ck", "out", "cq", "co", "gu0")}
        s_hi = {n: sem(f"operand_hi_{n}") for n in ("inb", "ck", "out", "cq", "co", "gu0")}
        NORMS = ["inb", "ck", "att", "conv", "cq", "gu0", "fin"]
        s_acc = {n: sem(f"square_added_{n}") for n in ("out", "co", "down1")}
        s_sq = {n: sem(f"squares_{n}") for n in NORMS}
        s_sum = {n: sem(f"sums_{n}") for n in NORMS}
        s_ms = {n: sem(f"meansq_{n}") for n in NORMS}
        s_rt = {n: sem(f"root_{n}") for n in NORMS}
        s_evac = {n: sem(f"evacuated_{n}") for n in NAMES}
        s_dve = sem("vector_step")
        s_out, s_kv_out = sem("outputs_stored"), sem("kv_rows_stored")
        s_sig = sem("sigmoid_done")
        s_h, s_hid = sem("hidden_step"), sem("hidden_ready")
        s_y, s_sq_early, s_mix = sem("y_rstd"), sem("early_squares"), sem("mixer_scaled")
        p_ = {n: sem(f"prompt_{n}") for n in ("qk_fixed", "bias_fixed", "v_fixed", "score", "beta", "om", "scan", "weight", "tr",
                                              "copied_a", "copied_d", "out", "out_copied")}
        m_ = {n: sem(f"sample_{n}") for n in ("queries", "k_copied_a", "k_copied_d", "score", "beta",
                                              "om", "run", "weight", "tr", "tr_copied", "pv", 
                                              "rows", "rows_tr", "rows_copied")}
        s_kp = [sem("k_pages0"), sem("k_pages1")]
        s_vp = [sem("v_pages0"), sem("v_pages1")]
        s_ktr = sem("k_page_transposed")
        c_ = {n: sem(f"cross_{n}") for n in ("score", "max", "exp", "prob", "tr", "tr_copied", "out", "out_copied",
                                             "queries", "zeroed", "rows", "rows_tr")}
        s_cmk, s_cmv = sem("mem_k_loaded"), [sem("mem_v_loaded0"), sem("mem_v_loaded1")]

        steps, grants = [0], [0]

        def step(dve, ins):
            steps[0] += 1
            ins.then_inc(s_dve, 1)
            dve.wait_ge(s_dve, steps[0])

        def grant(semaphore, n):
            grants[0] += 1
            nc.vector.memset(token[0:1, grants[0]:grants[0] + 1], 0.0).then_inc(semaphore, n)

        units = []

        def batch(pairs_):
            a = len(units)
            units.extend(pairs_)
            return range(a, len(units))

        def rows_of(m):
            return P if m < NB else NS

        def to_tokens(src, k0, m, dst):
            r = rows_of(m)
            return [src[:, k0 + j, m * P:m * P + r] for j in range(4)], tiled(dst[0:r, :])

        U_X = batch([([x_tok[0:rows_of(m), m, (4 * kh + j) * P:(4 * kh + j + 1) * P] for j in range(4)],
                      xT[:, 4 * kh:4 * kh + 4, m * P:m * P + rows_of(m)]) for m in range(5) for kh in range(2)])
        U_VEC = batch([([vec_rows[0:NVEC, :]], cvec[:, :].rearrange("p (a f) -> p a f", a=1)),
                       ([st_rows[0:2 * BS, j * P:(j + 1) * P] for j in range(4)], stT[:, :, :])])
        U_M = batch([([m_tok[:, m, (4 * kh + j) * P:(4 * kh + j + 1) * P] for j in range(4)],
                      mT[:, 4 * kh:4 * kh + 4, m * P:(m + 1) * P]) for m in range(MT) for kh in range(2)])
        U_VT = batch([to_tokens(pT, T_A, m, v_tok[:, m, :]) for m in range(5)])
        U_KT = batch([to_tokens(pT, T_K, m, k_rows[:, m, :]) for m in range(5)])
        U_MK = batch([([cs[:, j, :] for j in range(4)], tiled(cs_rows[0:18, :]))] + [([src[:, j, m * P:(m + 1) * P] for j in range(4)], tiled(dst[:, m, :]))
                      for src, dst in ((mkT, mk_rows), (mvT, mv_tok)) for m in range(MT)])
        U_SMK = [batch([([smk_tok[b][:, m, j * P:(j + 1) * P] for j in range(4)], smkT[:, b, :, m * P:(m + 1) * P])
                        for b in (2 * i, 2 * i + 1) for m in range(MT)]) for i in range(4)]
        U_Y = batch([to_tokens(yT, 4 * kh, m, y_rows[:, m, kh * 512:(kh + 1) * 512])
                     for m in range(5) for kh in range(2)])

        def copied(eng, u):
            eng.wait_ge(s_ev[0], u // 2 + 1)
            eng.wait_ge(s_ev[1], (u + 1) // 2)

        def tr_pe(pe, us):
            for u in us:
                srcs, _ = units[u]
                if u >= 2:
                    pe.wait_ge(s_ev[u % 2], u // 2)
                for j, src in enumerate(srcs):
                    p_in, f = src.shape[0], src.shape[-1]
                    op = nc.tensor.transpose(ps[0:f, 4 + u % 2, j * P:j * P + p_in], src, ident[0:p_in, 0:p_in])
                op.then_inc(s_tr, 1)

        def tr_copy(eng, us, scale=None):
            for u in us:
                srcs, dst = units[u]
                p_in, f = srcs[0].shape[0], srcs[0].shape[-1]
                eng.wait_ge(s_tr, u + 1)
                bank = tiled(ps[0:f, 4 + u % 2, 0:len(srcs) * P])[:, :, 0:p_in]
                c = scale(u) if scale else None
                if eng is nc.vector:
                    op = nc.vector.tensor_copy(dst, bank) if c is None else \
                        nc.vector.tensor_scalar(dst, bank, c, None, ALU.mult)
                else:
                    op = nc.scalar.activation(dst, bank, ACT.Copy, scale=1.0 if c is None else c)
                op.then_inc(s_ev[u % 2], 1)

        def even(us):
            return [u for u in us if u % 2 == 0]

        def odd(us):
            return [u for u in us if u % 2]

        def rms_pe(pe, name, total, n, after=None):
            if after:
                pe.wait_ge(s_rt[after], 1)
            pe.wait_ge(s_sum[name], 1)
            w = n // 2
            for hf in range(2):
                op = nc.tensor.matmul(ps[:, 6 + hf, 0:w], ones[:, :], total[:, hf * w:(hf + 1) * w],
                                      start=True, stop=True)
            op.then_inc(s_ms[name], 1)

        def rms_root(act, name, dst, n, feats):
            nc.scalar.preload_act_table(ACT.Sqrt)
            act.wait_ge(s_ms[name], 1)
            nc.scalar.activation(halves(dst), ps[:, 6:8, 0:n // 2], ACT.Sqrt,
                                 bias=cst[:, 0:1], scale=1.0 / feats).then_inc(s_rt[name], 1)

        def rms_inv(dve, name, buf):
            dve.wait_ge(s_rt[name], 1)
            step(dve, nc.vector.reciprocal(buf, buf))

        def hi_parts(act, name, src, g0, tiles, dst0=0):
            for k in tiles:
                scale = 1.0 if g0 is None else cvec[:, g0 + k:g0 + k + 1]
                hi = m_hi if name == "ck" else h_hi
                nc.scalar.activation(hi[:, dst0 + k, :], src[:, k, :], ACT.Copy, scale=scale).then_inc(s_hi[name], 1)

        def lo_parts(dve, name, src, g0, tiles, dst0=0, done=0):
            hi, lo = (m_hi, m_lo) if name == "ck" else (h_hi, h_lo)
            for n, k in enumerate(tiles):
                dve.wait_ge(s_hi[name], done + n + 1)
                h = hi[:, dst0 + k, :].bitcast(F32)
                if g0 is None:
                    op = nc.vector.tensor_tensor(lo[:, dst0 + k, :], src[:, k, :], h, ALU.subtract)
                else:
                    op = nc.vector.scalar_tensor_tensor(out=lo[:, dst0 + k, :], in0=src[:, k, :],
                                                        scalar=cvec[:, g0 + k:g0 + k + 1], in1=h,
                                                        op0=ALU.mult, op1=ALU.subtract)
                op.then_inc(s_op[name], 1)

        def load_stage(sp, name, grants=()):
            n0, kn = SLOT0[name], KN[name]

            def body(i):
                for s in range(2):
                    sp.wait_ge(s_wlo, i * 2 + (n0 + s - 1))
                    if name[:2] == "gu":
                        src = views["gate" if s == 0 else "up"][:, :, bass.ds(i * SLOTW + FF0[int(name[2])] * P, SLOTW)]
                    elif name[:4] == "down":
                        k0 = FF0[int(name[4])] + s * kn
                        src = views["down"][:, k0:k0 + kn, bass.ds(i * SLOTW, SLOTW)]
                    else:
                        src = views[name][:, :, bass.ds(i * (2 * SLOTW) + s * SLOTW, SLOTW)]
                    sp.dma_start(w_raw[s][:, 0:kn, :], src).then_inc(s_full[s], 16)
            if n0 == 0:
                with sp.Fori(1, PAIRS[name]) as i:
                    body(i)
            else:
                with sp.Fori(0, PAIRS[name]) as i:
                    body(i)

        def split_hi(act, name, i, s):
            act.wait_ge(s_full[s], i * 16 + (SLOT0[name] * 8 + 16))
            nc.scalar.activation(w_hi[s][:, 0:KN[name], :], w_raw[s][:, 0:KN[name], :], ACT.Copy).then_inc(s_whi, 1)

        def split_stage(act, name, more=None, between=None, after=None, first=True):
            prev = NAMES[NAMES.index(name) - 1] if name != "inb" else None
            for s in range(2 if first else 0):
                if prev:
                    act.wait_ge(s_tile[prev], 4 * PAIRS[prev] - 2 + 2 * s)
                split_hi(act, name, 0, s)
                if s == 0 and between:
                    between()
            if after:
                after()
            if more:
                more(0)
            if PAIRS[name] > 1:
                with act.Fori(1, PAIRS[name]) as i:
                    for s in range(2):
                        act.wait_ge(s_tile[name], i * 4 + (2 * s - 2))
                        split_hi(act, name, i, s)
                    if more:
                        more(i)

        def split_lo(s, ks):
            return nc.gpsimd.tensor_tensor(w_lo[s][:, ks, :], w_raw[s][:, ks, :], w_hi[s][:, ks, :].bitcast(F32),
                                           ALU.subtract)

        def split_hi_halves(act, name, first, second):
            act.wait_ge(s_full[0], SLOT0[name] * 8 + 16)
            nc.scalar.activation(w_hi[0][:, first, :], w_raw[0][:, first, :], ACT.Copy).then_inc(s_half_hi, 1)
            nc.scalar.activation(w_hi[0][:, second, :], w_raw[0][:, second, :], ACT.Copy).then_inc(s_whi, 1)

        LOW, HIGH = slice(0, KC), slice(KC, 2 * KC)

        def lo_stage(pool, name):
            def body(i, s):
                pool.wait_ge(s_whi, i * 2 + (SLOT0[name] + s + 1))
                split_lo(s, slice(0, KN[name])).then_inc(s_wlo, 1)
            halved = name in ("inb", "out")
            if halved:
                n = ("inb", "out").index(name) + 1
                pool.wait_ge(s_half_hi, n)
                split_lo(0, LOW if n == 1 else HIGH).then_inc(s_half_lo, 1)
                pool.wait_ge(s_whi, SLOT0[name] + 1)
                split_lo(0, HIGH if n == 1 else LOW).then_inc(s_wlo, 1)
                body(0, 1)
            with pool.Fori(1 if halved else 0, PAIRS[name]) as i:
                for s in range(2):
                    body(i, s)

        def gemm(pe, name, hi, lo, n=T, peel=False, hook=None, prev=None):
            kn, down = KN[name], name[:4] == "down"
            parts = [(a, min(a + HALF, n)) for a in range(0, n, HALF)]

            def products(s, t, ks, begin, end, k0=0):
                for k in ks:
                    for w, (weights, x) in enumerate(((w_hi, hi), (w_hi, lo), (w_lo, hi))):
                        for hf, (a, b) in enumerate(parts):
                            op = nc.tensor.matmul(ps[:, 2 * t + hf, 0:b - a], weights[s][:, k, t * P:(t + 1) * P],
                                                  x[:, k0 + k, a:b],
                                                  start=begin and k == ks[0] and w == 0,
                                                  stop=end and k == ks[-1] and w == 2)
                return op

            def slot(i, s, gu=None):
                pe.wait_ge(s_wlo, i * 2 + (SLOT0[name] + s + 1))
                for t in range(2):
                    if gu:
                        pe.wait_ge(s_free[gu], 4 * PAIRS[gu] + 1 + t)
                    elif not down:
                        pe.wait_ge(s_free[name], i * 4 + (2 * s + t + 1))
                    elif s == 0:
                        pe.wait_ge(s_free[name], i * 2 + (t + 1))
                    products(s, t, range(kn), not down or s == 0, not down or s == 1, s * kn if down else 0)\
                        .then_inc(s_tile[name], 1)

            if peel:
                if name == "inb":
                    pe.wait_ge(s_half_lo, 1)
                else:
                    pe.wait_ge(s_wlo, SLOT0[name] + 1)
                if prev:
                    pe.wait_ge(s_free[prev], 4 * PAIRS[prev] + 1)
                else:
                    pe.wait_ge(s_free[name], 2)
                for k in range(kn):
                    pe.wait_ge(s_op[name], k + 1)
                    if name == "inb" and k == KC:
                        pe.wait_ge(s_wlo, 1)
                    op = products(0, 0, [k], k == 0, k == kn - 1)
                op.then_inc(s_tile[name], 1)
                if hook:
                    hook()
                if prev:
                    pe.wait_ge(s_free[prev], 4 * PAIRS[prev] + 2)
                products(0, 1, range(kn), True, True).then_inc(s_tile[name], 1)
                slot(0, 1)
                if PAIRS[name] > 1:
                    with pe.Fori(1, PAIRS[name]) as i:
                        for s in range(2):
                            slot(i, s)
            elif down:
                gu = "gu" + name[4]
                pe.wait_ge(s_h, 8 * PAIRS["gu0"] * int(name[4]) + 24)
                slot(0, 0, gu)
                pe.wait_ge(s_hid, int(name[4]) + 1)
                slot(0, 1)
                with pe.Fori(1, PAIRS[name]) as i:
                    for s in range(2):
                        slot(i, s)
            else:
                with pe.Fori(0, PAIRS[name]) as i:
                    for s in range(2):
                        slot(i, s)

        def gemm_out(pe):
            def products(s, t, conv, ks):
                for k in ks:
                    for w, (weights, x) in enumerate(((w_hi, h_hi), (w_hi, h_lo), (w_lo, h_hi))):
                        for hf in range(2):
                            op = nc.tensor.matmul(ps[:, (0 if conv else 4) + 2 * t + hf, 0:HALF],
                                                  weights[s][:, k + (KC if conv else 0), t * P:(t + 1) * P],
                                                  x[:, k + (0 if conv else KC), hf * HALF:(hf + 1) * HALF],
                                                  start=k == 0 and w == 0, stop=k == KC - 1 and w == 2)
                return op

            def slot(i, s):
                pe.wait_ge(s_wlo, i * 2 + (SLOT0["out"] + s + 1))
                for t in range(2):
                    pe.wait_ge(s_free["out"], i * 4 + (2 * s + t + 1))
                    products(s, t, True, range(KC))
                    products(s, t, False, range(KC)).then_inc(s_tile["out"], 1)

            pe.wait_ge(s_half_lo, 2)
            for k in range(KC):
                pe.wait_ge(s_op["out"], k + 1)
                products(0, 0, True, [k])
            rms_pe(pe, "att", sq_a[:, 0, :], T, "conv")
            products(0, 1, True, range(KC))
            pe.wait_ge(s_wlo, SLOT0["out"] + 1)
            for k in range(KC):
                pe.wait_ge(s_op["out"], KC + k + 1)
                op = products(0, 0, False, [k])
            op.then_inc(s_tile["out"], 1)
            pe.wait_ge(s_rt["att"], 1)
            products(0, 1, False, range(KC)).then_inc(s_tile["out"], 1)
            slot(0, 1)
            with pe.Fori(1, PAIRS["out"]) as i:
                for s in range(2):
                    slot(i, s)

        def load_pages(eng, g, c, cache, buf, loaded, used, uses):
            for par in range(2):
                for s in range(2):
                    for j in range(4):
                        page = eng.value_load(ptb[0:1, bass.ds(g * 64 + (32 * s + 28 - 8 * c - 4 * par + j), 1)],
                                              min_val=0, max_val=N_POOL - 1)
                        if s == 0 and j == 0:
                            eng.wait_ge(used, g * (8 * uses) + (2 * c + par + 1) * uses)
                            eng.wait_ge(s_pt, 16)
                        eng.dma_start(buf[par][:, 4 * s + j:4 * s + j + 1, :],
                                      cache[0, bass.ds(page, 1)].rearrange("o p h d -> p o (h d)"))\
                            .then_inc(loaded[par], 16)

        def pair(t):
            return ps[:, 2 * t:2 * t + 2, 0:HALF]

        def tile_of(dst, i):
            return dst[:, bass.ds(i, 1), :].rearrange("p o (a b) -> p (o a) b", a=2)

        def evac_scaled(dve, name, dst, scale):
            with dve.Fori(0, PAIRS[name]) as i:
                for j in range(4):
                    dve.wait_ge(s_tile[name], i * 4 + (j + 1))
                    nc.vector.tensor_tensor(tile_of(dst, i * 4 + j), pair(j % 2), halves(scale), ALU.mult)\
                        .then_inc(s_free[name], 1)

        def evac_mem(dve, name, dst, between):
            for j in range(4):
                dve.wait_ge(s_tile[name], j + 1)
                nc.vector.tensor_tensor(dst[:, j, :], ps[:, 2 * (j % 2), 0:NMEM], rstd_m[:, :], ALU.mult)\
                    .then_inc(s_free[name], 1)
                between(j)

        def evac_residual(dve, name, total=None, square=None, scaled=None, next_lo=None):
            down = name[:4] == "down"
            n = 2 if down else 4
            if total is not None:
                step(dve, nc.vector.memset(total[:, :], 0.0))

            def tile(i, j, last=False):
                dve.wait_ge(s_tile[name], i * 4 + (j + 3 if down else j + 1))
                x = tile_of(xT, i * n + j)
                if last:
                    next_lo(range(2))
                if name == "out":
                    nc.vector.tensor_tensor(halves(square), pair(2 + j % 2), halves(rstd[:, :]), ALU.mult)\
                        .then_inc(s_mix, 1)
                    dve.wait_ge(s_mix, i * (2 * n) + (2 * j + 1))
                    nc.vector.tensor_tensor(x, x, halves(square), ALU.add).then_inc(s_mix, 1)
                    dve.wait_ge(s_mix, i * (2 * n) + (2 * j + 2))
                nc.vector.tensor_tensor(x, pair(j % 2), x, ALU.add).then_inc(s_free[name], 1)
                if total is not None:
                    if last:
                        next_lo(range(2, KD))
                    dve.wait_ge(s_free[name], i * n + (j + 3))
                    nc.vector.tensor_tensor(halves(square), x, x, ALU.mult).then_inc(s_acc[name], 1)
                    if scaled is not None:
                        nc.vector.tensor_scalar(tile_of(scaled, i * n + j), x,
                                                cvec[:, bass.ds(i * n + (G_FIN + j), 1)], None, ALU.mult)
                    dve.wait_ge(s_acc[name], i * (2 * n) + (2 * j + 1))
                    nc.vector.tensor_tensor(total[:, :], total[:, :], square[:, :], ALU.add).then_inc(s_acc[name], 1)
                    dve.wait_ge(s_acc[name], i * (2 * n) + (2 * j + 2))
            peeled = 1 if next_lo else 0
            with dve.Fori(0, PAIRS[name] - peeled) as i:
                for j in range(n):
                    tile(i, j)
            for j in range(n if peeled else 0):
                tile(PAIRS[name] - 1, j, j == n - 1)

        UNITS = CAH + 2

        def n_rows(u):
            return 4 if u < CAH else 1

        def own(u):
            return probT[:, u % 2, :, :].rearrange("p a b -> p (a b)").rearrange("p (b m r) -> p b m r", b=4, m=MT)

        def cross_exp(act, u):
            act.wait_ge(c_["max"], u + 1)
            for j in range(n_rows(u)):
                z = ps[:, 2 * (u % 2) + j // 2, (j % 2) * NMEM:(j % 2 + 1) * NMEM]
                op = nc.scalar.activation(prob[:, u % 2, j, :], z, ACT.Exp, scale=CA_SCALE,
                                          bias=sm[:, 4 + j:5 + j], accum_out=sm[:, 8 + j:9 + j])
            op.then_inc(c_["exp"], 1)

        def cross_act(act):
            nc.scalar.preload_act_table(ACT.Exp)
            cross_exp(act, 0)
            tr_copy(act, even(U_SMK[0]))
            for u in range(UNITS):
                act.wait_ge(c_["tr"], u + 1)
                if u < CAH:
                    nc.scalar.activation(probT[:, u % 2, :, :], ps[:, 2 * (u % 2):2 * (u % 2) + 2, :], ACT.Copy)\
                        .then_inc(c_["tr_copied"], 1)
                else:
                    act.wait_ge(c_["zeroed"], u - CAH + 1)
                    for m in range(MT):
                        src = ps[:, 2 * (u % 2) + m, 0:P].rearrange("p (h b t) -> p b h t", h=CAH, b=4)
                        dst = own(u)[:, :, m, :].rearrange("p b (h n) -> p b h n", h=CAH)
                        for b in range(4):
                            op = nc.scalar.activation(dst[:, b, :, 8 * b:8 * b + 8], src[:, b, :, :], ACT.Copy)
                    op.then_inc(c_["tr_copied"], 1)
                if u + 1 < 4:
                    tr_copy(act, even(U_SMK[u + 1]))
                if u + 1 < UNITS:
                    cross_exp(act, u + 1)
                if u == CAH:
                    for s in range(2):
                        split_hi(act, "co", 0, s)
                act.wait_ge(c_["out"], u + 1)
                if u < CAH:
                    dst, src = caoT[:, u, 0:SEQ], ps[:, 6 + u % 2, :]
                else:
                    nc.scalar.activation(ca_rows[:, :], ps[:, 6 + u % 2, 0:P], ACT.Copy).then_inc(c_["rows"], 1)
                    act.wait_ge(c_["rows_tr"], u - CAH + 1)
                    dst = caoT[:, :, SEQ + 32 * (u - CAH):SEQ + 32 * (u - CAH) + 32]
                    src = tiled(ps[:, 6 + u % 2, P:2 * P], 32)
                nc.scalar.activation(dst, src, ACT.Copy).then_inc(c_["out_copied"], 1)


        def hidden_dve(dve, half):
            name = f"gu{half}"
            h0 = 8 * PAIRS["gu0"] * half
            g0 = 2 * PAIRS["gu0"] * half
            with dve.Fori(0, PAIRS[name]) as i:
                for t in range(2):
                    dve.wait_ge(s_tile[name], i * 4 + (t + 1))
                    nc.vector.tensor_tensor(halves(gbuf[:, t, :]), pair(t), halves(rstd[:, :]), ALU.mult)\
                        .then_inc(s_free[name], 1)
                for t in range(2):
                    dve.wait_ge(s_tile[name], i * 4 + (t + 3))
                    nc.vector.tensor_tensor(halves(ubuf[:, t, :]), pair(t), halves(rstd[:, :]), ALU.mult)\
                        .then_inc(s_free[name], 1)
                    dve.wait_ge(s_sig, i * 2 + (g0 + t + 1))
                    nc.vector.tensor_tensor(gbuf[:, t, :], gbuf[:, t, :], sbuf_[:, t, :], ALU.mult).then_inc(s_h, 1)
                    dve.wait_ge(s_h, i * 8 + (h0 + 4 * t + 1))
                    nc.vector.tensor_tensor(ubuf[:, t, :], ubuf[:, t, :], gbuf[:, t, :], ALU.mult).then_inc(s_h, 1)
                    dve.wait_ge(s_h, i * 8 + (h0 + 4 * t + 2))
                    hi = f_hi[:, bass.ds(i * 2 + t, 1), :].rearrange("p o n -> p (o n)")
                    lo = f_lo[:, bass.ds(i * 2 + t, 1), :].rearrange("p o n -> p (o n)")
                    nc.vector.tensor_copy(hi, ubuf[:, t, :]).then_inc(s_h, 1)
                    dve.wait_ge(s_h, i * 8 + (h0 + 4 * t + 3))
                    nc.vector.tensor_tensor(lo, ubuf[:, t, :], hi.bitcast(F32), ALU.subtract).then_inc(s_h, 1)
            grant(s_hid, 1)

        def cross_queries(dve, gg):
            for b in range(4):
                c0 = SEQ + 32 * gg + 8 * b
                op = nc.vector.tensor_copy(qc[:, b, :, 8 * b:8 * b + 8], caq[:, :, c0:c0 + 8])
            op.then_inc(c_["queries"], 1)

        def cross_max(dve, u):
            n = n_rows(u)
            dve.wait_ge(c_["score"], u + 1)
            if n == 4:
                z = ps[:, 2 * (u % 2):2 * (u % 2) + 2, :].rearrange("p a (b m) -> p a b m", b=2)
                step(dve, nc.vector.tensor_reduce(sm[:, 0:4].rearrange("p (a b) -> p a b", a=2), z, AX.X, ALU.max))
            else:
                step(dve, nc.vector.tensor_reduce(sm[:, 0:1], ps[:, 2 * (u % 2), 0:NMEM], AX.X, ALU.max))
            nc.vector.tensor_scalar(sm[:, 4:4 + n], sm[:, 0:n], -CA_SCALE, None, ALU.mult).then_inc(c_["max"], 1)
            if u == CAH:
                cross_queries(dve, 1)

        def cross_norm(dve, u):
            n = n_rows(u)
            dve.wait_ge(c_["exp"], u + 1)
            step(dve, nc.vector.reciprocal(sm[:, 12:12 + n], sm[:, 8:8 + n]))
            for j in range(n):
                op = nc.vector.tensor_scalar(prob[:, u % 2, j, :], prob[:, u % 2, j, :], sm[:, 12 + j:13 + j], None,
                                             ALU.mult)
            op.then_inc(c_["prob"], 1)

        def cross_dve(dve):
            step(dve, nc.vector.memset(qc[:, :, :, :], 0.0))
            cross_queries(dve, 0)
            cross_max(dve, 0)
            tr_copy(dve, odd(U_SMK[0]))
            cross_norm(dve, 0)
            for u in range(1, UNITS):
                cross_max(dve, u)
                if u < 4:
                    tr_copy(dve, odd(U_SMK[u]))
                else:
                    dve.wait_ge(c_["out"], u - 1)
                    nc.vector.memset(own(u), 0.0).then_inc(c_["zeroed"], 1)
                cross_norm(dve, u)

        def cross_scores(pe, u):
            z0 = 2 * (u % 2)
            if u < CAH:
                for qb in range(NB):
                    op = nc.tensor.matmul(ps[:, z0 + qb // 2, (qb % 2) * NMEM:(qb % 2 + 1) * NMEM],
                                          caq[:, u, qb * P:(qb + 1) * P], mkT[:, u, :], start=True, stop=True)
            else:
                gg = u - CAH
                copied(pe, U_SMK[2 * gg + 1][-1])
                pe.wait_ge(c_["queries"], gg + 1)
                for b in range(4):
                    for h in range(CAH):
                        op = nc.tensor.matmul(ps[32 * h:32 * h + 32, z0, 0:NMEM], qc[:, b, h, :],
                                              smkT[:, 4 * gg + b, h, :], start=b == 0, stop=b == 3)
            op.then_inc(c_["score"], 1)

        def cross_pe(pe):
            pe.wait_ge(s_evac["cq"], 1)
            cross_scores(pe, 0)
            pe.wait_ge(s_cmk, 16 * BS)
            tr_pe(pe, U_SMK[0])
            cross_scores(pe, 1)
            for u in range(UNITS):
                pe.wait_ge(c_["prob"], u + 1)
                for m in range(MT):
                    for j in range(n_rows(u)):
                        op = nc.tensor.transpose(ps[:, 2 * (u % 2) + m, j * P:(j + 1) * P],
                                                 prob[:, u % 2, j, m * P:(m + 1) * P], ident)
                op.then_inc(c_["tr"], 1)
                if u + 1 < 4:
                    tr_pe(pe, U_SMK[u + 1])
                pe.wait_ge(c_["tr_copied"], u + 1)
                if u >= 2:
                    pe.wait_ge(c_["out_copied"], u - 1)
                if u < CAH:
                    for m in range(MT):
                        op = nc.tensor.matmul(ps[:, 6 + u % 2, :], mv_tok[:, m, u * P:(u + 1) * P],
                                              probT[:, u % 2, m, :], start=m == 0, stop=m == MT - 1)
                else:
                    pe.wait_ge(s_cmv[u - CAH], 64)
                    for b in range(4):
                        for m in range(MT):
                            for h in range(CAH):
                                op = nc.tensor.matmul(ps[32 * h:32 * h + 32, 6 + u % 2, 0:P],
                                                      own(u)[:, b, m, 32 * h:32 * h + 32],
                                                      smv_tok[4 * (u - CAH) + b][:, m, h * P:(h + 1) * P],
                                                      start=b == 0 and m == 0, stop=b == 3 and m == MT - 1)
                op.then_inc(c_["out"], 1)
                if u >= CAH:
                    pe.wait_ge(c_["rows"], u - CAH + 1)
                    nc.tensor.transpose(ps[:, 6 + u % 2, P:2 * P], ca_rows[:, :], ident).then_inc(c_["rows_tr"], 1)
                if u + 2 < UNITS:
                    cross_scores(pe, u + 2)

        block = ctx.enter_context(nc.Block())

        @block.sync
        def _(sp):
            sp.dma_start(cc[:, 0:P], shape_consts[:, 0:P]).then_inc(s_id, 16)
            for i in range(2):
                sp.dma_start(x_tok[:, 2 * i:2 * i + 2, :],
                             x_p[0, 2 * i * P:(2 * i + 2) * P].rearrange("(m p) n -> p m n", p=P)).then_inc(s_x[i], 16)
            sp.dma_start(x_tok[0:NS, NB, :], x_s.rearrange("b t n -> (b t) n")).then_inc(s_x[2], 16)
            sp.dma_start(w_raw[0][:, :, :], views["inb"][:, :, 0:SLOTW]).then_inc(s_full[0], 16)
            for k0, v, n in ((G_MIX, g_mix, 8), (G_MEM, g_mem, 8), (G_CA, g_ca, 8), (G_FFN, g_ffn, 8),
                             (G_ATT, g_att, 4), (G_CONV, g_conv, 4)):
                sp.dma_start(vec_rows[k0:k0 + n, :], v[0].rearrange("(k p) -> k p", p=P)).then_inc(s_const, 16)
            sp.dma_start(vec_rows[G_FIN:G_FIN + 8, :], g_fin.rearrange("(k p) -> k p", p=P)).then_inc(s_const, 16)
            sp.dma_start(vec_rows[W_CONV:NVEC, :], w_conv[0].rearrange("j (k p) -> (j k) p", p=P)).then_inc(s_const, 16)
            sp.dma_start(st_rows[0:2 * BS, :], st_conv[0].rearrange("b k n -> (b k) n")).then_inc(s_const, 16)
            sp.dma_start(bias_col[0:HEADS, :], sb_bias[0].rearrange("(h o) -> h o", o=1)).then_inc(s_const, 16)
            sp.dma_start(cc[:, P:NCONST], shape_consts[:, P:NCONST]).then_inc(s_const, 16)
            sp.dma_start(w_raw[1][:, :, :], views["inb"][:, :, SLOTW:2 * SLOTW]).then_inc(s_full[1], 16)
            sp.dma_start(m_tok[:, :, :], mem[0].rearrange("(m p) n -> p m n", p=P)).then_inc(s_m, 16)
            sp.dma_start(ptb[0:1, :], ptab.rearrange("(o b) n -> o (b n)", o=1)).then_inc(s_pt, 16)
            for name in ("inb", "in", "ck", "cv"):
                load_stage(sp, name)
            sp.wait_ge(s_pt, 16)
            with sp.Fori(0, GROUPS) as g:
                for c in range(CP):
                    load_pages(sp, g, c, ck, k_page, s_kp, s_ktr, 8)
            sp.wait_ge(m_["pv"], 8 * GROUPS + 1)
            load_stage(sp, "out")
            def load_mem(src, b, place):
                return sp.dma_start(place[:, :, :], src[0, b].rearrange("(m p) h d -> p m (h d)", p=P))
            sp.wait_ge(s_op["out"], KD)
            for b in range(BS):
                load_mem(cmk, b, smk_tok[b]).then_inc(s_cmk, 16)
            for b in range(2):
                load_mem(cmv, b, smv_tok[b]).then_inc(s_cmv[0], 16)
            load_stage(sp, "cq")
            for b in range(2, BS):
                sp.wait_ge(s_tr, U_SMK[(b - 2) // 2][-1] + 1)
                load_mem(cmv, b, smv_tok[b]).then_inc(s_cmv[b // 4], 16)
            for name in ("co", "gu0", "down0", "gu1", "down1"):
                load_stage(sp, name)
            sp.wait_ge(s_kv_out, 16 * 4)
            sp.wait_ge(s_out, 16 * 9)

        @block.gpsimd
        def _(pool):
            for name in ("inb", "in", "ck", "cv"):
                lo_stage(pool, name)
            pool.wait_ge(s_pt, 16)
            with pool.Fori(0, GROUPS) as g:
                for c in range(CP):
                    load_pages(pool, g, c, cv, v_page, s_vp, m_["pv"], 1)
            for name in NAMES[NAMES.index("out"):]:
                lo_stage(pool, name)

        @block.scalar
        def _(act):
            act.wait_ge(s_set, 2)
            for m in range(5):
                act.wait_ge(s_x[m // 2], 16)
                if m:
                    act.wait_ge(s_sq["inb"], m)
                nc.scalar.activation(x_sq[0:rows_of(m), :], x_tok[0:rows_of(m), m, :], ACT.Square,
                                     accum_out=x_ss[0:rows_of(m), m:m + 1]).then_inc(s_sq["inb"], 1)
                tr_copy(act, even(U_X[2 * m:2 * m + 2]))
            split_hi_halves(act, "inb", LOW, HIGH)
            tr_copy(act, U_VEC)
            copied(act, U_VEC[-1])
            hi_parts(act, "inb", xT, G_MIX, range(KD))
            split_hi(act, "inb", 0, 1)
            nc.scalar.preload_act_table(ACT.Sqrt)
            act.wait_ge(s_ms["inb"], 1)
            nc.scalar.activation(rstd[:, 0:SEQ], ps[:, 6, 0:SEQ], ACT.Sqrt, bias=cst[:, 0:1], scale=1.0 / D)
            nc.scalar.activation(rstd[:, SEQ:T], ps[:, 7, 0:NS], ACT.Sqrt, bias=cst[:, 0:1], scale=1.0 / D)\
                .then_inc(s_rt["inb"], 1)
            act.wait_ge(s_m, 16)
            for m in range(MT):
                if m:
                    act.wait_ge(s_sq["ck"], m)
                nc.scalar.activation(x_sq[:, :], m_tok[:, m, :], ACT.Square,
                                     accum_out=x_ss[:, 5 + m:6 + m]).then_inc(s_sq["ck"], 1)
            with act.Fori(1, PAIRS["inb"]) as i:
                for s in range(2):
                    act.wait_ge(s_tile["inb"], i * 4 + (2 * s - 2))
                    split_hi(act, "inb", i, s)

            def before_in():
                tr_copy(act, even(U_M))

            def bias_and_memory():
                act.wait_ge(s_bmm, 1)
                nc.scalar.activation(bias_p[:, 0, :], ps[:, 6, 0:HEADS], ACT.Copy).then_inc(s_bc, 1)
                nc.scalar.activation(bias_p[:, 1, :], ps[:, 6, 0:HEADS], ACT.Copy, scale=-1.0).then_inc(s_bc, 1)
                nc.scalar.activation(bias_s[:, 0:1], ps[:, 7, 0:1], ACT.Copy).then_inc(s_bc, 1)
                nc.scalar.activation(bias_s[:, 1:2], ps[:, 7, 0:1], ACT.Copy, scale=-1.0).then_inc(s_bc, 1)
                nc.scalar.activation(rstd_m[:, :], ps[:, 7, P:P + NMEM], ACT.Sqrt, bias=cst[:, 0:1], scale=1.0 / D)\
                    .then_inc(s_rt["ck"], 1)
                copied(act, U_M[-1])
                hi_parts(act, "ck", mT, G_MEM, range(KD))

            def norm_conv():
                rms_root(act, "conv", rstd_c[:, :], T, CH)

            def kv_rows():
                tr_copy(act, even(U_VT))
                tr_copy(act, even(U_KT))
                copied(act, U_KT[-1])
                for src, dst_p, dst_s in ((v_tok, out_v_p, out_v_s), (k_rows, out_k_p, out_k_s)):
                    act.dma_start(dst_p[0, 0].rearrange("(m p) h d -> p m (h d)", p=P), src[:, 0:NB, :])\
                        .then_inc(s_kv_out, 16)
                    act.dma_start(dst_s[0].rearrange("b t h d -> (b t) (h d)"), src[0:NS, NB, :])\
                        .then_inc(s_kv_out, 16)
            split_stage(act, "in", between=before_in, after=bias_and_memory)
            split_stage(act, "ck", between=norm_conv, after=kv_rows)
            split_stage(act, "cv", between=lambda: tr_copy(act, even(U_MK[0:3])))
            nc.scalar.preload_act_table(ACT.Sigmoid)
            tr_copy(act, even(U_MK[3:5]))
            copied(act, U_MK[-1])
            act.dma_start(out_c_p[0, 0], cs_rows[0:2, :]).then_inc(s_out, 16)
            act.dma_start(out_c_s[0].rearrange("b k n -> (b k) n"), cs_rows[2:18, :]).then_inc(s_out, 16)
            for src, dst in ((mk_rows, out_mk), (mv_tok, out_mv)):
                act.dma_start(dst[0, 0].rearrange("(m p) h d -> p m (h d)", p=P), src[:, :, :]).then_inc(s_out, 16)

            def copy_k(g, c):
                for q in range(0, 8, 2):
                    if q == 0:
                        act.wait_ge(m_["score"], g * 9 + (c + 1))
                    act.wait_ge(s_ktr, g * 64 + (8 * c + q + 17))
                    nc.scalar.activation(kT[:, q // 4, :, (q % 4) * P:(q % 4 + 1) * P], tiled(ps[:, q % 3, :]),
                                         ACT.Copy).then_inc(m_["k_copied_a"], 1)

            def sample_sigmoids(S, w):
                act.wait_ge(m_["score"], S + 1)
                act.wait_ge(m_["weight"], S + 1)
                nc.scalar.activation(beta_s[:, 0:w], ps[:, 3, 0:w], ACT.Sigmoid, scale=SB_SCALE,
                                     bias=bias_s[:, 0:1]).then_inc(m_["beta"], 1)
                nc.scalar.activation(om_s[:, 0:w], ps[:, 3, 0:w], ACT.Sigmoid, scale=-SB_SCALE,
                                     bias=bias_s[:, 1:2]).then_inc(m_["om"], 1)

            def copy_weights(S, new):
                act.wait_ge(m_["tr"], S + 2)
                if new:
                    nc.scalar.activation(awT_s[:, 0, :], ps[:, 4, 0:P], ACT.Copy).then_inc(m_["tr_copied"], 1)
                else:
                    nc.scalar.activation(awT_s[:, :, :], tiled(ps[:, 4, :]), ACT.Copy).then_inc(m_["tr_copied"], 1)

            def prompt_sigmoids(g, qb):
                nk = (qb + 1) * P
                act.wait_ge(p_["score"], g * 4 + (qb + 2))
                for h2 in range(2):
                    act.wait_ge(p_["weight"], g * 8 + (2 * qb + h2 + 1))
                    z = ps[:, 5 + 2 * h2, 0:nk]
                    nc.scalar.activation(beta[:, h2, 0:nk], z, ACT.Sigmoid, scale=SB_SCALE,
                                         bias=bias_fix[:, 0, h2:h2 + 1]).then_inc(p_["beta"], 1)
                    nc.scalar.activation(om[:, h2, 0:nk], z, ACT.Sigmoid, scale=-SB_SCALE,
                                         bias=bias_fix[:, 1, h2:h2 + 1]).then_inc(p_["om"], 1)

            def prompt_out(g, qb):
                act.wait_ge(p_["out"], g * 4 + (qb + 2))
                act.wait_ge(s_bc, 4)
                nc.scalar.activation(pT[:, bass.ds(g + T_A, 1), qb * P:(qb + 1) * P].rearrange("p o n -> p (o n)"),
                                     ps[:, 4, 0:P], ACT.Copy).then_inc(p_["out_copied"], 1)

            def fix_prompt(g, c):
                G = c // 8
                act.wait_ge(p_["score"], g * 4 + (4 * G + 1))
                act.wait_ge(s_bc, 4)
                nc.scalar.activation(q_fix[:, :], pT[:, bass.ds(g + (T_Q + G), 1), 0:SEQ].rearrange("p o n -> p (o n)"),
                                     ACT.Copy).then_inc(p_["qk_fixed"], 1)
                nc.scalar.activation(k_fix[:, :], pT[:, bass.ds(g + (T_K + G), 1), 0:SEQ].rearrange("p o n -> p (o n)"),
                                     ACT.Copy).then_inc(p_["qk_fixed"], 1)
                nc.scalar.activation(bias_fix[:, :, :], bias_p[:, :, bass.ds(g * 2 + 2 * G, 2)], ACT.Copy)\
                    .then_inc(p_["bias_fixed"], 1)
                act.wait_ge(p_["bias_fixed"], g + (G + 1))

            def group(g, last):
                for c in range(8):
                    sample_sigmoids(g * 9 + (c + 1), SEQ)
                    if c % 2 == 0 and c:
                        prompt_out(g, c // 2 - 1)
                    if c < 7 or not last:
                        copy_k(g, c + 1)
                    copy_weights(g * 9 + (c + 1), False)
                    if c % 2 == 0:
                        prompt_sigmoids(g, c // 2)
                    else:
                        act.wait_ge(p_["tr"], g * 4 + (c // 2 + 2))
                        nc.scalar.activation(awT[:, 0, 0:c // 2 + 1, :], tiled(ps[:, 5, 0:(c // 2 + 1) * P]), ACT.Copy)\
                            .then_inc(p_["copied_a"], 1)
                if not last:
                    sample_sigmoids(g * 9 + 9, NS)
                    fix_prompt(g, 8)
                else:
                    hi_parts(act, "out", pT[:, T_C:T_C + KC, :], None, range(KC))
                    split_hi_halves(act, "out", HIGH, LOW)
                    nc.scalar.activation(sq_a[:, 0:3, 0:SEQ], pT[:, T_A:T_A + 3, 0:SEQ], ACT.Square)\
                        .then_inc(s_sq_early, 1)
                prompt_out(g, 3)
                if not last:
                    copy_weights(g * 9 + 9, True)

            fix_prompt(0, 0)
            sample_sigmoids(0, NS)
            copy_k(0, 0)
            copy_weights(0, True)
            act.wait_ge(s_out, 16 * 4)
            with act.Fori(0, GROUPS - 1) as g:
                group(g, False)
            group(GROUPS - 1, True)

            act.wait_ge(m_["rows_copied"], GROUPS + 1)
            act.wait_ge(p_["out_copied"], 4 * GROUPS + 1)
            hi_parts(act, "out", pT[:, T_A:T_A + KC, :], G_ATT, range(KC), KC)
            nc.scalar.activation(sq_a[:, 3, 0:SEQ], pT[:, T_A + 3, 0:SEQ], ACT.Square)
            nc.scalar.activation(sq_a[:, :, SEQ:T], pT[:, T_A:T_A + KC, SEQ:T], ACT.Square).then_inc(s_sq["att"], 1)
            act.wait_ge(m_["pv"], 8 * GROUPS + 2)
            split_hi(act, "out", 0, 1)
            rms_root(act, "att", rstd[:, :], T, CH)
            split_stage(act, "out", first=False)

            def operand(name, g0, prev):
                def run_():
                    act.wait_ge(s_tile[prev], 4 * PAIRS[prev])
                    for k in range(KD):
                        act.wait_ge(s_free[prev], k + 3)
                        hi_parts(act, name, xT, g0, [k])
                return run_

            split_stage(act, "cq", between=operand("cq", G_CA, "out"),
                        after=lambda: rms_root(act, "cq", rstd[:, :], T, D))
            cross_act(act)

            def operand_co():
                hi_parts(act, "co", caoT, None, range(CAH))
            act.wait_ge(c_["out_copied"], CAH + 2)
            operand_co()
            split_stage(act, "co", first=False)
            def sigmoid_of(name):
                def more(i):
                    for t in range(2):
                        act.wait_ge(s_free[name], i * 4 + (t + 3))
                        nc.scalar.activation(sbuf_[:, t, :], gbuf[:, t, :], ACT.Sigmoid).then_inc(s_sig, 1)
                return more

            def after_gu0():
                rms_root(act, "gu0", rstd[:, :], T, D)
                nc.scalar.preload_act_table(ACT.Sigmoid)
            split_stage(act, "gu0", sigmoid_of("gu0"), between=operand("gu0", G_FFN, "co"), after=after_gu0)
            split_stage(act, "down0")
            split_stage(act, "gu1", sigmoid_of("gu1"))
            split_stage(act, "down1")
            nc.scalar.preload_act_table(ACT.Sqrt)
            act.wait_ge(s_ms["fin"], 1)
            nc.scalar.activation(y_r[:, :], ps[:, 6, 0:5], ACT.Sqrt, bias=cst[:, 0:1], scale=1.0 / D)\
                .then_inc(s_rt["fin"], 1)
            act.wait_ge(s_y, 1)
            for m in range(5):
                tr_copy(act, even(U_Y[2 * m:2 * m + 2]), lambda u: y_r[0:rows_of((u - U_Y[0]) // 2), (u - U_Y[0]) // 2:(u - U_Y[0]) // 2 + 1])
                copied(act, U_Y[2 * m + 1])
                if m < NB:
                    act.dma_start(y_p[0, m * P:(m + 1) * P, :], y_rows[:, m, :]).then_inc(s_out, 16)
            act.dma_start(y_s.rearrange("b t n -> (b t) n"), y_rows[0:NS, NB, :]).then_inc(s_out, 16)

        @block.vector
        def _(dve):
            nc.vector.memset(ones[:, :], 1.0).then_inc(s_set, 1)
            nc.vector.memset(cst[:, :], EPS).then_inc(s_set, 1)
            grant(s_free["inb"], 2)
            dve.wait_ge(s_id, 16)
            tr_copy(dve, odd(U_X))
            copied(dve, U_VEC[-1])
            lo_parts(dve, "inb", xT, G_MIX, range(KD))
            nc.vector.tensor_scalar(bias_dg[0:HEADS, :], ident[0:HEADS, 0:HEADS], bias_col[0:HEADS, 0:1], None,
                                    ALU.mult).then_inc(s_set, 1)
            for m in range(5):
                dve.wait_ge(s_sq["inb"], m + 1)
                op = nc.vector.tensor_scalar(x_dg[0:rows_of(m), m, :], ident[0:rows_of(m), :],
                                             x_ss[0:rows_of(m), m:m + 1], None, ALU.mult)
            op.then_inc(s_sum["inb"], 1)
            rms_inv(dve, "inb", rstd[:, :])
            for m in range(MT):
                dve.wait_ge(s_sq["ck"], m + 1)
                op = nc.vector.tensor_scalar(m_dg[:, m, :], ident, x_ss[:, 5 + m:6 + m], None, ALU.mult)
            op.then_inc(s_sum["ck"], 1)
            evac_scaled(dve, "inb", pT[:, T_B:, :], rstd[:, :])
            tr_copy(dve, odd(U_M))
            grant(s_free["in"], 2)
            step(dve, nc.vector.memset(c_sum[:, :], 0.0))

            def convolve(k):
                w = [cvec[:, W_CONV + 4 * j + k:W_CONV + 4 * j + k + 1] for j in range(3)]
                u, y = pT[:, T_U + k, :], pT[:, T_C + k, :]
                us, ys = (a[:, SEQ:T].rearrange("p (b t) -> p b t", t=TS) for a in (u, y))
                st = stT[:, k, :].rearrange("p (b j) -> p b j", j=2)

                def add(dst, src, wj):
                    step(dve, nc.vector.scalar_tensor_tensor(out=dst, in0=src, scalar=wj, in1=dst,
                                                             op0=ALU.mult, op1=ALU.add))
                step(dve, nc.vector.tensor_tensor(u, y, u, ALU.mult))
                step(dve, nc.vector.tensor_scalar(y, u, w[2], None, ALU.mult))
                add(y[:, 1:SEQ], u[:, 0:SEQ - 1], w[1])
                add(y[:, 2:SEQ], u[:, 0:SEQ - 2], w[0])
                add(ys[:, :, 1:TS], us[:, :, 0:TS - 1], w[1])
                add(ys[:, :, 0:1], st[:, :, 1:2], w[1])
                add(ys[:, :, 2:TS], us[:, :, 0:TS - 2], w[0])
                add(ys[:, :, 0:2], st[:, :, 0:2], w[0])
                nc.vector.tensor_copy(cs[:, k, 0:2], u[:, SEQ - 2:SEQ])
                nc.vector.tensor_copy(cs[:, k, 2:18].rearrange("p (b j) -> p b j", j=2), us[:, :, TS - 2:TS])

            def convolve_end(k):
                y = pT[:, T_C + k, :]
                step(dve, nc.vector.tensor_tensor(y, y, pT[:, T_B + k, :], ALU.mult))
                step(dve, nc.vector.tensor_tensor(c_sq[:, :], y, y, ALU.mult))
                step(dve, nc.vector.tensor_tensor(c_sum[:, :], c_sum[:, :], c_sq[:, :], ALU.add))

            for j in range(4 * PAIRS["in"]):
                dve.wait_ge(s_tile["in"], j + 1)
                step(dve, nc.vector.tensor_tensor(halves(pT[:, j, :]), pair(j % 2), halves(rstd[:, :]), ALU.mult))
                grant(s_free["in"], 1)
                if j < 2 * KC:
                    (convolve if j % 2 == 0 else convolve_end)(j // 2)
                elif j == 2 * KC:
                    grant(s_sum["conv"], 1)
                    lo_parts(dve, "ck", mT, G_MEM, range(KD))
            grant(s_evac["in"], 1)
            rms_inv(dve, "ck", rstd_m[:, :])
            grant(s_free["ck"], 2)
            grant(s_ktr, 8)
            tr_copy(dve, odd(U_VT))
            tr_copy(dve, odd(U_KT))
            nc.vector.memset(zeros[:, :], 0.0)
            nc.vector.memset(aw_s[:, :], 0.0)

            def inverse(j):
                if j % 2:
                    half = rstd_c[:, (j // 2) * HALF:(j // 2 + 1) * HALF]
                    step(dve, nc.vector.reciprocal(half, half))

            def norm(k):
                y = pT[:, T_C + k, :]
                step(dve, nc.vector.scalar_tensor_tensor(out=y, in0=y, scalar=cvec[:, G_CONV + k:G_CONV + k + 1],
                                                         in1=rstd_c[:, :], op0=ALU.mult, op1=ALU.mult))
                if k == 0:
                    dve.wait_ge(s_kv_out, 16 * 4)
                    grant(s_ktr, 8)
                if k == 2:
                    dve.wait_ge(s_wlo, SLOT0["out"])
                    grant(m_["pv"], 1)
            dve.wait_ge(s_rt["conv"], 1)
            evac_mem(dve, "ck", mkT, inverse)
            grant(s_evac["ck"], 1)
            grant(s_free["cv"], 2)
            tr_copy(dve, odd(U_MK[0:3]))
            evac_mem(dve, "cv", mvT, norm)
            grant(s_evac["cv"], 1)
            grant(m_["pv"], 1)
            tr_copy(dve, odd(U_MK[3:5]))

            dve.wait_ge(s_tile["cv"], 4)
            nc.vector.memset(run[:, :, P:SEQ + 1:P], 1.0)
            step(dve, nc.vector.memset(q_bd[:, :, :, :], 0.0))
            copied(dve, U_MK[-1])
            nc.vector.memset(v_tok[NS:P, NB, :], 0.0)
            for name, n in (("score", 1), ("weight", 2), ("tr", 1), ("out", 1), ("out_copied", 1)):
                grant(p_[name], n)
            for name, n in (("k_copied_a", 4), ("k_copied_d", 4), ("weight", 1),
                            ("tr", 1), ("tr_copied", 1), ("rows", 1), ("rows_copied", 1)):
                grant(m_[name], n)

            def copy_k(g, c):
                for q in range(1, 8, 2):
                    if q == 1:
                        dve.wait_ge(m_["score"], g * 9 + (c + 1))
                    dve.wait_ge(s_ktr, g * 64 + (8 * c + q + 17))
                    nc.vector.tensor_copy(kT[:, q // 4, :, (q % 4) * P:(q % 4 + 1) * P], tiled(ps[:, q % 3, :]))\
                        .then_inc(m_["k_copied_d"], 1)

            def weights(S, R, w):
                dve.wait_ge(m_["om"], S + 1)
                if w == NS:
                    nc.vector.memset(run_s[:, w:w + 1], 1.0).then_inc(m_["run"], 1)
                    dve.wait_ge(m_["run"], R + 1)
                    R = R + 1
                nc.vector.tensor_tensor_scan(run_s[:, 0:w][:, ::-1], om_s[:, 0:w][:, ::-1], om_s[:, 0:w][:, ::-1],
                                             run_s[:, w:w + 1], ALU.mult, ALU.bypass).then_inc(m_["run"], 1)
                dve.wait_ge(m_["run"], R + 1)
                dve.wait_ge(m_["tr"], S + 1)
                nc.vector.tensor_tensor(aw_s[:, 0:w], beta_s[:, 0:w], run_s[:, 1:w + 1], ALU.mult)\
                    .then_inc(m_["weight"], 1)
                dve.wait_ge(m_["weight"], S + 2)
                nc.vector.tensor_copy(run_s[:, SEQ:SEQ + 1], run_s[:, 0:1]).then_inc(m_["run"], 1)
                dve.wait_ge(m_["run"], R + 2)

            def prompt_weights(g, qb):
                nk = (qb + 1) * P
                for h2 in range(2):
                    dve.wait_ge(p_["om"], g * 8 + (2 * qb + h2 + 1))
                    nc.vector.tensor_tensor_scan(run[:, h2, 0:nk][:, ::-1], om[:, h2, 0:nk][:, ::-1],
                                                 om[:, h2, 0:nk][:, ::-1], 1.0, ALU.mult, ALU.bypass)\
                        .then_inc(p_["scan"], 1)
                    dve.wait_ge(p_["scan"], g * 8 + (2 * qb + h2 + 1))
                    if h2 == 0:
                        dve.wait_ge(p_["tr"], g * 4 + (qb + 1))
                    nc.vector.tensor_tensor(aw[:, h2, 0:nk], beta[:, h2, 0:nk], run[:, h2, 1:nk + 1], ALU.mult)\
                        .then_inc(p_["weight"], 1)

            def queries(g, c):
                G = c // 8
                for s in range(2):
                    for h2 in range(2):
                        op = nc.vector.tensor_copy(
                            q_bd[64 * h2:64 * h2 + 64, s, :, 16 * s + 8 * h2:16 * s + 8 * h2 + 8],
                            pT[64 * h2:64 * h2 + 64, T_Q:T_Q + HP, bass.ds(g * 16 + (SEQ + 8 * s + 16 * G), 8)])
                op.then_inc(m_["queries"], 1)

            def fix_values(g, c):
                G = c // 8
                dve.wait_ge(p_["out"], g * 4 + (4 * G + 1))
                nc.vector.tensor_copy(v_fix[:, :, :], v_tok[:, 0:NB, bass.ds(g * P + G * P, P)])\
                    .then_inc(p_["v_fixed"], 1)

            def group(g, last):
                for c in range(8):
                    weights(g * 9 + (c + 1), g * 19 + (3 + 2 * c), SEQ)
                    if c < 7 or not last:
                        copy_k(g, c + 1)
                    if c % 2 == 0:
                        prompt_weights(g, c // 2)
                    else:
                        dve.wait_ge(p_["tr"], g * 4 + (c // 2 + 2))
                        nc.vector.tensor_copy(awT[:, 1, 0:c // 2 + 1, :], tiled(ps[:, 7, 0:(c // 2 + 1) * P]))\
                            .then_inc(p_["copied_d"], 1)
                if not last:
                    queries(g, 8)
                    weights(g * 9 + 9, g * 19 + 19, NS)
                else:
                    lo_parts(dve, "out", pT[:, T_C:T_C + KC, :], None, range(KC))
                dve.wait_ge(m_["pv"], g * 8 + 10)
                nc.vector.tensor_copy(o_pair[:, :, :], tiled(ps[:, 6, 0:2 * P])).then_inc(m_["rows"], 1)
                dve.wait_ge(m_["rows_tr"], g + 1)
                for s in range(2):
                    for h2 in range(2):
                        rows = tiled(ps[64 * h2:64 * h2 + 64, 6, s * P:(s + 1) * P], 32)
                        op = nc.vector.tensor_copy(
                            pT[64 * h2:64 * h2 + 64, T_A:T_A + HP, bass.ds(g * 16 + (SEQ + 8 * s), 8)],
                            rows[:, :, 16 * s + 8 * h2:16 * s + 8 * h2 + 8])
                op.then_inc(m_["rows_copied"], 1)
                if not last:
                    fix_values(g, 8)

            queries(0, 0)
            fix_values(0, 0)
            weights(0, 0, NS)
            copy_k(0, 0)
            with dve.Fori(0, GROUPS - 1) as g:
                group(g, False)
            group(GROUPS - 1, True)

            grant(s_free["out"], 2)
            dve.wait_ge(s_sq_early, 1)
            for k in (1, 2):
                step(dve, nc.vector.tensor_tensor(sq_a[:, 0, 0:SEQ], sq_a[:, 0, 0:SEQ], sq_a[:, k, 0:SEQ], ALU.add))
            dve.wait_ge(p_["out_copied"], 4 * GROUPS + 1)
            lo_parts(dve, "out", pT[:, T_A:T_A + KC, :], G_ATT, range(KC), KC, KC)
            dve.wait_ge(s_sq["att"], 1)
            for k in range(1, KC):
                step(dve, nc.vector.tensor_tensor(sq_a[:, 0, SEQ:T], sq_a[:, 0, SEQ:T], sq_a[:, k, SEQ:T], ALU.add))
            nc.vector.tensor_tensor(sq_a[:, 0, 0:SEQ], sq_a[:, 0, 0:SEQ], sq_a[:, 3, 0:SEQ], ALU.add)\
                .then_inc(s_sum["att"], 1)
            rms_inv(dve, "att", rstd[:, :])
            def operand_lo(name, g0):
                return lambda tiles: lo_parts(dve, name, xT, g0, tiles, 0, tiles[0])
            evac_residual(dve, "out", r_sum, r_sq, next_lo=operand_lo("cq", G_CA))
            grant(s_sum["cq"], 1)
            grant(s_free["cq"], 2)
            rms_inv(dve, "cq", rstd[:, :])
            evac_scaled(dve, "cq", caq, rstd[:, :])
            grant(s_evac["cq"], 1)
            dve.wait_ge(s_evac["cq"], 1)
            cross_dve(dve)
            grant(s_free["co"], 2)
            dve.wait_ge(c_["out_copied"], CAH + 2)
            lo_parts(dve, "co", caoT, None, range(CAH))
            evac_residual(dve, "co", r_sum, r_sq, next_lo=operand_lo("gu0", G_FFN))
            grant(s_sum["gu0"], 1)
            grant(s_free["gu0"], 2)
            rms_inv(dve, "gu0", rstd[:, :])
            for half in range(2):
                hidden_dve(dve, half)
                name = f"down{half}"
                grant(s_free[name], 2)
                if half == 0:
                    evac_residual(dve, name)
                    grant(s_free["gu1"], 2)
                else:
                    evac_residual(dve, name, gbuf[:, 0, :], gbuf[:, 1, :], yT)
            grant(s_sum["fin"], 1)
            grant(s_evac["down1"], 1)
            dve.wait_ge(s_rt["fin"], 1)
            step(dve, nc.vector.reciprocal(y_r[:, :], y_r[:, :]))
            grant(s_y, 1)
            for m in range(5):
                tr_copy(dve, odd(U_Y[2 * m:2 * m + 2]), lambda u: y_r[0:rows_of((u - U_Y[0]) // 2), (u - U_Y[0]) // 2:(u - U_Y[0]) // 2 + 1])

        @block.tensor
        def _(pe):
            pe.wait_ge(s_id, 16)
            for m in range(5):
                pe.wait_ge(s_x[m // 2], 16)
                tr_pe(pe, U_X[2 * m:2 * m + 2])
            pe.wait_ge(s_set, 1)
            pe.wait_ge(s_const, 16 * 11)
            tr_pe(pe, U_VEC)

            def bias_and_memory():
                pe.wait_ge(s_m, 16)
                tr_pe(pe, U_M)
                pe.wait_ge(s_set, 3)
                pe.wait_ge(s_rt["inb"], 1)
                nc.tensor.matmul(ps[:, 6, 0:HEADS], ones[0:HEADS, :], bias_dg[0:HEADS, :], start=True, stop=True)
                nc.tensor.matmul(ps[:, 7, 0:1], cc[0:HEADS, C_SEL:C_SEL + P], bias_col[0:HEADS, :],
                                 start=True, stop=True)
                pe.wait_ge(s_sum["ck"], 1)
                for m in range(MT):
                    op = nc.tensor.matmul(ps[:, 7, (m + 1) * P:(m + 2) * P], ones[:, :], m_dg[:, m, :],
                                          start=True, stop=True)
                op.then_inc(s_bmm, 1)

            def x_rms():
                pe.wait_ge(s_sum["inb"], 1)
                for m in range(5):
                    r = rows_of(m)
                    c = (m % 4) * P
                    op = nc.tensor.matmul(ps[:, 6 + m // 4, c:c + r], ones[0:r, :], x_dg[0:r, m, 0:r], start=True, stop=True)
                op.then_inc(s_ms["inb"], 1)

            gemm(pe, "inb", h_hi, h_lo, peel=True, hook=x_rms)
            bias_and_memory()
            gemm(pe, "in", h_hi, h_lo)
            rms_pe(pe, "conv", c_sum, T, "ck")
            pe.wait_ge(s_evac["in"], 1)
            tr_pe(pe, U_VT)
            tr_pe(pe, U_KT)
            pe.wait_ge(s_op["ck"], KD)
            gemm(pe, "ck", m_hi, m_lo, NMEM)
            pe.wait_ge(s_evac["ck"], 1)
            tr_pe(pe, U_MK[0:3])
            gemm(pe, "cv", m_hi, m_lo, NMEM)
            pe.wait_ge(s_evac["cv"], 1)
            tr_pe(pe, U_MK[3:5])

            def prompt_scores(g, qb):
                if qb == 0:
                    pe.wait_ge(p_["qk_fixed"], g * 2 + 2)
                for h2 in range(2):
                    r = slice(64 * h2, 64 * h2 + 64)
                    nc.tensor.matmul(ps[:, 5 + 2 * h2, 0:(qb + 1) * P], q_fix[r, qb * P:(qb + 1) * P],
                                     k_fix[r, 0:(qb + 1) * P], start=True, stop=False)
                for h2 in range(2):
                    op = nc.tensor.matmul(ps[:, 5 + 2 * h2, qb * P:(qb + 1) * P], ident, cc[:, C_CMASK:C_CMASK + P],
                                          start=False, stop=True)
                op.then_inc(p_["score"], 1)

            def prompt_transposes(g, qb):
                pe.wait_ge(p_["weight"], g * 8 + (2 * qb + 4))
                for h2 in range(2):
                    for kb in range(qb + 1):
                        op = nc.tensor.transpose(ps[:, 5 + 2 * h2, kb * P:(kb + 1) * P], aw[:, h2, kb * P:(kb + 1) * P],
                                                 ident)
                op.then_inc(p_["tr"], 1)

            def prompt_sums(g, qb):
                if qb == 0:
                    pe.wait_ge(p_["v_fixed"], g + 1)
                pe.wait_ge(p_["copied_a"], g * 4 + (qb + 1))
                pe.wait_ge(p_["copied_d"], g * 4 + (qb + 1))
                for h2 in range(2):
                    for kb in range(qb + 1):
                        op = nc.tensor.matmul(ps[64 * h2:64 * h2 + 64, 4, 0:P], v_fix[:, kb, 64 * h2:64 * h2 + 64],
                                              awT[:, h2, kb, :], start=kb == 0, stop=kb == qb)
                op.then_inc(p_["out"], 1)

            def k_transposes(g, c):
                for q in range(8):
                    if q == 0:
                        pe.wait_ge(s_kp[c % 2], g * 512 + 128 * (c // 2 + 1))
                    last = (q - 3) if q >= 3 else (6, 7, 5)[q] - 8
                    pe.wait_ge(m_["k_copied_a" if last % 2 == 0 else "k_copied_d"],
                               g * 32 + (4 * c + 4 + last // 2 + 1))
                    for j in range(HP):
                        op = nc.tensor.transpose(ps[:, q % 3, j * P:(j + 1) * P],
                                                 k_page[c % 2][:, q, j * P:(j + 1) * P], ident)
                    op.then_inc(s_ktr, 1)

            def new_scores(g, c):
                G = c // 8
                pe.wait_ge(m_["queries"], g + (G + 1))
                nc.tensor.matmul(ps[:, 3, 0:NS], ident, cc[:, bass.ds(g * NS + (C_SMASK + G * NS), NS)],
                                 start=True, stop=False)
                for s in range(2):
                    for j in range(HP):
                        op = nc.tensor.matmul(ps[32 * j:32 * j + 32, 3, 0:NS], q_bd[:, s, j, :],
                                              pT[:, T_K + j, SEQ:T], start=False, stop=s == 1)
                op.then_inc(m_["score"], 1)

            def scores(g, c):
                pe.wait_ge(m_["k_copied_a"], g * 32 + (4 * c + 8))
                pe.wait_ge(m_["k_copied_d"], g * 32 + (4 * c + 8))
                for s in range(2):
                    for j in range(HP):
                        op = nc.tensor.matmul(ps[32 * j:32 * j + 32, 3, :], q_bd[:, s, j, :], kT[:, s, j, :],
                                              start=s == 0, stop=s == 1)
                op.then_inc(m_["score"], 1)

            def weight_transposes(g, c):
                S = g * 9 + (c + 1)
                if c % 2 == 0:
                    pe.wait_ge(p_["out_copied"], g * 4 + (c // 2 + 1))
                pe.wait_ge(m_["weight"], S + 2)
                pe.wait_ge(m_["tr_copied"], S + 1)
                for j in range(4):
                    op = nc.tensor.transpose(ps[:, 4, j * P:(j + 1) * P], aw_s[:, j * P:(j + 1) * P], ident)
                op.then_inc(m_["tr"], 1)

            def new_transposes(g, c):
                S = g * 9 + 9 * (c // 8)
                pe.wait_ge(p_["out_copied"], g * 4 + (4 * (c // 8) + 1))
                pe.wait_ge(m_["weight"], S + 2)
                pe.wait_ge(m_["tr_copied"], S + 1)
                nc.tensor.transpose(ps[:, 4, 0:P], aw_s[:, 0:P], ident).then_inc(m_["tr"], 1)

            def new_sums(g, c):
                pe.wait_ge(m_["tr_copied"], g * 9 + (9 * (c // 8) + 2))
                pe.wait_ge(m_["rows_copied"], g + (c // 8 + 1))
                for j in range(HP):
                    v = v_tok[:, NB:NB + 1, j * P:(j + 1) * P].to_broadcast([P, 2, P])
                    nc.tensor.matmul(tiled(ps[32 * j:32 * j + 32, 6, 0:2 * P]), awT_s[:, 0, 32 * j:32 * j + 32],
                                     v, start=True, stop=False)

            def sums(g, c):
                pe.wait_ge(m_["tr_copied"], g * 9 + (c + 3))
                pe.wait_ge(s_vp[c % 2], g * 512 + 128 * (c // 2 + 1))
                for s in range(2):
                    for q in range(4):
                        for j in range(HP):
                            op = nc.tensor.matmul(ps[32 * j:32 * j + 32, 6, s * P:(s + 1) * P],
                                                  awT_s[:, q, 32 * j:32 * j + 32],
                                                  v_page[c % 2][:, 4 * s + q, j * P:(j + 1) * P],
                                                  start=False, stop=False, skip_group_check=True)
                if c == 7:
                    for j in range(HP):
                        op = nc.tensor.matmul(tiled(ps[32 * j:32 * j + 32, 6, 0:2 * P]), zeros[:, :], tiled(cc[:, 0:2 * P]),
                                              start=False, stop=True)
                op.then_inc(m_["pv"], 1)

            def group(g, last):
                for c in range(8):
                    if c < 7 or not last:
                        k_transposes(g, c + 1)
                    weight_transposes(g, c)
                    if c % 2 == 0:
                        prompt_scores(g, c // 2)
                    else:
                        prompt_transposes(g, c // 2)
                    if c < 7:
                        scores(g, c + 1)
                    elif not last:
                        new_scores(g, 8)
                    sums(g, c)
                    if c % 2 == 1:
                        prompt_sums(g, c // 2)
                pe.wait_ge(m_["rows"], g + 2)
                for s in range(2):
                    op = nc.tensor.transpose(ps[:, 6, s * P:(s + 1) * P], o_pair[:, s, :], ident)
                op.then_inc(m_["rows_tr"], 1)
                if not last:
                    new_transposes(g, 8)
                    scores(g, 8)
                    new_sums(g, 8)

            new_scores(0, 0)
            k_transposes(0, 0)
            new_transposes(0, 0)
            scores(0, 0)
            new_sums(0, 0)
            with pe.Fori(0, GROUPS - 1) as g:
                group(g, False)
            group(GROUPS - 1, True)

            pe.wait_ge(p_["out_copied"], 4 * GROUPS + 1)
            gemm_out(pe)
            gemm(pe, "cq", h_hi, h_lo, peel=True, prev="out", hook=lambda: rms_pe(pe, "cq", r_sum, T))
            cross_pe(pe)
            gemm(pe, "co", h_hi, h_lo, peel=True)
            gemm(pe, "gu0", h_hi, h_lo, peel=True, prev="co", hook=lambda: rms_pe(pe, "gu0", r_sum, T))
            gemm(pe, "down0", f_hi, f_lo)
            gemm(pe, "gu1", h_hi, h_lo)
            gemm(pe, "down1", f_hi, f_lo)
            pe.wait_ge(s_sum["fin"], 1)
            for m in range(5):
                op = nc.tensor.matmul(ps[0:rows_of(m), 6, m:m + 1], gbuf[:, 0, m * P:m * P + rows_of(m)],
                                      ones[:, 0:1], start=True, stop=True)
            op.then_inc(s_ms["fin"], 1)
            tr_pe(pe, U_Y)


def shape_table():
    c = np.zeros((P, NCONST), np.float32)
    i = np.arange(P)
    c[i, C_ID + i] = 1.0
    seq, step_ = (i // 16) % 2, i % 8
    for g in range(GROUPS):
        for b in range(BS):
            for t in range(TS):
                seen = (b == 2 * g + seq) & (t < step_)
                c[:, C_SMASK + g * NS + b * TS + t] = np.where(seen, 0.0, -1e30)
    c[:, C_CMASK:C_CMASK + P] = np.where(i[None, :] < i[:, None], 0.0, -1e30)
    head = 2 * (i // 32) + (i // 8) % 2
    c[head, C_SEL + i] = 1.0
    return c


_INS = ["x_prompt", "x_sample", "mem_prompt", "cache_sb_k", "cache_sb_v", "cache_mem_k", "cache_mem_v", "state_conv",
        "page_table", "g_mix", "w_in", "sb_bias", "w_conv", "g_attn_out", "g_conv_out", "w_out", "g_mem", "g_ca",
        "w_cq", "w_ck", "w_cv", "w_co", "g_ffn", "w_gate", "w_up", "w_down", "g_final"]
_OUTS = [(1, SEQ, D), (BS, TS, D), (1, 1, SEQ, HEADS, HD), (1, 1, SEQ, HEADS, HD), (1, 1, 2, CH),
         (1, 1, NMEM, CAH, P), (1, 1, NMEM, CAH, P), (1, BS, TS, HEADS, HD), (1, BS, TS, HEADS, HD), (1, BS, 2, CH)]


def kernel(**inputs):
    import concourse.bacc as bacc
    from concourse.bass_utils import run_bass_kernel_spmd

    nc = bacc.Bacc("TRN2", target_bir_lowering=False, num_devices=1)
    arrays, args = {}, []
    for name in _INS:
        a = np.ascontiguousarray(inputs[name])
        arrays[f"in_{name}"] = a
        args.append(nc.dram_tensor(f"in_{name}", a.shape, mybir.dt.from_np(a.dtype), kind="ExternalInput").ap())
    arrays["shape_constants"] = shape_table()
    args.append(nc.dram_tensor("shape_constants", (P, NCONST), F32, kind="ExternalInput").ap())
    for i, shape in enumerate(_OUTS):
        args.append(nc.dram_tensor(f"out_{i}", shape, F32, kind="ExternalOutput").ap())
    hybrid_layer(nc, *args)
    r = run_bass_kernel_spmd(nc, [arrays], core_ids=[0])
    return tuple(r.results[0][f"out_{i}"] for i in range(len(_OUTS)))
```
